# Optimizing a Trainium2 kernel written in Bass

```python
import math
import jax
import jax.numpy as jnp
from jax import lax
import numpy as np

D_MODEL = 1024
BATCH = 1
SEQ = 128
DEPTH = 2
DEC_BATCH = 1
DEC_SEQ = 512
PAST_LEN = 256

GRID_W = 64
N_AB = (DEPTH + 1) // 2
N_C = DEPTH // 2
D_A = D_MODEL // 2
A_HEADS = 4
A_DK = D_A // A_HEADS
A_DV = D_A // A_HEADS
CHUNK = 32
D_B = D_MODEL // 2
B_BLOCKS = 8
B_BLOCK = D_B // B_BLOCKS
CONV_W = 4
LRU_C = 8.0
D_IN_AB = 5 * D_A + 2 * D_B
C_HEAD = 64
C_HEADS = D_MODEL // C_HEAD
W_LORA = 64
A_LORA = 64
G_LORA = 128
W_DECAY_SCALE = math.exp(-0.5)
N_EXPERTS = 16
N_GROUPS = 4
TOP_K = 2
D_EXPERT = 256
RMS_EPS = 1e-6
GN_EPS = 64e-5
POS_BASE = 10000.0
F32 = jnp.float32

kernel_name = 'hybrid_hgrn2_rglru_rwkv7_moe_diffusion_step'

def rmsnorm(x, g):
    x32 = x.astype(F32)
    y = x32 * lax.rsqrt(jnp.mean(x32 * x32, axis=-1, keepdims=True) + RMS_EPS)
    return (y * g.astype(F32)).astype(x.dtype)

def ada_modulation(cvec, w, b):
    m = jnp.matmul(jax.nn.silu(cvec), w) + b
    return jnp.split(m[..., None, :], 6, axis=-1)

def grid_pos_embed(n_tok):
    rows = n_tok // GRID_W
    r, cl = jnp.meshgrid(jnp.arange(rows, dtype=F32), jnp.arange(GRID_W, dtype=F32), indexing='ij')
    quarter = D_MODEL // 4
    omega = 1.0 / (POS_BASE ** (jnp.arange(quarter, dtype=F32) / quarter))
    ang_r = r.reshape(-1, 1) * omega
    ang_c = cl.reshape(-1, 1) * omega
    return jnp.concatenate([jnp.sin(ang_r), jnp.cos(ang_r), jnp.sin(ang_c), jnp.cos(ang_c)], axis=-1)

def flip_t(z):
    return jnp.flip(z, axis=1)

def ident(z):
    return z

def gla_chunked(q, k, v, logf, s0):
    bsz, t, nh, _ = q.shape
    n = t // CHUNK

    def to_chunks(a):
        return jnp.moveaxis(a.reshape(bsz, n, CHUNK, *a.shape[2:]), 1, 0)

    causal = jnp.tril(jnp.ones((CHUNK, CHUNK), dtype=bool))[None, :, :, None, None]

    def step(s, inp):
        qc, kc, vc, gc = inp
        b = jnp.cumsum(gc, axis=1)
        diff = b[:, :, None] - b[:, None, :]
        decay = jnp.where(causal, jnp.exp(jnp.minimum(diff, 0.0)), 0.0)
        att = jnp.einsum('bthk,bshk,btshk->btsh', qc, kc, decay)
        o = jnp.einsum('btsh,bshv->bthv', att, vc) + jnp.einsum('bthk,bhkv->bthv', qc * jnp.exp(b), s)
        b_last = b[:, -1]
        s = s * jnp.exp(b_last)[..., None] + jnp.einsum('bshk,bshv->bhkv', kc * jnp.exp(b_last[:, None] - b), vc)
        return s, o

    s_fin, o = lax.scan(step, s0.astype(F32), (to_chunks(q), to_chunks(k), to_chunks(v), to_chunks(logf)))
    o = jnp.moveaxis(o, 0, 1).reshape(bsz, t, nh, v.shape[-1])
    return o, s_fin

def linear_scan(a, b, h0):
    def combine(lft, rgt):
        return lft[0] * rgt[0], rgt[0] * lft[1] + rgt[1]
    a_c, b_c = lax.associative_scan(combine, (a, b), axis=1)
    h = a_c * h0.astype(F32)[:, None] + b_c
    return h, h[:, -1]

def centred_dwconv(x, w, bias):
    t = x.shape[1]
    left = CONV_W // 2
    xp = jnp.pad(x, ((0, 0), (left, CONV_W - 1 - left), (0, 0)))
    out = bias
    for j in range(CONV_W):
        out = out + xp[:, j:j + t] * w[j]
    return out

def rwkv7_scan(r, w, k, v, kk, a, s0):
    def step(s, inp):
        r_t, w_t, k_t, v_t, kk_t, a_t = inp
        sa = jnp.einsum('bhvk,bhk->bhv', s, -kk_t)
        s = s * w_t[:, :, None, :] + sa[..., None] * (kk_t * a_t)[:, :, None, :] + v_t[..., None] * k_t[:, :, None, :]
        return s, jnp.einsum('bhvk,bhk->bhv', s, r_t)
    xs = tuple(jnp.moveaxis(z, 1, 0) for z in (r, w, k, v, kk, a))
    s_fin, o = lax.scan(step, s0.astype(F32), xs)
    return jnp.moveaxis(o, 0, 1), s_fin

def moe_ffn(h, router_w, router_b, w1, w3, w2):
    bsz, t, d = h.shape
    hf = h.reshape(-1, d)
    scores = jax.nn.sigmoid(jnp.matmul(hf, router_w).astype(F32))
    sel = scores + router_b.astype(F32)
    grp = sel.reshape(-1, N_GROUPS, N_EXPERTS // N_GROUPS)
    grp_score = jnp.sum(lax.top_k(grp, TOP_K)[0], axis=-1)
    best = jnp.argmax(grp_score, axis=-1)
    in_grp = (jnp.arange(N_EXPERTS) // (N_EXPERTS // N_GROUPS))[None, :] == best[:, None]
    _, idx = lax.top_k(jnp.where(in_grp, sel, -jnp.inf), TOP_K)
    wsel = jnp.take_along_axis(scores, idx, axis=-1)
    wsel = wsel / jnp.sum(wsel, axis=-1, keepdims=True)
    combine = jnp.sum(jax.nn.one_hot(idx, N_EXPERTS, dtype=F32) * wsel[..., None], axis=1)
    hid = jax.nn.silu(jnp.einsum('md,edf->mef', hf, w1)) * jnp.einsum('md,edf->mef', hf, w3)
    hid = hid * combine[..., None].astype(hid.dtype)
    return jnp.einsum('mef,efd->md', hid, w2).reshape(bsz, t, d)

def setup_inputs(seed: int = 0) -> dict:
    key = jax.random.key(seed)
    ks = iter(jax.random.split(key, 64))

    def nrm(shape, scale):
        return scale * jax.random.normal(next(ks), shape, F32)

    D = D_MODEL
    u = jax.random.uniform(next(ks), (N_AB, 2, D_B), F32, minval=0.9, maxval=0.999)
    base = u ** (1.0 / LRU_C)
    rg_lambda = jnp.log(base) - jnp.log1p(-base)
    return {
        'x_prompt': nrm((BATCH, SEQ, D), 1.0),
        'x_sample': nrm((DEC_BATCH, DEC_SEQ, D), 1.0),
        'state_hgrn': nrm((DEC_BATCH, N_AB, 2, A_HEADS, A_DK, A_DV), 0.3),
        'state_rglru': nrm((DEC_BATCH, N_AB, 2, D_B), 0.5),
        'state_rwkv': nrm((DEC_BATCH, N_C, 2, C_HEADS, C_HEAD, C_HEAD), 0.1),
        'c': nrm((DEC_BATCH, D), 1.0),
        'c_ctx': nrm((D,), 1.0),
        'norm_mix_g': 1.0 + nrm((DEPTH, D), 0.05),
        'norm_ffn_g': 1.0 + nrm((DEPTH, D), 0.05),
        'w_mod': nrm((DEPTH, D, 6 * D), 0.5 * D ** -0.5),
        'b_mod': nrm((DEPTH, 6 * D), 0.02),
        'ab_w_in': nrm((N_AB, D, D_IN_AB), D ** -0.5),
        'ab_w_out': nrm((N_AB, D_A + D_B, D), (D_A + D_B) ** -0.5),
        'hgrn_lb': nrm((2, N_AB + 1, D_A), 0.5),
        'hgrn_norm_g': 1.0 + nrm((N_AB, A_DV), 0.05),
        'rg_conv_w': nrm((N_AB, CONV_W, D_B), CONV_W ** -0.5),
        'rg_conv_b': nrm((N_AB, D_B), 0.02),
        'rg_wa': nrm((N_AB, 2, B_BLOCKS, B_BLOCK, B_BLOCK), B_BLOCK ** -0.5),
        'rg_ba': nrm((N_AB, 2, D_B), 0.02),
        'rg_wx': nrm((N_AB, 2, B_BLOCKS, B_BLOCK, B_BLOCK), B_BLOCK ** -0.5),
        'rg_bx': nrm((N_AB, 2, D_B), 0.02),
        'rg_lambda': rg_lambda,
        'rw_mu': jax.random.uniform(next(ks), (N_C, 6, D), F32),
        'rw_wr': nrm((N_C, D, D), D ** -0.5),
        'rw_wk': nrm((N_C, D, D), D ** -0.5),
        'rw_wv': nrm((N_C, D, D), D ** -0.5),
        'rw_wo': nrm((N_C, D, D), D ** -0.5),
        'rw_w0': nrm((N_C, 2, D), 1.0),
        'rw_w1': nrm((N_C, 2, D, W_LORA), D ** -0.5),
        'rw_w2': nrm((N_C, 2, W_LORA, D), 0.5 * W_LORA ** -0.5),
        'rw_a0': nrm((N_C, 2, D), 0.5),
        'rw_a1': nrm((N_C, 2, D, A_LORA), D ** -0.5),
        'rw_a2': nrm((N_C, 2, A_LORA, D), 0.5 * A_LORA ** -0.5),
        'rw_g1': nrm((N_C, D, G_LORA), D ** -0.5),
        'rw_g2': nrm((N_C, G_LORA, D), G_LORA ** -0.5),
        'rw_kk': 0.85 + nrm((N_C, D), 0.05),
        'rw_ka': 1.0 + nrm((N_C, D), 0.05),
        'rw_rk': nrm((N_C, C_HEADS, C_HEAD), 0.1),
        'rw_lnw': 1.0 + nrm((N_C, D), 0.05),
        'rw_lnb': nrm((N_C, D), 0.02),
        'moe_router': nrm((D, N_EXPERTS), D ** -0.5),
        'moe_router_bias': nrm((N_EXPERTS,), 0.01),
        'moe_w1': nrm((DEPTH, N_EXPERTS, D, D_EXPERT), D ** -0.5),
        'moe_w3': nrm((DEPTH, N_EXPERTS, D, D_EXPERT), D ** -0.5),
        'moe_w2': nrm((DEPTH, N_EXPERTS, D_EXPERT, D), D_EXPERT ** -0.5),
        'norm_f_g': 1.0 + nrm((D,), 0.05),
    }

def reference(x_prompt, x_sample, state_hgrn, state_rglru, state_rwkv, c, c_ctx,
              norm_mix_g, norm_ffn_g, w_mod, b_mod,
              ab_w_in, ab_w_out, hgrn_lb, hgrn_norm_g,
              rg_conv_w, rg_conv_b, rg_wa, rg_ba, rg_wx, rg_bx, rg_lambda,
              rw_mu, rw_wr, rw_wk, rw_wv, rw_wo, rw_w0, rw_w1, rw_w2, rw_a0, rw_a1, rw_a2,
              rw_g1, rw_g2, rw_kk, rw_ka, rw_rk, rw_lnw, rw_lnb,
              moe_router, moe_router_bias, moe_w1, moe_w3, moe_w2, norm_f_g):
    lower_bounds = jnp.cumsum(jax.nn.softmax(hgrn_lb.astype(F32), axis=1), axis=1)

    def mixer_ab(h, j, s_hgrn, s_rglru):
        bsz, t, _ = h.shape
        proj = jnp.matmul(h, ab_w_in[j])
        cuts = [D_A, 2 * D_A, 3 * D_A, 4 * D_A, 5 * D_A, 5 * D_A + D_B]
        q, f_fw, f_bw, v, og, xr, yr = jnp.split(proj, cuts, axis=-1)

        def heads(z):
            return z.astype(F32).reshape(bsz, t, A_HEADS, A_DK)
        qh = heads(jax.nn.silu(q))
        vh = v.astype(F32).reshape(bsz, t, A_HEADS, A_DV)
        outs, finals = [], []
        for d, f_raw in enumerate((f_fw, f_bw)):
            lb = lower_bounds[d, j]
            logf = jnp.log(lb + (1.0 - lb) * jax.nn.sigmoid(f_raw.astype(F32)))
            kh = heads(-jnp.expm1(logf))
            gh = heads(logf)
            fl = flip_t if d == 1 else ident
            o_d, s_d = gla_chunked(fl(qh), fl(kh), fl(vh), fl(gh), s_hgrn[:, d])
            outs.append(fl(o_d))
            finals.append(s_d)
        o_a = rmsnorm(outs[0] + outs[1], hgrn_norm_g[j]).reshape(bsz, t, D_A) * jax.nn.silu(og.astype(F32))
        xc = centred_dwconv(xr, rg_conv_w[j], rg_conv_b[j]).astype(F32)
        xblk = xc.reshape(bsz, t, B_BLOCKS, B_BLOCK)
        hs, lru_finals = [], []
        for d in range(2):
            gate_r = jax.nn.sigmoid(jnp.einsum('btgi,gij->btgj', xblk, rg_wa[j, d]).reshape(bsz, t, D_B) + rg_ba[j, d])
            gate_i = jax.nn.sigmoid(jnp.einsum('btgi,gij->btgj', xblk, rg_wx[j, d]).reshape(bsz, t, D_B) + rg_bx[j, d])
            log_a = -LRU_C * gate_r * jax.nn.softplus(-rg_lambda[j, d].astype(F32))
            b_in = jnp.sqrt(-jnp.expm1(2.0 * log_a)) * gate_i * xc
            fl = flip_t if d == 1 else ident
            h_d, s_d = linear_scan(fl(jnp.exp(log_a)), fl(b_in), s_rglru[:, d])
            hs.append(fl(h_d))
            lru_finals.append(s_d)
        o_b = (hs[0] + hs[1]) * jax.nn.gelu(yr.astype(F32))
        y = jnp.matmul(jnp.concatenate([o_a, o_b], axis=-1).astype(h.dtype), ab_w_out[j])
        return y, jnp.stack(finals, axis=1), jnp.stack(lru_finals, axis=1)

    def mixer_c(h, j, s_rwkv):
        bsz, t, _ = h.shape
        hp = jnp.pad(h, ((0, 0), (1, 1), (0, 0)))
        xx = 0.5 * (hp[:, :-2] + hp[:, 2:]) - h
        xr, xw, xk, xv, xa, xg = [h + xx * rw_mu[j, i] for i in range(6)]

        def heads(z):
            return z.astype(F32).reshape(bsz, t, C_HEADS, C_HEAD)
        r = heads(jnp.matmul(xr, rw_wr[j]))
        k = jnp.matmul(xk, rw_wk[j])
        v = heads(jnp.matmul(xv, rw_wv[j]))
        g = jnp.matmul(jax.nn.sigmoid(jnp.matmul(xg, rw_g1[j])), rw_g2[j]).astype(F32)
        kk = heads(k * rw_kk[j])
        kk = kk / jnp.maximum(jnp.sqrt(jnp.sum(kk * kk, axis=-1, keepdims=True)), 1e-12)
        kh = heads(k)
        k_a = rw_ka[j].astype(F32).reshape(C_HEADS, C_HEAD)
        r_k = rw_rk[j].astype(F32)
        o_sum = 0.0
        bonus = 0.0
        finals = []
        for d in range(2):
            w_in = rw_w0[j, d] + jnp.matmul(jnp.tanh(jnp.matmul(xw, rw_w1[j, d])), rw_w2[j, d])
            w = heads(jnp.exp(-W_DECAY_SCALE * jax.nn.sigmoid(w_in.astype(F32))))
            a = heads(jax.nn.sigmoid((rw_a0[j, d] + jnp.matmul(jnp.matmul(xa, rw_a1[j, d]), rw_a2[j, d])).astype(F32)))
            kd = kh * (1.0 + (a - 1.0) * k_a)
            fl = flip_t if d == 1 else ident
            o_d, s_d = rwkv7_scan(fl(r), fl(w), fl(kd), fl(v), fl(kk), fl(a), s_rwkv[:, d])
            o_sum = o_sum + fl(o_d)
            bonus = bonus + jnp.sum(r * kd * r_k, axis=-1, keepdims=True) * v
            finals.append(s_d)
        mu = jnp.mean(o_sum, axis=-1, keepdims=True)
        var = jnp.mean(jnp.square(o_sum - mu), axis=-1, keepdims=True)
        o = (o_sum - mu) * lax.rsqrt(var + GN_EPS) * rw_lnw[j].astype(F32).reshape(C_HEADS, C_HEAD) \
            + rw_lnb[j].astype(F32).reshape(C_HEADS, C_HEAD)
        o = (o + bonus).reshape(bsz, t, D_MODEL) * g
        return jnp.matmul(o.astype(h.dtype), rw_wo[j]), jnp.stack(finals, axis=1)

    def trunk(x, cvec, s_hgrn, s_rglru, s_rwkv):
        st_h, st_r, st_w = [], [], []
        for l in range(DEPTH):
            sh1, sc1, gt1, sh2, sc2, gt2 = [m.astype(x.dtype) for m in ada_modulation(cvec, w_mod[l], b_mod[l])]
            h = rmsnorm(x, norm_mix_g[l]) * (1.0 + sc1) + sh1
            j = l // 2
            if l % 2 == 0:
                y, s_a, s_b = mixer_ab(h, j, s_hgrn[:, j], s_rglru[:, j])
                st_h.append(s_a)
                st_r.append(s_b)
            else:
                y, s_c = mixer_c(h, j, s_rwkv[:, j])
                st_w.append(s_c)
            x = x + gt1 * y.astype(x.dtype)
            h = rmsnorm(x, norm_ffn_g[l]) * (1.0 + sc2) + sh2
            x = x + gt2 * moe_ffn(h, moe_router, moe_router_bias, moe_w1[l], moe_w3[l], moe_w2[l]).astype(x.dtype)
        return rmsnorm(x, norm_f_g), jnp.stack(st_h, axis=1), jnp.stack(st_r, axis=1), jnp.stack(st_w, axis=1)

    bp = x_prompt.shape[0]
    z_h = jnp.zeros((bp, N_AB, 2, A_HEADS, A_DK, A_DV), F32)
    z_r = jnp.zeros((bp, N_AB, 2, D_B), F32)
    z_w = jnp.zeros((bp, N_C, 2, C_HEADS, C_HEAD, C_HEAD), F32)
    y_prompt, new_state_hgrn, new_state_rglru, new_state_rwkv = trunk(x_prompt, c_ctx, z_h, z_r, z_w)

    xs = x_sample + grid_pos_embed(x_sample.shape[1]).astype(x_sample.dtype)
    y_sample, _, _, _ = trunk(xs, c, state_hgrn, state_rglru, state_rwkv)
    return (y_prompt, y_sample, new_state_hgrn, new_state_rglru, new_state_rwkv)


_drawn_inputs = setup_inputs


def setup_inputs(seed=0):
    import zlib

    import numpy as np

    out = dict(_drawn_inputs(seed))
    spreads = {}
    factors = {'state_hgrn': 64.0,
     'state_rwkv': 8.0,
     'rg_ba': 17.155,
     'rg_bx': 4.012,
     'rw_lnw': 4.374,
     'rw_lnb': 7.164}
    for name, (base, spread) in spreads.items():
        noise = np.random.default_rng([zlib.crc32(name.encode()), seed]).standard_normal(out[name].shape)
        drawn = base * np.exp(spread * noise) if base else spread * noise
        out[name] = jnp.asarray(drawn.astype(out[name].dtype))
    for name, factor in factors.items():
        out[name] = (out[name] * factor).astype(out[name].dtype)
    return out
```

```python
import concourse.bass as bass
from concourse import mybir
from contextlib import ExitStack

P = 128
D = 1024
KT = D // P
CTX = 128
LAT = 512
NT = CTX + LAT
NCH = NT // P
SEGS = ((0, CTX), (CTX, NT))
GRID_W = 64
DA = D // 2
NH_A = DA // P
NTA = DA // P
LEVELS = 7
HD = 64
EPS_RMS = 1e-6
EPS_GN = 64e-5
W_DECAY = 0.6065306597126334
LRU_C = 8.0
NE = 16
NG = 4
EPG = NE // NG
DE = 256
SLOT = 2048
RING_W = 3
RING_P = 4
TW = 1024
HG = 4
NGRP = 16 // HG
UC = HG // 2
UW = UC * P

C_IDENT, C_ONES, C_BONES, C_HSEL, C_EPS = 0, 128, 256, 384, 386
C_RMASK = 388
C_GMASK = C_RMASK + 4 * P
C_PERSIST = C_GMASK + 2 * P + 2 * (LEVELS - 1) * HD
C_LMASK = C_PERSIST
C_SCAN = C_LMASK + LEVELS * P
C_POS = C_SCAN + 2 * NT
C_ALL = C_POS + 4 * (LAT // GRID_W) + 4 * GRID_W

VECS = [("b_mod", 96), ("hgrn_lb", 16), ("hgrn_norm_g", 1), ("c", 8),
        ("rw_mu", 48), ("rg_conv_w", 16), ("rg_conv_b", 4), ("rg_ba", 8), ("rg_bx", 8), ("rg_lambda", 8),
        ("norm_f_g", 8), ("c_ctx", 8), ("state_rglru", 8),
        ("norm_mix_g", 16), ("norm_ffn_g", 16), ("rw_w0", 16), ("rw_a0", 16), ("rw_kk", 8), ("rw_ka", 8),
        ("rw_rk", 8), ("rw_lnw", 8), ("rw_lnb", 8)]


def vec_places():
    at, place = 0, {}
    for name, rows in VECS:
        if at // P != (at + rows - 1) // P:
            at = (at // P + 1) * P
        place[name] = at
        at += rows
    assert at <= 3 * P
    return place


def mod_pieces(layer, part):
    return range(0, 8) if (layer, part) == (0, 0) else range(8, 24) if layer == 0 else range(0, 24)


def next_step(g, st):
    return (g, st + 1) if st + 1 < NCH else (g + 1, 0)


def tile_plan():
    names = [("vecT", 1)]
    names += [("xT", KT), ("mod0a", 8), ("norm0", 1), ("xr", 4), ("yr", 4)]
    for u in range(8):
        names += [(f"gate{u}", 2), (f"qk{u}", 1)]
        if u % 2 == 1:
            names += [(f"mod0b{u // 2}", 4)]
    names += [("kb", 4), ("v", NCH), ("og", 4), ("lruT", 1)]
    for h in range(NH_A):
        names += [(f"lvl{h}", LEVELS + 1), (f"khT{h}", 2), (f"U{h}", 2), (f"o{h}", 1), (f"on{h}", 1)]
    names += [("wout", KT), ("norm1", 1), ("router0", 1), ("combT0", 1)]
    for e in range(NE):
        names += [(f"ex0_{e}", 5), (f"mod1_{e}", 2 if e < 8 else 1)]
    names += [("w2_0", KT), ("norm2", 1), ("lora", 3), ("r", KT), ("k", KT), ("V", 2 * NCH), ("stT", 2)]
    for g in range(NGRP):
        for st in range(NCH):
            u = f"_{g}_{st}"
            if (g, st) == (0, 0):
                names += [("P" + u, 2)]
            names += [("AR" + u, 2), ("BR" + u, 2), ("AN" + u, 2), ("M0" + u, 2)]
            for lv in range(1, LEVELS):
                names += [(f"G{lv}" + u, 2)]
                if lv == 2 and (g, st) != (NGRP - 1, NCH - 1):
                    gn, sn = next_step(g, st)
                    names += [(f"P_{gn}_{sn}", 2)]
                names += [(f"D{lv}" + u, 2)]
            names += [("N6" + u, 2), ("RHS" + u, 2), ("Us" + u, 2), ("OT" + u, 2)]
            if st == 0:
                names += [("fin" + u, 1)]
    for k in range(KT):
        names += [(f"post{k}", 3)]
    names += [("wo", KT), ("norm3", 1), ("router1", 1), ("combT1", 1)]
    names += [(f"ex1_{e}", 5) for e in range(NE)]
    names += [("w2_1", KT), ("norm4", 1), ("yT", NCH)]
    base, at = {}, 0
    for name, n in names:
        base[name] = at
        at += n
    return base


def build(nc, A, const, outs, xspill):
    f32 = mybir.dt.float32
    i32 = mybir.dt.int32
    ALU = mybir.AluOpType
    ACT = mybir.ActivationFunctionType
    AX = mybir.AxisListType
    T = tile_plan()
    VB = vec_places()
    ctx = ExitStack()
    with ctx:
        def sb(name, n):
            return ctx.enter_context(nc.sbuf_tensor(name, [P, n], f32))

        def sem(name):
            return ctx.enter_context(nc.semaphore(name))

        Xf = sb("x_resid", KT * NT)
        Hf = sb("h_normed", KT * NT)
        Wf = sb("weight_ring", RING_W * SLOT)
        CO = sb("consts", C_PERSIST)
        VT = sb("vectors", 3 * P)
        MODf = sb("modulation", 2 * 48 * 2)
        SM = sb("small", 432)
        ARENA_N = 53200 - (2 * KT * NT + RING_W * SLOT + C_PERSIST + 3 * P + 192 + 432)
        AR = sb("arena", ARENA_N)
        PSt = ctx.enter_context(nc.psum_tensor("psum_ring", [P, RING_P * TW], f32))

        X = Xf[:, :].rearrange("p (k t) -> p k t", k=KT)
        H = Hf[:, :].rearrange("p (k t) -> p k t", k=KT)
        MOD = MODf[:, :].rearrange("p (l j s) -> p l j s", l=2, j=48)
        ident = CO[:, C_IDENT:C_IDENT + P]
        ones = CO[:, C_ONES:C_ONES + P]
        bones = CO[:, C_BONES:C_BONES + P]
        hsel = CO[:, C_HSEL:C_HSEL + 2]
        eps_rms = CO[:, C_EPS:C_EPS + 1]
        eps_gn = CO[:, C_EPS + 1:C_EPS + 2]

        def vcol(name, i, n=1):
            return VT[:, VB[name] + i:VB[name] + i + n]

        arena_at = [0, 0]

        def carve(n):
            a = arena_at[0]
            arena_at[0] += n
            assert arena_at[0] <= ARENA_N, (arena_at[0], ARENA_N)
            return AR[:, a:a + n]

        sm_at = [0]

        def small(n):
            a = sm_at[0]
            sm_at[0] += n
            assert sm_at[0] <= 432
            return SM[:, a:a + n]

        silu_c = small(16)
        coef = [small(16) for _ in range(4)]
        lb = small(8)
        omlb = small(8)
        lbt = small(16)
        splam = small(8)
        nsp8 = small(8)
        psp8 = small(8)
        lru_fin = small(8)
        nw0 = small(16)
        na0 = small(16)
        omka = small(8)
        gend = small(16)
        half_one = small(4)
        hb = small(8)
        em = small(8)
        rwR = small(KT * NE)
        rbias = small(NE)
        lut = small(48)

        psum_full = sem("psum_full")
        psum_free = [sem(f"psum_free{i}") for i in range(RING_P)]
        w_landed = [sem(f"w_landed{i}") for i in range(RING_W)]
        dve_chain = sem("dve_chain")
        act_chain = sem("act_chain")
        S = {name: sem(name) for name in (
            "consts_in", "consts_l0", "vec_clear", "vec_in", "x_in", "silu_c", "lb_diff", "lb_exp", "lb_done",
            "sq_ready", "coef_ready", "rms_root", "h_scaled", "h_affine",
            "gates_clear", "gates_in", "router_in", "conv_base", "lru_th", "lru_q", "lru_root", "lru_done",
            "lru_rows", "lru_sent", "f_log", "b_ready", "head_diff", "head_exp", "head_ready",
            "lvl_diff", "lvl_exp", "lvl_q", "lvl_k", "st_in", "s_final", "s_final_sent", "on_root", "o_a_ready",
            "comb_ready", "hid_done", "x_parked", "x_back", "xi_ready", "lora_in", "rw_st_in", "rw_clear",
            "kk_sq", "gates_exp", "kk_norm", "decay_sum", "decay_exp", "unit_ready", "kb_t", "mn_ready",
            "rhs_out", "r0_ready", "n_out", "gates_clamped", "gates_done", "ctx_state", "ctx_state_sent", "scan_done", "gn_centred", "gn_sq", "gn_var", "gn_root",
            "z_ready", "y_sent")}

        def full(eng, n):
            eng.wait_ge(psum_full, n + 1)
            return tile(n)

        def tile(n):
            return PSt[:, (n % RING_P) * TW:(n % RING_P + 1) * TW]

        def free(ins, n):
            ins.then_inc(psum_free[n % RING_P], 1)

        def read_out(eng, n):
            eng.wait_ge(psum_free[n % RING_P], n // RING_P + 1)

        stream = []

        def cols(w, c0, n, kt=KT):
            return (lambda s: s[:, 0:kt * n].rearrange("p (k c) -> p k c", c=n),
                    w.rearrange("(k p) c -> p k c", p=P)[:, :, c0:c0 + n])

        def add(key, last_tile, *parts):
            stream.append((key, last_tile, parts))

        def add_mod(layer, i, n):
            add(("mod", layer, i), n, cols(A["w_mod"][layer], 256 * i, 256))

        def add_in(i, n):
            add(("in", i), n, cols(A["ab_w_in"][0], 256 * i, 256))

        for i in range(8):
            add_mod(0, i, T["mod0a"] + i)
        for i in range(2):
            add_in(10 + i, T["xr"] + 2 * i + 1)
        for i in range(2):
            add_in(12 + i, T["yr"] + 2 * i + 1)
        for u in range(1, 8, 2):
            add_in(u // 2, T[f"qk{u}"])
            for q in range(4):
                add_mod(0, 8 + 4 * (u // 2) + q, T[f"mod0b{u // 2}"] + q)
        for i in range(2):
            add_in(4 + i, T["kb"] + 2 * i + 1)
        for i in range(2):
            add_in(6 + i, T["v"] + NCH - 1)
        for i in range(2):
            add_in(8 + i, T["og"] + 2 * i + 1)
        for i in range(4):
            add(("ab_w_out", i), T["wout"] + 2 * i + 1, cols(A["ab_w_out"][0], 256 * i, 256))

        def mods_of_expert(e):
            return (2 * e, 2 * e + 1) if e < 8 else (8 + e,)

        def add_moe(l):
            for e in range(NE):
                n = T[f"ex{l}_{e}"]
                add(("w1", l, e), n + 3, cols(A["moe_w1"][l, e], 0, DE))
                add(("w3", l, e), n + 4, cols(A["moe_w3"][l, e], 0, DE))
                if l == 0:
                    for q, i in enumerate(mods_of_expert(e)):
                        add_mod(1, i, T[f"mod1_{e}"] + q)
            w2 = A["moe_w2"][l].rearrange("e (f p) d -> p (e f) d", p=P)
            for dt in range(KT):
                for hf in range(2):
                    add(("w2", l, dt, hf), T[f"w2_{l}"] + dt,
                        (lambda s: s.rearrange("p (a c) -> p a c", c=P),
                         w2[:, 16 * hf:16 * hf + 16, dt * P:(dt + 1) * P]))

        add_moe(0)
        for q, name in enumerate(("rw_w1", "rw_a1")):
            w = A[name][0]
            add((name, 0), T["lora"] + q,
                *[((lambda s, d=d: s[:, 0:KT * P].rearrange("p (k c) -> p k c", c=P)[:, :, HD * d:HD * d + HD]),
                   w[d].rearrange("(k p) c -> p k c", p=P)) for d in range(2)])
        add(("rw_g1", 0), T["lora"] + 2, cols(A["rw_g1"][0], 0, P))
        for name, tn in (("rw_wr", "r"), ("rw_wk", "k")):
            for i in range(4):
                add((name, i), T[tn] + 2 * i + 1, cols(A[name][0], 256 * i, 256))
        for i in range(4):
            add(("rw_wv", i), T["V"] + NCH * (i // 2) + NCH - 1, cols(A["rw_wv"][0], 256 * i, 256))
        add(("rw_g2", 0), T["post7"] + 2, (lambda s: s[:, 0:D], A["rw_g2"][0]))
        for i in range(4):
            add(("rw_wo", i), T["wo"] + 2 * i + 1, cols(A["rw_wo"][0], 256 * i, 256))
        add_moe(1)
        slot_no = {key: i for i, (key, _, _) in enumerate(stream)}
        landed_at, per_slot = [], [0] * RING_W
        for i, (_, _, parts) in enumerate(stream):
            per_slot[i % RING_W] += 16 * len(parts)
            landed_at.append(per_slot[i % RING_W])

        def slot(i):
            return Wf[:, (i % RING_W) * SLOT:(i % RING_W + 1) * SLOT]

        l0c = carve(C_ALL - C_PERSIST)
        lmask = [l0c[:, i * P:(i + 1) * P] for i in range(LEVELS)]
        scanm = [l0c[:, C_SCAN - C_PERSIST + d * NT:C_SCAN - C_PERSIST + (d + 1) * NT] for d in range(2)]
        pos_r = l0c[:, C_POS - C_PERSIST:C_POS - C_PERSIST + 32]
        pos_c = l0c[:, C_POS - C_PERSIST + 32:C_POS - C_PERSIST + 32 + 256]
        nA = NTA * NT
        XCf, YGf, Qf, OGf = carve(nA), carve(nA), carve(nA), carve(nA)
        Kf = [carve(nA), carve(nA)]
        Bf = [carve(nA), carve(nA)]
        VAf = carve(NCH * DA)
        GW = carve(16 * P)
        lr, li, la, lth, lh = [carve(NT) for _ in range(5)]
        t3 = lambda a, k=NTA: a.rearrange("p (k t) -> p k t", k=k)
        XC, YG, Q, OG = t3(XCf), t3(YGf), t3(Qf), t3(OGf)
        K = [t3(a) for a in Kf]
        B = [t3(a) for a in Bf]
        VA = t3(VAf, NCH)
        vrow = XCf[:, 0:3 * P]
        xtok = Hf[:, :].rearrange("p (c d) -> p c d", d=D)
        hs_at = [0]

        def hcarve(n):
            a = hs_at[0]
            hs_at[0] += n
            return Hf[:, a:a + n]

        ATT = hcarve(NT)
        EQ = [hcarve(NT) for _ in range(2)]
        EK = [hcarve(NT) for _ in range(2)]
        QIN = [hcarve(NT) for _ in range(2)]
        hs_at[0] == 7 * NT
        KHT = [XCf[:, 0:NT], XCf[:, NT:2 * NT]]
        KH = [XCf[:, 2 * NT:3 * NT], XCf[:, 3 * NT:4 * NT]]
        SST = [GW[:, 0:4 * P], GW[:, 4 * P:8 * P]]
        SIN = GW[:, 8 * P:16 * P]
        OCP, OSQ = lr, li
        SFIN = [la[:, 0:P], la[:, P:2 * P]]
        l0_end = arena_at[0]

        arena_at[0] = 0
        HID = carve(2 * NE * NT).rearrange("p (j t) -> p j t", t=NT)
        SG = [carve(NT) for _ in range(2)]
        CB = [carve(NT) for _ in range(2)]
        combT = carve(NT)
        sc_, sl_, ch_, gs_, w0_, w1_, w2_ = [carve(NCH * NE) for _ in range(7)]

        arena_at[0] = 0
        Rf, KKf, VVf = carve(KT * NT), carve(KT * NT), carve(NCH * D)
        R1 = Rf.rearrange("p (k t) -> p k t", k=KT)
        K1 = KKf.rearrange("p (k t) -> p k t", k=KT)
        V1 = VVf.rearrange("p (c d) -> p c d", d=D)
        hw, ha, hg = carve(NT), carve(NT), carve(NT)
        W2s, A2s = carve(D), carve(D)
        STf = carve(16 * HD)
        ST = STf.rearrange("p (j v) -> p j v", v=HD)
        BON = carve(NCH * 16).rearrange("p (c h) -> p c h", h=16)
        mark = arena_at[0]
        XXf = carve(KT * NT)
        XX = XXf.rearrange("p (k t) -> p k t", k=KT)
        XIf = Xf
        XI = XIf[:, :].rearrange("p (k t) -> p k t", k=KT)
        arena_at[0] = mark
        OT = Hf[:, :].rearrange("p (c d) -> p c d", d=D)
        STR = []
        xat = [0]

        def stream_carve(n):
            if arena_at[0] + n <= ARENA_N:
                return carve(n)
            a = xat[0]
            xat[0] += n
            assert xat[0] <= KT * NT, (xat, arena_at, ARENA_N)
            return Xf[:, a:a + n]

        for d in range(2):
            z = {}
            for name, n in (("LA", 2 * UW), ("B", UW), ("E1", UW), ("E2", UW), ("E3", UW), ("KK", UW), ("SQ", UW),
                            ("BE", UW), ("KP", UW), ("RHS4_0", 4 * UW), ("RHS4_1", 4 * UW), ("KBT", 2 * UW),
                            ("AR", HG * 256), ("BR", HG * 256), ("M", HG * P), ("N", HG * P), ("G", HG * HD),
                            ("RHU", 2 * HG * HD), ("R0", UC * HD), ("SF", UC * HD)):
                z[name] = stream_carve(n)
            z["RH"], z["U"] = z["RHU"][:, 0:HG * HD], z["RHU"][:, HG * HD:]
            z["KD"] = z["B"]
            STR.append(z)
        NATST = STR[0]["AR"], STR[0]["BR"]
        FINB = STR[1]["RHU"]
        OC = R1
        Z2 = KKf.rearrange("p (c d) -> p c d", d=D)
        GNS = [STR[0]["AR"][:, i * 16 * NCH:(i + 1) * 16 * NCH] for i in range(3)]
        YT = AR[:, 0:NCH * D].rearrange("p (c d) -> p c d", d=D)
        KSUM, LROWS = lh, lth

        def unit_id(g, st, d):
            return (g * NCH + st) * 2 + d

        def n_count(g, st, lv, d):
            return 2 * ((g * NCH + st) * (LEVELS - 2) + lv - 2) + d + 1

        def chunk_of(st, d):
            return 0 if st == 0 else (st if d == 0 else NCH - st)

        def hgrn_state(d, c, h):
            if c == (1 if d == 0 else NCH - 1):
                return SIN[:, (d * NH_A + h) * P:(d * NH_A + h + 1) * P]
            return SST[d][:, (c - 1) * P:c * P]

        block = ctx.enter_context(nc.Block())

        @block.sync
        def _(sp):
            sp.dma_start(CO[:, :], const[:, 0:C_PERSIST]).then_inc(S["consts_in"], 16)
            sp.dma_start(l0c, const[:, C_PERSIST:C_ALL]).then_inc(S["consts_l0"], 16)
            sp.dma_start(xtok[:, 0, :], A["x_prompt"][0]).then_inc(S["x_in"], 16)
            sp.dma_start(xtok[:, 1:NCH, :], A["x_sample"][0].rearrange("(c p) d -> p c d", p=P)).then_inc(S["x_in"], 16)
            for i, (key, _, parts) in enumerate(stream):
                if i >= RING_W:
                    sp.wait_ge(psum_full, stream[i - RING_W][1] + 1)
                for view, src in parts:
                    sp.dma_start(view(slot(i)), src).then_inc(w_landed[i % RING_W], 16)
            for c in range(NCH):
                read_out(sp, T["yT"] + c)
                dst = outs["y_prompt"][0] if c == 0 else outs["y_sample"][0, (c - 1) * P:c * P, :]
                sp.dma_start(dst, YT[:, c, :]).then_inc(S["y_sent"], 16)
            sp.wait_ge(S["y_sent"], 16 * NCH)

        @block.gpsimd
        def _(pool):
            nc.gpsimd.memset(vrow, 0.0).then_inc(S["vec_clear"], 1)
            pool.wait_ge(S["vec_clear"], 1)
            for name, rows in VECS:
                at = VB[name]
                src = A[name]
                nd = len(src.shape)
                letters = " ".join("abcdefg"[:nd])
                flat = src.rearrange(f"{letters} -> ({letters})") if nd > 1 else src
                pool.dma_start(vrow[at % P:at % P + rows, (at // P) * P:(at // P + 1) * P],
                               flat.rearrange("(r c) -> r c", c=P)).then_inc(S["vec_in"], 16)
            nc.gpsimd.memset(GW, 0.0).then_inc(S["gates_clear"], 1)
            pool.wait_ge(S["gates_clear"], 1)
            gw = GW.rearrange("p (j c) -> p j c", c=P)
            for wi, name in enumerate(("rg_wa", "rg_wx")):
                for d in range(2):
                    src = A[name][0, d].rearrange("(c b) i j -> b i c j", b=2)
                    for b in range(2):
                        j0 = (d * 2 + wi) * 4
                        pool.dma_start(gw[HD * b:HD * b + HD, j0:j0 + 4, HD * b:HD * b + HD],
                                       src[b]).then_inc(S["gates_in"], 16)
            pool.dma_start(rwR.rearrange("p (k e) -> p k e", e=NE),
                           A["moe_router"].rearrange("(k p) e -> p k e", p=P)).then_inc(S["router_in"], 16)
            rb = A["moe_router_bias"].rearrange("(o e) -> o e", o=1)
            pool.dma_start(rbias, rb.to_broadcast([P, NE])).then_inc(S["router_in"], 16)
            pool.wait_ge(psum_full, T["gate7"] + 2)
            pool.dma_start(SIN.rearrange("p (j v) -> p j v", v=P),
                           A["state_hgrn"][0, 0].rearrange("d h k v -> k (d h) v")).then_inc(S["st_in"], 16)
            for h in range(NH_A):
                for lv in range(LEVELS):
                    i = h * LEVELS + lv
                    s = 1 << lv
                    nb = NT // (2 * s)
                    ek = EK[i % 2].rearrange("p (n two s) -> p n two s", two=2, s=s)
                    kf = K[0][:, h, :].rearrange("p (n two s) -> p n two s", two=2, s=s)
                    kb = K[1][:, h, :].rearrange("p (n two s) -> p n two s", two=2, s=s)
                    pool.wait_ge(S["lvl_exp"], 2 * i + 2)
                    nc.gpsimd.tensor_tensor(ek[:, :, 0, :], ek[:, :, 0, :], kf[:, :, 0, :], ALU.mult)
                    nc.gpsimd.tensor_tensor(ek[:, :, 1, :], ek[:, :, 1, :], kb[:, :, 1, :],
                                            ALU.mult).then_inc(S["lvl_k"], 1)
            pool.wait_ge(psum_full, T["w2_0"] + KT)
            for dst, name in ((W2s, "rw_w2"), (A2s, "rw_a2")):
                pool.dma_start(dst, A[name][0].rearrange("d r c -> (d r) c")).then_inc(S["lora_in"], 16)
            pool.wait_ge(psum_full, T["V"] + 2 * NCH)
            stsrc = A["state_rwkv"][0, 0]
            for d in range(2):
                pool.dma_start(NATST[d][0:HD, :].rearrange("v (h k) -> v h k", k=HD),
                               stsrc[d].rearrange("h v k -> v h k")).then_inc(S["rw_st_in"], 16)
            for d in range(2):
                for q in range(2):
                    nc.gpsimd.memset(STR[d][f"RHS4_{q}"], 0.0).then_inc(S["rw_clear"], 1)
            nc.gpsimd.memset(Hf[:, :], 0.0).then_inc(S["rw_clear"], 1)
            nc.gpsimd.memset(BON, 0.0).then_inc(S["rw_clear"], 1)

        @block.tensor
        def _(pe):
            nxt = [0]

            def open_tile(n):
                assert n == nxt[0], (n, nxt[0])
                nxt[0] += 1
                if n >= RING_P:
                    pe.wait_ge(psum_free[n % RING_P], n // RING_P)
                return tile(n)

            def done(ins):
                ins.then_inc(psum_full, 1)

            def weights(key, c=256, kt=KT):
                i = slot_no[key]
                pe.wait_ge(w_landed[i % RING_W], landed_at[i])
                return slot(i)[:, 0:kt * c].rearrange("p (k c) -> p k c", c=c)

            def mm(out, lhsT, rhs, start=True, stop=True):
                return nc.tensor.matmul(out, lhsT, rhs, start=start, stop=stop)

            def wide(ps, lhsT, rhs, start=True, stop=True):
                mm(ps[:, 0:512], lhsT, rhs[:, 0:512], start, stop)
                return mm(ps[:, 512:NT], lhsT, rhs[:, 512:NT], start, stop)

            def project(n, key, j, rhs, c=256):
                w = weights(key, c)
                ps = open_tile(n)
                for k in range(KT):
                    ins = wide(ps, w[:, k, j * P:(j + 1) * P], rhs(k), k == 0, k == KT - 1)
                done(ins)

            def project_tokens(n0, keys, lhs):
                ws = [weights(key) for key in keys]
                for c in range(NCH):
                    ps = open_tile(n0 + c)
                    for q in range(2):
                        for k in range(KT):
                            ins = mm(ps[:, 256 * q:256 * q + 256], lhs[:, k, c * P:(c + 1) * P], ws[q][:, k, :],
                                     k == 0, k == KT - 1)
                    done(ins)

            def mod_piece(n, layer, i):
                w = weights(("mod", layer, i))
                ps = open_tile(n)
                for j in range(2):
                    for k in range(KT):
                        ins = mm(ps[:, 2 * j:2 * j + 2], w[:, k, j * P:(j + 1) * P], silu_c[:, 2 * k:2 * k + 2],
                                 k == 0, k == KT - 1)
                done(ins)

            def norm_sums(i):
                ps = open_tile(T[f"norm{i}"])
                for k in range(KT):
                    pe.wait_ge(S["sq_ready"], KT * i + k + 1)
                    ins = wide(ps, ones, H[:, k, :], k == 0, k == KT - 1)
                done(ins)

            def h_ready(i):
                pe.wait_ge(S["h_affine"], 2 * KT * (i + 1))

            def moe(l):
                if l == 0:
                    pe.wait_ge(S["router_in"], 32)
                ps = open_tile(T[f"router{l}"])
                for c in range(NCH):
                    for k in range(KT):
                        ins = mm(ps[:, c * NE:(c + 1) * NE], H[:, k, c * P:(c + 1) * P], rwR[:, k * NE:(k + 1) * NE],
                                 k == 0, k == KT - 1)
                done(ins)
                pe.wait_ge(S["comb_ready"], l + 1)
                ps = open_tile(T[f"combT{l}"])
                for c in range(NCH):
                    ins = nc.tensor.transpose(ps[0:NE, c * P:(c + 1) * P], ch_[:, c * NE:(c + 1) * NE], ident)
                done(ins)
                read_out(pe, T[f"combT{l}"])
                for e in range(NE):
                    n = T[f"ex{l}_{e}"]
                    ps = open_tile(n)
                    done(wide(ps, ident[0:NE, e:e + 1].to_broadcast([NE, P]), combT[0:NE, :]))
                    for j in range(2):
                        project(n + 1 + 2 * j, ("w1", l, e), j, lambda k: H[:, k, :])
                        project(n + 2 + 2 * j, ("w3", l, e), j, lambda k: H[:, k, :])
                    if l == 0:
                        for q, i in enumerate(mods_of_expert(e)):
                            mod_piece(T[f"mod1_{e}"] + q, 1, i)
                pe.wait_ge(S["hid_done"], 2 * NE * (l + 1))
                for dt in range(KT):
                    ps = open_tile(T[f"w2_{l}"] + dt)
                    for hf in range(2):
                        w = weights(("w2", l, dt, hf), P, 16)
                        for a in range(16):
                            ins = wide(ps, w[:, a, :], HID[:, 16 * hf + a, :], hf + a == 0, hf == 1 and a == 15)
                    done(ins)

            pe.wait_ge(S["consts_in"], 16)
            pe.wait_ge(S["vec_in"], 16 * len(VECS))
            ps = open_tile(T["vecT"])
            for i in range(3):
                ins = nc.tensor.transpose(ps[:, i * P:(i + 1) * P], vrow[:, i * P:(i + 1) * P], ident)
            done(ins)
            pe.wait_ge(S["x_in"], 32)
            for k in range(KT):
                ps = open_tile(T["xT"] + k)
                for c in range(NCH):
                    ins = nc.tensor.transpose(ps[:, c * P:(c + 1) * P], xtok[:, c, k * P:(k + 1) * P], ident)
                done(ins)
            pe.wait_ge(S["silu_c"], 1)
            for i in range(8):
                mod_piece(T["mod0a"] + i, 0, i)
            norm_sums(0)
            h_ready(0)
            for j in range(4):
                project(T["xr"] + j, ("in", 10 + j // 2), j % 2, lambda k: H[:, k, :])
            for j in range(4):
                project(T["yr"] + j, ("in", 12 + j // 2), j % 2, lambda k: H[:, k, :])
            gw = GW.rearrange("p (j c) -> p j c", c=P)
            pe.wait_ge(S["gates_in"], 16 * 8)
            for u in range(8):
                c, d = u // 2, u % 2
                read_out(pe, T["xr"] + c)
                for g in range(2):
                    ps = open_tile(T[f"gate{u}"] + g)
                    done(wide(ps, gw[:, (d * 2 + g) * 4 + c, :], XC[:, c, :]))
                project(T[f"qk{u}"], ("in", u // 2), u % 2, lambda k: H[:, k, :])
                if u % 2 == 1:
                    for q in range(4):
                        mod_piece(T[f"mod0b{u // 2}"] + q, 0, 8 + 4 * (u // 2) + q)
            for j in range(4):
                project(T["kb"] + j, ("in", 4 + j // 2), j % 2, lambda k: H[:, k, :])
            project_tokens(T["v"], [("in", 6), ("in", 7)], H)
            for j in range(4):
                project(T["og"] + j, ("in", 8 + j // 2), j % 2, lambda k: H[:, k, :])
            pe.wait_ge(S["lru_done"], 8)
            ps = open_tile(T["lruT"])
            done(nc.tensor.transpose(ps[0:8, 0:P], lru_fin, ident))
            pe.wait_ge(S["st_in"], 16)
            for h in range(NH_A):
                for lv in range(LEVELS):
                    i = h * LEVELS + lv
                    pe.wait_ge(S["lvl_q"], i + 1)
                    pe.wait_ge(S["lvl_k"], i + 1)
                    ps = open_tile(T[f"lvl{h}"] + lv)
                    for c in range(NCH):
                        cs = slice(c * P, (c + 1) * P)
                        ins = mm(ps[:, cs], EK[i % 2][:, cs], EQ[i % 2][:, cs])
                    done(ins)
                pe.wait_ge(S["head_ready"], h + 1)
                ps = open_tile(T[f"lvl{h}"] + LEVELS)
                for c in range(NCH):
                    cs = slice(c * P, (c + 1) * P)
                    ins = mm(ps[:, cs], KSUM[:, cs], Q[:, h, cs])
                done(ins)
                for d in range(2):
                    ps = open_tile(T[f"khT{h}"] + d)
                    for c in range(NCH):
                        ins = nc.tensor.transpose(ps[:, c * P:(c + 1) * P], KH[d][:, c * P:(c + 1) * P], ident)
                    done(ins)
                for d in range(2):
                    read_out(pe, T[f"khT{h}"] + d)
                    ps = open_tile(T[f"U{h}"] + d)
                    for c in range(NCH):
                        ins = mm(ps[:, c * P:(c + 1) * P], KHT[d][:, c * P:(c + 1) * P], VA[:, c, h * P:(h + 1) * P])
                    done(ins)
                read_out(pe, T[f"lvl{h}"] + LEVELS)
                for d in range(2):
                    read_out(pe, T[f"U{h}"] + d)
                ps = open_tile(T[f"o{h}"])
                for c in range(NCH):
                    cs = slice(c * P, (c + 1) * P)
                    ins = mm(ps[:, cs], VA[:, c, h * P:(h + 1) * P], ATT[:, cs], True, c == 0)
                    if c:
                        for d in range(2):
                            ins = mm(ps[:, cs], hgrn_state(d, c, h), QIN[d][:, cs], False, d == 1)
                done(ins)
                read_out(pe, T[f"o{h}"])
                ps = open_tile(T[f"on{h}"])
                done(wide(ps, ones, OSQ))
            pe.wait_ge(S["o_a_ready"], NH_A)
            for j in range(KT):
                project(T["wout"] + j, ("ab_w_out", j // 2), j % 2,
                        lambda k: OG[:, k, :] if k < NTA else YG[:, k - NTA, :])
            norm_sums(1)
            h_ready(1)
            moe(0)
            norm_sums(2)
            for q, name in enumerate(("rw_w1", "rw_a1", "rw_g1")):
                pe.wait_ge(S["xi_ready"], KT * (q + 1))
                project(T["lora"] + q, (name, 0), 0, lambda k: XI[:, k, :], P)
            for q, (tn, name) in enumerate((("r", "rw_wr"), ("k", "rw_wk"))):
                pe.wait_ge(S["xi_ready"], KT * (q + 4))
                for j in range(KT):
                    project(T[tn] + j, (name, j // 2), j % 2, lambda k: XI[:, k, :])
            pe.wait_ge(S["xi_ready"], KT * 6)
            for hf in range(2):
                project_tokens(T["V"] + hf * NCH, [("rw_wv", 2 * hf), ("rw_wv", 2 * hf + 1)], XI)
            pe.wait_ge(S["rw_st_in"], 32)
            for d in range(2):
                ps = open_tile(T["stT"] + d)
                for j in range(KT):
                    ins = nc.tensor.transpose(ps[:, j * HD:(j + 1) * HD], NATST[d][0:HD, j * P:(j + 1) * P],
                                              ident[0:HD, 0:HD])
                done(ins)
            pe.wait_ge(S["lora_in"], 32)

            def gate_tiles(g, st):
                for d in range(2):
                    z, ch, uid = STR[d], chunk_of(st, d), unit_id(g, st, d)
                    lo, ts = slice(HD * d, HD * d + HD), slice(ch * P, (ch + 1) * P)
                    ps = open_tile(T[f"P_{g}_{st}"] + d)
                    for q, (w2, hid) in enumerate(((W2s, hw), (A2s, ha))):
                        for j in range(UC):
                            ct = UC * g + j
                            mm(ps[:, (UC * q + j) * P:(UC * q + j + 1) * P], w2[lo, ct * P:(ct + 1) * P], hid[lo, ts])
                    pe.wait_ge(S["kk_sq"], uid + 1)
                    done(mm(ps[:, 2 * UW:3 * UW], bones, z["SQ"]))

            gate_tiles(0, 0)
            for g in range(NGRP):
                for st in range(NCH):
                    u = f"_{g}_{st}"
                    rh = f"RHS4_{(g * NCH + st) % 2}"
                    for d in range(2):
                        z = STR[d]
                        pe.wait_ge(S["unit_ready"], unit_id(g, st, d) + 1)
                        ps = open_tile(T["AR" + u] + d)
                        for j in range(UC):
                            ins = mm(ps[:, 512 * j:512 * j + 512], z["BE"][:, j * P:(j + 1) * P],
                                     z[rh][:, 512 * j:512 * j + 512])
                        done(ins)
                    for d in range(2):
                        z = STR[d]
                        ps = open_tile(T["BR" + u] + d)
                        for j in range(UC):
                            ins = mm(ps[:, 512 * j:512 * j + 512], z["KP"][:, j * P:(j + 1) * P],
                                     z[rh][:, 512 * j:512 * j + 512])
                        done(ins)
                    for d in range(2):
                        z = STR[d]
                        ps = open_tile(T["AN" + u] + d)
                        for j in range(UC):
                            mm(ps[:, 2 * j:2 * j + 2], z["SQ"][:, j * P:(j + 1) * P], hsel)
                        for q, key in enumerate(("KP", "BE")):
                            for j in range(UC):
                                c0 = 512 + (UC * q + j) * P
                                ins = nc.tensor.transpose(ps[:, c0:c0 + P], z[key][:, j * P:(j + 1) * P], ident)
                        done(ins)

                    def turn_over(ps, c0, src):
                        for hl in range(HG):
                            ins = nc.tensor.transpose(ps[:, c0 + hl * P:c0 + (hl + 1) * P],
                                                      src[:, hl * P:(hl + 1) * P], ident)
                        return ins

                    for d in range(2):
                        pe.wait_ge(S["mn_ready"], unit_id(g, st, d) + 1)
                        ps = open_tile(T["M0" + u] + d)
                        done(turn_over(ps, 0, STR[d]["N"]))
                    for lv in range(1, LEVELS):
                        s = 1 << lv
                        for d in range(2):
                            z = STR[d]
                            if lv == 1:
                                read_out(pe, T["M0" + u] + d)
                            else:
                                read_out(pe, T[f"D{lv - 1}" + u] + d)
                            ps = open_tile(T[f"G{lv}" + u] + d)
                            if lv > 1:
                                turn_over(ps, 512, z["M"])
                            for hl in range(HG):
                                m = z["M"][:, hl * P:(hl + 1) * P].rearrange("p (n w s) -> p n w s", w=2, s=s)
                                ins = mm(ps[:, hl * HD:(hl + 1) * HD], z["AR"][:, hl * 256:hl * 256 + P], m[:, :, d, :])
                            done(ins)
                        if lv == 2 and (g, st) != (NGRP - 1, NCH - 1):
                            gate_tiles(*next_step(g, st))
                        for d in range(2):
                            z, uid = STR[d], unit_id(g, st, d)
                            read_out(pe, T[f"G{lv}" + u] + d)
                            if lv > 1:
                                pe.wait_ge(S["n_out"], n_count(g, st, lv, d))
                            ps = open_tile(T[f"D{lv}" + u] + d)
                            for hl in range(HG):
                                ins = mm(ps[:, hl * HD:(hl + 1) * HD], z["N"][:, hl * P:(hl + 1) * P],
                                         z["G"][:, hl * HD:(hl + 1) * HD])
                            done(ins)
                    for d in range(2):
                        read_out(pe, T[f"D{LEVELS - 1}" + u] + d)
                        ps = open_tile(T["N6" + u] + d)
                        done(turn_over(ps, 0, STR[d]["M"]))
                    for d in range(2):
                        z, ch = STR[d], chunk_of(st, d)
                        if st:
                            pe.wait_ge(S["r0_ready"], 2 * (g * (NCH - 1) + st - 1) + d + 1)
                        ps = open_tile(T["RHS" + u] + d)
                        for hl in range(HG):
                            out = ps[:, hl * HD:(hl + 1) * HD]
                            hv = slice((HG * g + hl) * HD, (HG * g + hl + 1) * HD)
                            if st:
                                mm(out, z[rh][:, hl * 256:hl * 256 + P], z["R0"][:, (hl // 2) * HD:(hl // 2 + 1) * HD],
                                   True, False)
                            ins = mm(out, z["BR"][:, hl * 256:hl * 256 + P], V1[:, ch, hv], st == 0, True)
                        done(ins)
                    for d in range(2):
                        z = STR[d]
                        read_out(pe, T["RHS" + u] + d)
                        read_out(pe, T["N6" + u] + d)
                        ps = open_tile(T["Us" + u] + d)
                        for hl in range(HG):
                            ins = mm(ps[:, hl * HD:(hl + 1) * HD], z["N"][:, hl * P:(hl + 1) * P],
                                     z["RH"][:, hl * HD:(hl + 1) * HD])
                        done(ins)
                    for d in range(2):
                        z, ch = STR[d], chunk_of(st, d)
                        ps = open_tile(T["OT" + u] + d)
                        read_out(pe, T["Us" + u] + d)
                        pe.wait_ge(S["kb_t"], unit_id(g, st, d) + 1)
                        for j in range(UC):
                            out = ps[:, 512 + j * P:512 + (j + 1) * P]
                            pv = slice((UC * g + j) * P, (UC * g + j + 1) * P)
                            mm(out, z["KBT"][:, j * P:(j + 1) * P], V1[:, ch, pv], True, False)
                            mm(out, z["KBT"][:, (UC + j) * P:(UC + j + 1) * P], z["U"][:, j * P:(j + 1) * P],
                               False, True)
                        for hl in range(HG):
                            out = ps[:, hl * HD:(hl + 1) * HD]
                            hv = slice((HG * g + hl) * HD, (HG * g + hl + 1) * HD)
                            mm(out, z["BR"][:, hl * 256 + P:(hl + 1) * 256], V1[:, ch, hv], True, False)
                            ins = mm(out, z["AR"][:, hl * 256 + P:(hl + 1) * 256], z["U"][:, hl * HD:(hl + 1) * HD],
                                     False, st == 0)
                            if st:
                                ins = mm(out, z[rh][:, hl * 256 + P:(hl + 1) * 256],
                                         z["R0"][:, (hl // 2) * HD:(hl // 2 + 1) * HD], False, True)
                        done(ins)
                    if st == 0:
                        pe.wait_ge(S["ctx_state"], 2 * g + 2)
                        ps = open_tile(T["fin" + u])
                        for d in range(2):
                            for j in range(UC):
                                ins = nc.tensor.transpose(ps[0:HD, (UC * d + j) * P:(UC * d + j + 1) * P],
                                                          STR[d]["SF"][:, j * HD:(j + 1) * HD], ident)
                        done(ins)
            pe.wait_ge(S["z_ready"], NCH)
            for k in range(KT):
                for q, src in enumerate((OT, Z2)):
                    ps = open_tile(T[f"post{k}"] + q)
                    for c in range(NCH):
                        ins = nc.tensor.transpose(ps[:, c * P:(c + 1) * P], src[:, c, k * P:(k + 1) * P], ident)
                    done(ins)
                w = weights(("rw_g2", 0), D, 1)
                ps = open_tile(T[f"post{k}"] + 2)
                done(wide(ps, w[:, 0, k * P:(k + 1) * P], hg))
            read_out(pe, T["post7"] + 2)
            for j in range(KT):
                project(T["wo"] + j, ("rw_wo", j // 2), j % 2, lambda k: OC[:, k, :])
            norm_sums(3)
            h_ready(3)
            moe(1)
            norm_sums(4)
            pe.wait_ge(S["h_affine"], 4 * 2 * KT + KT)
            for c in range(NCH):
                ps = open_tile(T["yT"] + c)
                for k in range(KT):
                    ins = nc.tensor.transpose(ps[:, k * P:(k + 1) * P], H[:, k, c * P:(c + 1) * P], ident)
                done(ins)

        @block.scalar
        def _(act):
            n_chain = [0]
            A_ = nc.scalar.activation

            def link(ins):
                n_chain[0] += 1
                ins.then_inc(act_chain, 1)
                act.wait_ge(act_chain, n_chain[0])

            def squares():
                for k in range(KT):
                    A_(H[:, k, :], X[:, k, :], ACT.Square).then_inc(S["sq_ready"], 1)

            def norm_tail(i, layer, shift):
                n = T[f"norm{i}"]
                ps = full(act, n)
                A_(ps[:, 0:NT], ps[:, 0:NT], ACT.Sqrt, bias=eps_rms, scale=1.0 / D).then_inc(S["rms_root"], 1)
                if i < 4:
                    act.wait_ge(S["coef_ready"], i + 1)
                for k in range(KT):
                    if k % 4 == 0:
                        act.wait_ge(S["h_scaled"], 2 * i + k // 4 + 1)
                    if i == 4:
                        A_(H[:, k, :], H[:, k, :], ACT.Identity, scale=vcol("norm_f_g", k)).then_inc(S["h_affine"], 1)
                        continue
                    for s, (a, b) in enumerate(SEGS):
                        A_(H[:, k, a:b], H[:, k, a:b], ACT.Identity, scale=coef[i][:, 2 * k + s:2 * k + s + 1],
                           bias=MOD[:, layer, shift + k, s:s + 1]).then_inc(S["h_affine"], 1)

            def moe(l):
                n = T[f"router{l}"]
                ps = full(act, n)
                free(A_(sc_, ps[:, 0:NCH * NE], ACT.Sigmoid), n)
                for e in range(NE):
                    n = T[f"ex{l}_{e}"]
                    i = l * NE + e
                    ps = full(act, n)
                    if e >= 2:
                        act.wait_ge(S["hid_done"], 2 * (i - 1))
                    free(A_(CB[e % 2], ps[:, 0:NT], ACT.Copy), n)
                    for j in range(2):
                        ps = full(act, n + 1 + 2 * j)
                        if e >= 1:
                            act.wait_ge(S["hid_done"], 2 * (i - 1) + j + 1)
                        free(A_(SG[j], ps[:, 0:NT], ACT.Silu), n + 1 + 2 * j)

            read_out(act, T["vecT"])
            sc2 = silu_c.rearrange("p (k s) -> p k s", s=2)
            A_(sc2[:, :, 0], vcol("c_ctx", 0, KT), ACT.Silu)
            A_(sc2[:, :, 1], vcol("c", 0, KT), ACT.Silu).then_inc(S["silu_c"], 1)
            act.wait_ge(S["lb_diff"], 1)
            A_(lbt, lbt, ACT.Exp)
            A_(splam, splam, ACT.Exp, scale=-1.0).then_inc(S["lb_exp"], 1)
            read_out(act, T["xT"] + KT - 1)
            squares()
            norm_tail(0, 0, 0)
            act.wait_ge(S["lb_done"], 1)
            for j in range(4):
                n = T["xr"] + j
                ps = full(act, n)
                A_(XC[:, j, :], ps[:, 0:NT], ACT.Identity, scale=vcol("rg_conv_w", 2 * NTA + j),
                   bias=vcol("rg_conv_b", j)).then_inc(S["conv_base"], 1)
            for j in range(4):
                n = T["yr"] + j
                ps = full(act, n)
                free(A_(YG[:, j, :], ps[:, 0:NT], ACT.Gelu_apprx_tanh), n)
            for u in range(8):
                c, d = u // 2, u % 2
                n = T[f"gate{u}"]
                if u:
                    act.wait_ge(S["lru_done"], u)
                ps = full(act, n)
                free(A_(lr, ps[:, 0:NT], ACT.Sigmoid, bias=vcol("rg_ba", 4 * d + c)), n)
                ps = full(act, n + 1)
                free(A_(li, ps[:, 0:NT], ACT.Sigmoid, bias=vcol("rg_bx", 4 * d + c)), n + 1)
                read_out(act, n)
                A_(lth, lr, ACT.Tanh, scale=psp8[:, 4 * d + c:4 * d + c + 1])
                A_(la, lr, ACT.Exp, scale=nsp8[:, 4 * d + c:4 * d + c + 1]).then_inc(S["lru_th"], 1)
                act.wait_ge(S["lru_q"], u + 1)
                A_(lth, lth, ACT.Sqrt, scale=2.0).then_inc(S["lru_root"], 1)
                n = T[f"qk{u}"]
                ps = full(act, n)
                if u < 4:
                    free(A_(Q[:, u, :], ps[:, 0:NT], ACT.Silu), n)
                else:
                    A_(B[0][:, u - 4, :], ps[:, 0:NT], ACT.Sigmoid)
                    free(A_(K[0][:, u - 4, :], ps[:, 0:NT], ACT.Sigmoid, scale=-1.0), n)
            for j in range(4):
                n = T["kb"] + j
                ps = full(act, n)
                A_(B[1][:, j, :], ps[:, 0:NT], ACT.Sigmoid)
                free(A_(K[1][:, j, :], ps[:, 0:NT], ACT.Sigmoid, scale=-1.0), n)
            for c in range(NCH):
                n = T["v"] + c
                ps = full(act, n)
                free(A_(VA[:, c, :], ps[:, 0:DA], ACT.Copy), n)
            for d in range(2):
                if d == 1:
                    read_out(act, T["kb"] + 3)
                else:
                    read_out(act, T["qk7"])
                for j in range(4):
                    A_(B[d][:, j, :], B[d][:, j, :], ACT.Ln, scale=omlb[:, 4 * d + j:4 * d + j + 1],
                       bias=lb[:, 4 * d + j:4 * d + j + 1]).then_inc(S["f_log"], 1)
            for j in range(4):
                n = T["og"] + j
                ps = full(act, n)
                free(A_(OG[:, j, :], ps[:, 0:NT], ACT.Silu), n)
            read_out(act, T["lruT"])
            act.dma_start(outs["rglru"][0, 0].rearrange("d (c p) -> (d c) p", p=P),
                          LROWS[0:8, 0:P]).then_inc(S["lru_sent"], 16)
            for h in range(NH_A):
                act.wait_ge(S["head_diff"], h + 1)
                for d in range(2):
                    A_(KH[d], KH[d], ACT.Exp)
                    A_(QIN[d][:, CTX:NT], B[d][:, h, CTX:NT], ACT.Exp)
                    e0 = P - 1 if d == 0 else 0
                    ins = A_(gend[:, NCH * d:NCH * (d + 1)], B[d][:, h, e0::P], ACT.Exp)
                ins.then_inc(S["head_exp"], 1)
                for lv in range(LEVELS):
                    i = h * LEVELS + lv
                    act.wait_ge(S["lvl_diff"], i + 1)
                    A_(EQ[i % 2], EQ[i % 2], ACT.Exp).then_inc(S["lvl_exp"], 1)
                    A_(EK[i % 2], EK[i % 2], ACT.Exp).then_inc(S["lvl_exp"], 1)
                for d in range(2):
                    n = T[f"khT{h}"] + d
                    ps = full(act, n)
                    free(A_(KHT[d], ps[:, 0:NT], ACT.Copy), n)
                for d in range(2):
                    act.wait_ge(S["s_final"], 2 * h + d + 1)
                    act.dma_start(outs["hgrn"][0, 0, d, h], SFIN[d]).then_inc(S["s_final_sent"], 16)
                n = T[f"o{h}"]
                ps = full(act, n)
                if h:
                    act.wait_ge(S["o_a_ready"], h)
                A_(OCP, ps[:, 0:NT], ACT.Copy)
                free(A_(OSQ, ps[:, 0:NT], ACT.Square), n)
                n = T[f"on{h}"]
                ps = full(act, n)
                A_(ps[:, 0:NT], ps[:, 0:NT], ACT.Sqrt, bias=eps_rms, scale=1.0 / P).then_inc(S["on_root"], 1)
            act.wait_ge(S["lru_sent"], 16)
            act.wait_ge(S["s_final_sent"], 16 * 2 * NH_A)
            read_out(act, T["wout"] + KT - 1)
            squares()
            norm_tail(1, 0, 24)
            moe(0)
            read_out(act, T["w2_0"] + KT - 1)
            squares()
            norm_tail(2, 1, 0)
            act.dma_start(xspill, Xf[:, :]).then_inc(S["x_parked"], 16)
            for q, f in enumerate((ACT.Tanh, ACT.Copy, ACT.Sigmoid)):
                n = T["lora"] + q
                ps = full(act, n)
                free(A_((hw, ha, hg)[q], ps[:, 0:NT], f), n)
            for tn, dst in (("r", R1), ("k", K1)):
                for j in range(KT):
                    n = T[tn] + j
                    ps = full(act, n)
                    free(A_(dst[:, j, :], ps[:, 0:NT], ACT.Copy), n)
            for hf in range(2):
                for c in range(NCH):
                    n = T["V"] + hf * NCH + c
                    ps = full(act, n)
                    free(A_(V1[:, c, 512 * hf:512 * hf + 512], ps[:, 0:512], ACT.Copy), n)
            read_out(act, T["k"] + KT - 1)

            def key_squares(g, st, d):
                z, ch, uid = STR[d], chunk_of(st, d), unit_id(g, st, d)
                ts = slice(ch * P, (ch + 1) * P)
                if uid >= 2:
                    act.wait_ge(S["unit_ready"], uid - 1)
                    pg, pst = (g, st - 1) if st else (g - 1, NCH - 1)
                    act.wait_ge(psum_full, T[f"AN_{pg}_{pst}"] + d + 1)
                else:
                    act.wait_ge(psum_full, T["V"] + 2 * NCH)
                for j in range(UC):
                    ct = UC * g + j
                    ins = A_(z["KK"][:, j * P:(j + 1) * P], K1[:, ct, ts], ACT.Identity, scale=vcol("rw_kk", ct))
                link(ins)
                A_(z["SQ"], z["KK"], ACT.Square).then_inc(S["kk_sq"], 1)

            def gate_exps(g, st, d):
                z = STR[d]
                n = T[f"P_{g}_{st}"] + d
                ps = full(act, n)
                for q, nb in enumerate((nw0, na0)):
                    for j in range(UC):
                        c0 = (UC * q + j) * P
                        bi = 8 * d + UC * g + j
                        ins = A_(z["LA"][:, c0:c0 + P], ps[:, c0:c0 + P], ACT.Exp, scale=-1.0, bias=nb[:, bi:bi + 1])
                ins.then_inc(S["gates_exp"], 1)

            def gate_logs(g, st, d):
                z, uid = STR[d], unit_id(g, st, d)
                act.wait_ge(S["gates_clamped"], uid + 1)
                A_(z["SQ"], z["SQ"], ACT.Ln)
                link(A_(z["LA"], z["LA"], ACT.Ln, bias=half_one[:, 0:1]))
                A_(z["SQ"], z["SQ"], ACT.Exp, scale=-0.5)
                A_(z["LA"], z["LA"], ACT.Exp, scale=-1.0).then_inc(S["gates_done"], 1)

            def decay_exps(g, st, d):
                z, uid = STR[d], unit_id(g, st, d)
                h0 = 4 * ((g * NCH + st) % 2) + 2 * d
                act.wait_ge(S["decay_sum"], uid + 1)
                A_(em[:, h0:h0 + 2], hb[:, h0:h0 + 2], ACT.Exp, scale=-W_DECAY)
                A_(z["E1"], z["B"], ACT.Exp, scale=-W_DECAY)
                A_(z["E2"], z["B"], ACT.Exp, scale=W_DECAY)
                A_(z["E3"], z["E3"], ACT.Exp, scale=-W_DECAY).then_inc(S["decay_exp"], 1)

            act.preload_act_table_set("natural_log_exp_and_others")
            for stage in (key_squares, gate_exps, gate_logs, decay_exps):
                for d in range(2):
                    stage(0, 0, d)
            for g in range(NGRP):
                for st in range(NCH):
                    u = f"_{g}_{st}"
                    nx = None if (g, st) == (NGRP - 1, NCH - 1) else next_step(g, st)
                    for d in range(2):
                        n = T["AN" + u] + d
                        ps = full(act, n)
                        A_(STR[d]["KBT"], ps[:, 512:512 + 2 * UW], ACT.Copy).then_inc(S["kb_t"], 1)
                    for d in range(2):
                        n = T["M0" + u] + d
                        ps = full(act, n)
                        free(A_(STR[d]["M"], ps[:, 0:HG * P], ACT.Copy), n)
                    if nx:
                        for d in range(2):
                            key_squares(*nx, d)
                    for lv in range(2, LEVELS):
                        for d in range(2):
                            ps = full(act, T[f"G{lv}" + u] + d)
                            A_(STR[d]["N"], ps[:, 512:512 + HG * P], ACT.Copy).then_inc(S["n_out"], 1)
                        if nx:
                            if lv == 2:
                                gate_exps(*nx, 0)
                                gate_exps(*nx, 1)
                            elif lv == 3:
                                gate_logs(*nx, 0)
                                gate_logs(*nx, 1)
                            elif lv == 4:
                                decay_exps(*nx, 0)
                            elif lv == 5:
                                decay_exps(*nx, 1)
                    for name, key, size, scale in (("N6", "N", HG * P, 1.0), ("RHS", "RH", HG * HD, 1.0),
                                                   ("Us", "U", HG * HD, -1.0)):
                        for d in range(2):
                            n = T[name + u] + d
                            ps = full(act, n)
                            if name == "RHS" and st == 1:
                                act.wait_ge(S["ctx_state_sent"], 32 * (g + 1))
                            free(A_(STR[d][key], ps[:, 0:size], ACT.Copy, scale=scale), n)
                    if st == 0:
                        read_out(act, T["fin" + u])
                        for d in range(2):
                            act.dma_start(outs["rwkv"][0, 0, d, HG * g:HG * (g + 1)].rearrange("h v k -> v h k"),
                                          FINB[0:HD, d * 256:(d + 1) * 256].rearrange("v (h k) -> v h k", k=HD)
                                          ).then_inc(S["ctx_state_sent"], 16)
            act.wait_ge(S["ctx_state_sent"], 32 * NGRP)
            act.wait_ge(S["scan_done"], 1)
            act.dma_start(Xf[:, :], xspill).then_inc(S["x_back"], 16)
            for c in range(NCH):
                act.wait_ge(S["gn_centred"], c + 1)
                A_(Z2[:, c, :], OT[:, c, :], ACT.Square).then_inc(S["gn_sq"], 1)
                act.wait_ge(S["gn_var"], c + 1)
                A_(GNS[1][:, 16 * c:16 * c + 16], GNS[1][:, 16 * c:16 * c + 16], ACT.Sqrt, bias=eps_gn,
                   scale=1.0 / HD).then_inc(S["gn_root"], 1)
            for k in range(KT):
                n = T[f"post{k}"]
                ps = full(act, n)
                free(A_(OC[:, k, :], ps[:, 0:NT], ACT.Identity, scale=vcol("rw_lnw", k), bias=vcol("rw_lnb", k)), n)
            read_out(act, T["wo"] + KT - 1)
            squares()
            norm_tail(3, 1, 24)
            moe(1)
            read_out(act, T["w2_1"] + KT - 1)
            squares()
            norm_tail(4, 1, 0)

        @block.vector
        def _(dve):
            n_chain = [0]
            TT = nc.vector.tensor_tensor
            TS = nc.vector.tensor_scalar
            STT = nc.vector.scalar_tensor_tensor

            def link(ins):
                n_chain[0] += 1
                ins.then_inc(dve_chain, 1)
                dve.wait_ge(dve_chain, n_chain[0])

            def mod_evac(n, layer, i):
                ps = full(dve, n)
                b = vcol("b_mod", 48 * layer + 2 * i, 2).unsqueeze(2).broadcast_to([P, 2, 2])
                free(TT(MOD[:, layer, 2 * i:2 * i + 2, :], ps[:, 0:4].rearrange("p (j s) -> p j s", s=2), b, ALU.add), n)

            def make_coef(i, layer, scale, g):
                gv = g.unsqueeze(2).broadcast_to([P, KT, 2])
                STT(coef[i].rearrange("p (k s) -> p k s", s=2), MOD[:, layer, scale:scale + KT, :], 1.0, gv,
                    ALU.add, ALU.mult).then_inc(S["coef_ready"], 1)

            def norm_apply(i):
                n = T[f"norm{i}"]
                dve.wait_ge(S["rms_root"], i + 1)
                ps = tile(n)
                link(nc.vector.reciprocal(ps[:, 0:NT], ps[:, 0:NT]))
                for q in range(2):
                    r = ps[:, 0:NT].unsqueeze(1).broadcast_to([P, 4, NT])
                    TT(H[:, 4 * q:4 * q + 4, :], X[:, 4 * q:4 * q + 4, :], r, ALU.mult).then_inc(S["h_scaled"], 1)
                dve.wait_ge(S["h_scaled"], 2 * i + 2)
                free(nc.vector.tensor_copy(lut[:, 0:1], ps[:, 0:1]), n)

            def residual(tn, layer, gate):
                for k in range(KT):
                    n = T[tn] + k
                    ps = full(dve, n)
                    for s, (a, b) in enumerate(SEGS):
                        ins = STT(X[:, k, a:b], ps[:, a:b], MOD[:, layer, gate + k, s:s + 1], X[:, k, a:b],
                                  ALU.mult, ALU.add)
                    free(ins, n)

            def moe(l):
                n = T[f"router{l}"]
                read_out(dve, n)
                sc3 = sc_.rearrange("p (c e) -> p c e", e=NE)
                sl3 = sl_.rearrange("p (c e) -> p c e", e=NE)
                bias = rbias.unsqueeze(1).broadcast_to([P, NCH, NE])
                link(TT(sl3, sc3, bias, ALU.add))
                sl = sl_.rearrange("p (g i) -> p g i", i=EPG)
                NGT = NCH * NG
                rank = w0_.rearrange("p (g i) -> p g i", i=EPG)
                t0, t1 = w1_[:, 0:NGT], w1_[:, NGT:2 * NGT]
                gsc, gmx = w1_[:, 2 * NGT:3 * NGT], w1_[:, 3 * NGT:4 * NGT]
                link(TT(gsc, sl[:, :, 0], sl[:, :, 1], ALU.add))
                for i in range(EPG):
                    for j in range(i + 1, EPG):
                        if (i, j) != (0, 1):
                            link(TT(t0, sl[:, :, i], sl[:, :, j], ALU.add))
                            link(TT(gsc, gsc, t0, ALU.max))
                g3 = gsc.rearrange("p (c g) -> p c g", g=NG)
                best = gs_[:, 0:NGT].rearrange("p (c g) -> p c g", g=NG)
                mx = gmx[:, 0:NCH]
                link(nc.vector.reduce_max(mx, g3, AX.X))
                link(TT(best, g3, mx.unsqueeze(2).broadcast_to([P, NCH, NG]), ALU.is_ge))
                seen = gmx[:, NCH:2 * NCH]
                inv = gmx[:, 2 * NCH:3 * NCH]
                link(nc.vector.tensor_copy(seen, best[:, :, 0]))
                for g in range(1, NG):
                    link(TS(inv, seen, -1.0, 1.0, ALU.mult, ALU.add))
                    link(TT(best[:, :, g], best[:, :, g], inv, ALU.mult))
                    link(TT(seen, seen, best[:, :, g], ALU.add))
                for i in range(EPG):
                    first = True
                    for j in range(EPG):
                        if j == i:
                            continue
                        op = ALU.is_ge if j < i else ALU.is_gt
                        if first:
                            link(TT(rank[:, :, i], sl[:, :, j], sl[:, :, i], op))
                            first = False
                        else:
                            link(TT(t0, sl[:, :, j], sl[:, :, i], op))
                            link(TT(rank[:, :, i], rank[:, :, i], t0, ALU.add))
                link(TS(w0_, w0_, 1.5, None, ALU.is_lt))
                link(TT(rank, rank, gs_[:, 0:NGT].unsqueeze(2).broadcast_to([P, NGT, EPG]), ALU.mult))
                link(TT(w0_, w0_, sc_, ALU.mult))
                link(nc.vector.reduce_sum(w2_[:, 0:NCH], w0_.rearrange("p (c e) -> p c e", e=NE), AX.X))
                link(nc.vector.reciprocal(w2_[:, 0:NCH], w2_[:, 0:NCH]))
                TT(ch_.rearrange("p (c e) -> p c e", e=NE), w0_.rearrange("p (c e) -> p c e", e=NE),
                   w2_[:, 0:NCH].unsqueeze(2).broadcast_to([P, NCH, NE]), ALU.mult).then_inc(S["comb_ready"], 1)
                n = T[f"combT{l}"]
                ps = full(dve, n)
                free(nc.vector.tensor_copy(combT[0:NE, :], ps[0:NE, 0:NT]), n)
                for e in range(NE):
                    n = T[f"ex{l}_{e}"]
                    for j in range(2):
                        read_out(dve, n + 1 + 2 * j)
                        ps = full(dve, n + 2 + 2 * j)
                        hid = HID[:, 2 * e + j, :]
                        free(TT(hid, SG[j], ps[:, 0:NT], ALU.mult), n + 2 + 2 * j)
                        if j == 0:
                            read_out(dve, n)
                        read_out(dve, n + 2 + 2 * j)
                        TT(hid, hid, CB[e % 2], ALU.mult).then_inc(S["hid_done"], 1)
                    if l == 0:
                        for q, i in enumerate(mods_of_expert(e)):
                            mod_evac(T[f"mod1_{e}"] + q, 1, i)
                residual(f"w2_{l}", l, 40)

            ps = full(dve, T["vecT"])
            free(nc.vector.tensor_copy(VT[:, :], ps[:, 0:3 * P]), T["vecT"])
            read_out(dve, T["vecT"])
            raw = vcol("hgrn_lb", 0, 16).rearrange("p (d n c) -> p d n c", d=2, n=2)
            l4 = lbt.rearrange("p (d n c) -> p d n c", d=2, n=2)
            m2 = lut[:, 0:8].rearrange("p (d c) -> p d c", d=2)
            link(TT(m2, raw[:, :, 0, :], raw[:, :, 1, :], ALU.max))
            for q in range(2):
                TT(l4[:, :, q, :], raw[:, :, q, :], m2, ALU.subtract)
            lam = vcol("rg_lambda", 0, 8)
            link(TS(lut[:, 8:16], lam, -1.0, None, ALU.mult))
            link(TS(lut[:, 8:16], lut[:, 8:16], 0.0, None, ALU.max))
            link(TS(lut[:, 16:24], lam, -1.0, None, ALU.mult))
            TT(splam, lam, lut[:, 16:24], ALU.max).then_inc(S["lb_diff"], 1)
            dve.wait_ge(S["consts_l0"], 16)
            for k in range(KT):
                n = T["xT"] + k
                ps = full(dve, n)
                nc.vector.tensor_copy(X[:, k, 0:CTX], ps[:, 0:CTX])
                rows = LAT // GRID_W
                if k < KT // 2:
                    pos = pos_r[:, k * rows:(k + 1) * rows].unsqueeze(2).broadcast_to([P, rows, GRID_W])
                else:
                    q = k - KT // 2
                    pos = pos_c[:, q * GRID_W:(q + 1) * GRID_W].unsqueeze(1).broadcast_to([P, rows, GRID_W])
                free(TT(X[:, k, CTX:NT].rearrange("p (r c) -> p r c", c=GRID_W),
                        ps[:, CTX:NT].rearrange("p (r c) -> p r c", c=GRID_W), pos, ALU.add), n)
            for i in range(8):
                mod_evac(T["mod0a"] + i, 0, i)
            read_out(dve, T["mod0a"] + 7)
            make_coef(0, 0, 8, vcol("norm_mix_g", 0, KT))
            dve.wait_ge(S["lb_exp"], 1)
            m3 = lut[:, 0:8].rearrange("p (d c) -> p d c", d=2)
            link(TT(m3, l4[:, :, 0, :], l4[:, :, 1, :], ALU.add))
            link(nc.vector.reciprocal(lut[:, 0:8], lut[:, 0:8]))
            TT(lb.rearrange("p (d c) -> p d c", d=2), l4[:, :, 0, :], m3, ALU.mult)
            TT(omlb.rearrange("p (d c) -> p d c", d=2), l4[:, :, 1, :], m3, ALU.mult)
            zz, z2, acc = lut[:, 16:24], lut[:, 24:32], lut[:, 32:40]
            link(TS(zz, splam, 2.0, None, ALU.add))
            link(nc.vector.reciprocal(zz, zz))
            link(TT(zz, zz, splam, ALU.mult))
            link(TT(z2, zz, zz, ALU.mult))
            link(TS(acc, z2, 1.0 / 17, 1.0 / 15, ALU.mult, ALU.add))
            for q in (13, 11, 9, 7, 5, 3, 1):
                link(TT(acc, acc, z2, ALU.mult))
                link(TS(acc, acc, 1.0 / q, None, ALU.add))
            link(TT(acc, acc, zz, ALU.mult))
            link(STT(splam, acc, 2.0, lut[:, 8:16], ALU.mult, ALU.add))
            TS(nsp8, splam, -LRU_C, None, ALU.mult)
            TS(psp8, splam, LRU_C, None, ALU.mult)
            TS(nw0, vcol("rw_w0", 0, 16), -1.0, None, ALU.mult)
            TS(na0, vcol("rw_a0", 0, 16), -1.0, None, ALU.mult)
            nc.vector.memset(half_one, 1.0)
            TS(omka, vcol("rw_ka", 0, 8), -1.0, 1.0, ALU.mult, ALU.add).then_inc(S["lb_done"], 1)
            norm_apply(0)
            for j in range(4):
                n = T["xr"] + j
                dve.wait_ge(S["conv_base"], j + 1)
                ps = tile(n)
                for tap, off in ((0, -2), (1, -1), (3, 1)):
                    w = vcol("rg_conv_w", tap * NTA + j)
                    for a, b in SEGS:
                        lo, hi = max(a, a - off), min(b, b - off)
                        ins = STT(XC[:, j, lo:hi], ps[:, lo + off:hi + off], w, XC[:, j, lo:hi], ALU.mult, ALU.add)
                    if tap == 3:
                        free(ins, n)
                    else:
                        link(ins)
            read_out(dve, T["xr"] + 3)

            def lru_unit(u):
                c, d = u // 2, u % 2
                dve.wait_ge(S["lru_th"], u + 1)
                if c == 0 and d == 0:
                    read_out(dve, T["yr"] + 3)
                link(TS(lr, lth, 1.0, None, ALU.add))
                link(nc.vector.reciprocal(lr, lr))
                TT(lth, lth, lr, ALU.mult).then_inc(S["lru_q"], 1)
                link(TT(li, li, XC[:, c, :], ALU.mult))
                dve.wait_ge(S["lru_root"], u + 1)
                link(TT(lth, lth, li, ALU.mult))
                dst = lh if d == 0 else lr
                for s, (a, b) in enumerate(SEGS):
                    init = 0.0 if s == 0 else vcol("state_rglru", 4 * d + c)
                    if d == 0:
                        o_, a_, b_ = dst[:, a:b], la[:, a:b], lth[:, a:b]
                    else:
                        r = slice(b - 1, a - 1 if a else None, -1)
                        o_, a_, b_ = dst[:, r], la[:, r], lth[:, r]
                    link(nc.vector.tensor_tensor_scan(o_, a_, b_, init, ALU.mult, ALU.add))
                e0 = CTX - 1 if d == 0 else 0
                ins = nc.vector.tensor_copy(lru_fin[:, 4 * d + c:4 * d + c + 1], dst[:, e0:e0 + 1])
                if d == 1:
                    link(TT(lh, lh, lr, ALU.add))
                    ins = TT(YG[:, c, :], YG[:, c, :], lh, ALU.mult)
                ins.then_inc(S["lru_done"], 1)

            for u in range(8):
                lru_unit(u)
                if u % 2 == 1:
                    for q in range(4):
                        mod_evac(T[f"mod0b{u // 2}"] + q, 0, 8 + 4 * (u // 2) + q)
            read_out(dve, T["mod0b3"] + 3)
            make_coef(1, 0, 32, vcol("norm_ffn_g", 0, KT))
            n = T["lruT"]
            read_out(dve, T["kb"] + 3)
            for d in range(2):
                for j in range(4):
                    TS(K[d][:, j, :], K[d][:, j, :], omlb[:, 4 * d + j:4 * d + j + 1], None, ALU.mult)
            for d in range(2):
                for j in range(4):
                    dve.wait_ge(S["f_log"], 4 * d + j + 1)
                    m = scanm[d]
                    v = B[d][:, j, :]
                    if d == 0:
                        ins = nc.vector.tensor_tensor_scan(v, m, v, 0.0, ALU.mult, ALU.add)
                    else:
                        ins = nc.vector.tensor_tensor_scan(v[:, ::-1], m[:, ::-1], v[:, ::-1], 0.0, ALU.mult, ALU.add)
            link(ins)
            ps = full(dve, n)
            free(nc.vector.tensor_copy(LROWS[0:8, 0:P], ps[0:8, 0:P]), n)

            def level_views(ap, s):
                return ap.rearrange("p (n w s) -> p n w s", w=2, s=s)

            def level_diff(h, lv):
                i = h * LEVELS + lv
                s = 1 << lv
                nb = NT // (2 * s)
                if i >= 2:
                    hp, lp = divmod(i - 2, LEVELS)
                    dve.wait_ge(psum_full, T[f"lvl{hp}"] + lp + 1)
                f, b = level_views(B[0][:, h, :], s), level_views(B[1][:, h, :], s)
                fm = f[:, :, 0, s - 1:s].broadcast_to([P, nb, s])
                bm = b[:, :, 1, 0:1].broadcast_to([P, nb, s])
                eq, ek = level_views(EQ[i % 2], s), level_views(EK[i % 2], s)
                TT(eq[:, :, 0, :], b[:, :, 0, :], bm, ALU.subtract)
                TT(eq[:, :, 1, :], f[:, :, 1, :], fm, ALU.subtract)
                TT(ek[:, :, 0, :], fm, f[:, :, 0, :], ALU.subtract)
                TT(ek[:, :, 1, :], bm, b[:, :, 1, :], ALU.subtract).then_inc(S["lvl_diff"], 1)

            att3 = ATT.rearrange("p (c t) -> p c t", t=P)

            def level_take(h, lv):
                n = T[f"lvl{h}"] + lv
                if lv:
                    read_out(dve, n - 1)
                ps = full(dve, n)
                m = (lmask[lv] if lv < LEVELS else ident).bitcast(i32)
                m = m.unsqueeze(1).broadcast_to([P, NCH, P])
                free(nc.vector.copy_predicated(att3, m, ps[:, 0:NT].rearrange("p (c t) -> p c t", t=P)), n)

            read_out(dve, T["og"] + 3)
            for h in range(NH_A):
                if h:
                    dve.wait_ge(psum_full, T[f"o{h - 1}"] + 1)
                for d in range(2):
                    b3 = B[d][:, h, :].rearrange("p (c t) -> p c t", t=P)
                    e0 = P - 1 if d == 0 else 0
                    end = b3[:, :, e0:e0 + 1].broadcast_to([P, NCH, P])
                    ins = TT(KH[d].rearrange("p (c t) -> p c t", t=P), end, b3, ALU.subtract)
                ins.then_inc(S["head_diff"], 1)
                level_diff(h, 0)
                TT(KSUM, K[0][:, h, :], K[1][:, h, :], ALU.add)
                dve.wait_ge(S["head_exp"], h + 1)
                for d in range(2):
                    TT(KH[d], KH[d], K[d][:, h, :], ALU.mult)
                    ins = TT(QIN[d][:, CTX:NT], QIN[d][:, CTX:NT], Q[:, h, CTX:NT], ALU.mult)
                ins.then_inc(S["head_ready"], 1)
                for lv in range(LEVELS):
                    i = h * LEVELS + lv
                    if lv + 1 < LEVELS:
                        level_diff(h, lv + 1)
                    dve.wait_ge(S["lvl_exp"], 2 * i + 1)
                    TT(EQ[i % 2], EQ[i % 2], Q[:, h, :], ALU.mult).then_inc(S["lvl_q"], 1)
                    if lv:
                        level_take(h, lv - 1)
                level_take(h, LEVELS - 1)
                level_take(h, LEVELS)
                if h:
                    dve.wait_ge(S["s_final_sent"], 32 * h)
                for d in range(2):
                    n = T[f"U{h}"] + d
                    ps = full(dve, n)
                    nc.vector.tensor_copy(SFIN[d], ps[:, 0:P]).then_inc(S["s_final"], 1)
                    order = range(1, NCH - 1) if d == 0 else range(NCH - 1, 1, -1)
                    for c in order:
                        nxt_c = c + 1 if d == 0 else c - 1
                        ins = STT(hgrn_state(d, nxt_c, h), hgrn_state(d, c, h), gend[:, NCH * d + c:NCH * d + c + 1],
                                  ps[:, c * P:(c + 1) * P], ALU.mult, ALU.add)
                        if c == order[-1]:
                            free(ins, n)
                        else:
                            link(ins)
                n = T[f"on{h}"]
                dve.wait_ge(S["on_root"], h + 1)
                ps = tile(n)
                link(nc.vector.reciprocal(ps[:, 0:NT], ps[:, 0:NT]))
                free(STT(OCP, OCP, vcol("hgrn_norm_g", 0), ps[:, 0:NT], ALU.mult, ALU.mult), n)
                read_out(dve, n)
                TT(OG[:, h, :], OG[:, h, :], OCP, ALU.mult).then_inc(S["o_a_ready"], 1)
            residual("wout", 0, 16)
            norm_apply(1)
            moe(0)
            read_out(dve, T["mod1_15"])
            make_coef(2, 1, 8, vcol("norm_mix_g", KT, KT))
            make_coef(3, 1, 32, vcol("norm_ffn_g", KT, KT))
            norm_apply(2)
            dve.wait_ge(S["h_affine"], 3 * 2 * KT)
            for a, b in SEGS:
                TT(XX[:, :, a + 1:b - 1], H[:, :, a:b - 2], H[:, :, a + 2:b], ALU.add)
                nc.vector.tensor_copy(XX[:, :, a:a + 1], H[:, :, a + 1:a + 2])
                ins = nc.vector.tensor_copy(XX[:, :, b - 1:b], H[:, :, b - 2:b - 1])
            link(ins)
            link(STT(XXf, XXf, 0.5, Hf[:, :], ALU.mult, ALU.subtract))
            dve.wait_ge(S["x_parked"], 16)
            after = [None, T["lora"], T["lora"] + 1, T["lora"] + 2, T["r"] + KT - 1, T["k"] + KT - 1]
            for q, mi in enumerate((1, 4, 5, 0, 2, 3)):
                if after[q] is not None:
                    dve.wait_ge(psum_full, after[q] + 1)
                for k in range(KT):
                    STT(XI[:, k, :], XX[:, k, :], vcol("rw_mu", mi * KT + k), H[:, k, :], ALU.mult,
                        ALU.add).then_inc(S["xi_ready"], 1)
            for d in range(2):
                n = T["stT"] + d
                ps = full(dve, n)
                free(nc.vector.tensor_copy(ST[:, KT * d:KT * (d + 1), :],
                                           ps[:, 0:KT * HD].rearrange("p (j v) -> p j v", v=HD)), n)
            read_out(dve, T["stT"] + 1)
            dve.wait_ge(S["rw_clear"], 6)

            def c3(a):
                return a.rearrange("p (j t) -> p j t", t=P)

            def h3(a):
                return a.rearrange("p (h c) -> p h c", c=P)

            def clamp_gates(g, st, d):
                z, uid = STR[d], unit_id(g, st, d)
                n = T[f"P_{g}_{st}"] + d
                dve.wait_ge(S["gates_exp"], uid + 1)
                free(TS(z["SQ"], tile(n)[:, 2 * UW:3 * UW], 1e-24, 65536.0, ALU.max, ALU.mult), n)
                read_out(dve, n)
                TS(z["LA"], z["LA"], 2.0 ** 62, None, ALU.min).then_inc(S["gates_clamped"], 1)

            def sum_decays(g, st, d):
                z, uid = STR[d], unit_id(g, st, d)
                h0 = 4 * ((g * NCH + st) % 2) + 2 * d
                dve.wait_ge(S["gates_done"], uid + 1)
                one = half_one[:, 0:1].broadcast_to([P, P])
                for j in range(UC):
                    js = slice(j * P, (j + 1) * P) if d == 0 else slice((j + 1) * P - 1, j * P - 1 if j else None, -1)
                    ins = nc.vector.tensor_tensor_scan(z["B"][:, js], one, z["LA"][:, js], 0.0, ALU.mult, ALU.add)
                link(ins)
                e0 = P - 1 if d == 0 else 0
                link(TS(hb[:, h0:h0 + 2], z["B"][:, e0::P], 0.5, None, ALU.mult))
                b3 = c3(z["B"])
                link(TT(b3, b3, hb[:, h0:h0 + 2].unsqueeze(2).broadcast_to([P, UC, P]), ALU.subtract))
                TT(z["E3"], z["B"], z["LA"][:, 0:UW], ALU.subtract).then_inc(S["decay_sum"], 1)

            def make_operands(g, st, d):
                z, ch, uid = STR[d], chunk_of(st, d), unit_id(g, st, d)
                ts, cg = slice(ch * P, (ch + 1) * P), slice(UC * g, UC * (g + 1))
                aa = z["LA"][:, UW:2 * UW]
                for j in range(UC):
                    ct = UC * g + j
                    js = slice(j * P, (j + 1) * P)
                    TS(z["KP"][:, js], aa[:, js], vcol("rw_ka", ct), omka[:, ct:ct + 1], ALU.mult, ALU.add)
                link(STT(z["KK"], z["KK"], 256.0, z["SQ"], ALU.mult, ALU.mult))
                TT(z["BE"], z["KK"], aa, ALU.mult)
                dve.wait_ge(S["decay_exp"], uid + 1)
                link(TT(c3(z["KD"]), K1[:, cg, ts], c3(z["KP"]), ALU.mult))
                for j in range(UC):
                    ct = UC * g + j
                    js = slice(j * P, (j + 1) * P)
                    STT(z["SQ"][:, js], R1[:, ct, ts], vcol("rw_rk", ct), z["KD"][:, js], ALU.mult, ALU.mult)
                TT(z["KP"], z["KD"], z["E2"], ALU.mult)
                TT(z["BE"], z["BE"], z["E2"], ALU.mult)
                r5 = z[f"RHS4_{(g * NCH + st) % 2}"].rearrange("p (j h a t) -> p j h a t", j=UC, h=2, a=2)
                for hh in range(2):
                    pr = slice(HD * hh, HD * hh + HD)
                    TT(r5[pr, :, hh, 0, :], c3(z["KK"])[pr], c3(z["E3"])[pr], ALU.mult)
                    ins = TT(r5[pr, :, hh, 1, :], R1[pr, cg, ts], c3(z["E1"])[pr], ALU.mult)
                ins.then_inc(S["unit_ready"], 1)

            for stage in (clamp_gates, sum_decays, make_operands):
                for d in range(2):
                    stage(0, 0, d)
            idb = ident.unsqueeze(1).broadcast_to([P, HG, P])
            for g in range(NGRP):
                for st in range(NCH):
                    u = f"_{g}_{st}"
                    nx = None if (g, st) == (NGRP - 1, NCH - 1) else next_step(g, st)
                    par = 4 * ((g * NCH + st) % 2)
                    for d in range(2):
                        z, uid = STR[d], unit_id(g, st, d)
                        n = T["AR" + u] + d
                        ps = full(dve, n)
                        m = CO[:, C_RMASK + 256 * d:C_RMASK + 256 * d + 256].unsqueeze(1).broadcast_to([P, HG, 256])
                        free(TT(z["AR"].rearrange("p (h c) -> p h c", c=256),
                                ps.rearrange("p (h c) -> p h c", c=256), m, ALU.mult), n)
                        read_out(dve, n)
                        at = z["AR"].rearrange("p (h c) -> p h c", c=256)[:, :, 0:P]
                        g0 = CO[:, C_GMASK + (1 - d) * P:C_GMASK + (2 - d) * P].unsqueeze(1).broadcast_to([P, HG, P])
                        link(TT(h3(z["N"]), at, g0, ALU.mult))
                        TT(h3(z["N"]), idb, h3(z["N"]), ALU.subtract).then_inc(S["mn_ready"], 1)
                    for d in range(2):
                        z = STR[d]
                        n = T["BR" + u] + d
                        ps = full(dve, n)
                        m = CO[:, C_RMASK + 256 * d:C_RMASK + 256 * d + 256].unsqueeze(1).broadcast_to([P, HG, 256])
                        free(TT(z["BR"].rearrange("p (h c) -> p h c", c=256),
                                ps.rearrange("p (h c) -> p h c", c=256), m, ALU.mult), n)
                    for d in range(2):
                        ch, uid = chunk_of(st, d), unit_id(g, st, d)
                        n = T["AN" + u] + d
                        dve.wait_ge(S["kb_t"], uid + 1)
                        if d:
                            read_out(dve, n - 1)
                        bo = BON[:, ch, HG * g:HG * (g + 1)]
                        free(TT(bo, bo, tile(n)[:, 0:HG], ALU.add), n)
                    if st:
                        for d in range(2):
                            TT(STR[d]["R0"].rearrange("p (j v) -> p j v", v=HD),
                               ST[:, KT * d + UC * g:KT * d + UC * (g + 1), :],
                               em[:, par + 2 * d:par + 2 * d + 2].unsqueeze(2).broadcast_to([P, UC, HD]),
                               ALU.mult).then_inc(S["r0_ready"], 1)
                    for lv in range(1, LEVELS):
                        s = 1 << lv
                        for d in range(2):
                            z = STR[d]
                            n = T[f"G{lv}" + u] + d
                            ps = full(dve, n)
                            o = C_GMASK + 2 * P + (d * (LEVELS - 1) + lv - 1) * HD
                            gm = CO[:, o:o + HD].unsqueeze(1).broadcast_to([P, HG, HD])
                            free(TT(z["G"].rearrange("p (h c) -> p h c", c=HD),
                                    ps[:, 0:HG * HD].rearrange("p (h c) -> p h c", c=HD), gm, ALU.mult), n)
                        if nx and lv == 2:
                            clamp_gates(*nx, 0)
                            clamp_gates(*nx, 1)
                        for d in range(2):
                            z = STR[d]
                            n = T[f"D{lv}" + u] + d
                            ps = full(dve, n)
                            mv = z["M"].rearrange("p (n w s) -> p n w s", w=2, s=s)[:, :, d, :]
                            free(TT(mv, mv, ps[:, 0:HG * HD].rearrange("p (n s) -> p n s", s=s), ALU.subtract), n)
                        if nx:
                            if lv == 3:
                                sum_decays(*nx, 0)
                            elif lv == 4:
                                sum_decays(*nx, 1)
                            elif lv == 5:
                                make_operands(*nx, 0)
                            elif lv == 6:
                                make_operands(*nx, 1)
                    for d in range(2):
                        z, ch = STR[d], chunk_of(st, d)
                        n = T["OT" + u] + d
                        ps = full(dve, n)
                        tt = ps[:, 512:512 + UC * P].rearrange("p (j c) -> p j c", c=P)
                        r0 = z["R0"].rearrange("p (j v) -> p j v", v=HD)
                        eb = em[:, par + 2 * d:par + 2 * d + 2]
                        if st:
                            for hh in range(2):
                                pr = slice(HD * hh, HD * hh + HD)
                                ins = TT(r0[pr], r0[pr], tt[pr, :, HD * hh:HD * hh + HD], ALU.add)
                            link(ins)
                            link(TT(ST[:, KT * d + UC * g:KT * d + UC * (g + 1), :], r0,
                                    eb.unsqueeze(2).broadcast_to([P, UC, HD]), ALU.mult))
                        else:
                            sf = z["SF"].rearrange("p (j v) -> p j v", v=HD)
                            for hh in range(2):
                                pr = slice(HD * hh, HD * hh + HD)
                                e2 = eb[pr].unsqueeze(2).broadcast_to([HD, UC, HD])
                                ins = TT(sf[pr], tt[pr, :, HD * hh:HD * hh + HD], e2, ALU.mult)
                            ins.then_inc(S["ctx_state"], 1)
                        o = OT[:, ch, HG * HD * g:HG * HD * (g + 1)]
                        if st == 0 and d:
                            read_out(dve, n - 1)
                        free(TT(o, o, ps[:, 0:HG * HD], ALU.add), n)
                    if st == 0:
                        n = T["fin" + u]
                        ps = full(dve, n)
                        free(nc.vector.tensor_copy(FINB[0:HD, :], ps[0:HD, 0:4 * P]), n)
            read_out(dve, T[f"OT_{NGRP - 1}_{NCH - 1}"] + 1)
            nc.vector.memset(lut[:, 2:3], 0.0).then_inc(S["scan_done"], 1)
            for c in range(NCH):
                cs = slice(16 * c, 16 * c + 16)
                o3 = OT[:, c, :].rearrange("p (h v) -> p h v", v=HD)
                mu, var = GNS[0][:, cs], GNS[1][:, cs]
                bc = lambda a: a.unsqueeze(2).broadcast_to([P, 16, HD])
                link(nc.vector.reduce_sum(mu, o3, AX.X))
                link(TS(mu, mu, 1.0 / HD, None, ALU.mult))
                TT(o3, o3, bc(mu), ALU.subtract).then_inc(S["gn_centred"], 1)
                dve.wait_ge(S["gn_sq"], c + 1)
                nc.vector.reduce_sum(var, Z2[:, c, :].rearrange("p (h v) -> p h v", v=HD), AX.X).then_inc(S["gn_var"], 1)
                dve.wait_ge(S["gn_root"], c + 1)
                link(nc.vector.reciprocal(var, var))
                TT(o3, o3, bc(var), ALU.mult)
                TT(Z2[:, c, :].rearrange("p (h v) -> p h v", v=HD), V1[:, c, :].rearrange("p (h v) -> p h v", v=HD),
                   bc(BON[:, c, :]), ALU.mult).then_inc(S["z_ready"], 1)
            for k in range(KT):
                n = T[f"post{k}"]
                read_out(dve, n)
                ps = full(dve, n + 1)
                free(TT(OC[:, k, :], OC[:, k, :], ps[:, 0:NT], ALU.add), n + 1)
                ps = full(dve, n + 2)
                read_out(dve, n + 1)
                free(TT(OC[:, k, :], OC[:, k, :], ps[:, 0:NT], ALU.mult), n + 2)
            dve.wait_ge(S["x_back"], 16)
            residual("wo", 1, 16)
            norm_apply(3)
            moe(1)
            norm_apply(4)
            for c in range(NCH):
                n = T["yT"] + c
                ps = full(dve, n)
                free(nc.vector.tensor_copy(YT[:, c, :], ps), n)


_NAMES = ["x_prompt", "x_sample", "state_hgrn", "state_rglru", "state_rwkv", "c", "c_ctx", "norm_mix_g", "norm_ffn_g",
          "w_mod", "b_mod", "ab_w_in", "ab_w_out", "hgrn_lb", "hgrn_norm_g", "rg_conv_w", "rg_conv_b", "rg_wa", "rg_ba",
          "rg_wx", "rg_bx", "rg_lambda", "rw_mu", "rw_wr", "rw_wk", "rw_wv", "rw_wo", "rw_w0", "rw_w1", "rw_w2",
          "rw_a0", "rw_a1", "rw_a2", "rw_g1", "rw_g2", "rw_kk", "rw_ka", "rw_rk", "rw_lnw", "rw_lnb", "moe_router",
          "moe_router_bias", "moe_w1", "moe_w3", "moe_w2", "norm_f_g"]
_OUTS = [("y_prompt", (1, CTX, D)), ("y_sample", (1, LAT, D)), ("hgrn", (1, 1, 2, NH_A, P, P)),
         ("rglru", (1, 1, 2, DA)), ("rwkv", (1, 1, 2, 16, HD, HD))]


def shape_constants(np):
    c = np.zeros((P, C_ALL), np.float32)
    i, j = np.arange(P)[:, None], np.arange(P)[None, :]
    c[:, C_IDENT:C_IDENT + P] = i == j
    c[:, C_ONES:C_ONES + P] = 1.0
    c[:, C_BONES:C_BONES + P] = i // HD == j // HD
    c[:, C_HSEL:C_HSEL + 2] = np.arange(2)[None, :] == i // HD
    c[:, C_EPS] = EPS_RMS
    c[:, C_EPS + 1] = EPS_GN
    for d in range(2):
        o = C_RMASK + 256 * d
        c[:, o:o + P] = (i < j) if d == 0 else (i > j)
        c[:, o + P:o + 2 * P] = (i <= j) if d == 0 else (i >= j)
    for lv in range(LEVELS):
        s = 1 << lv
        g = (i // (2 * s) == j // (2 * s)) & ((i // s) % 2 == 1) & ((j // s) % 2 == 0)
        for d, gd in enumerate((g, g.T)):
            if lv == 0:
                c[:, C_GMASK + d * P:C_GMASK + (d + 1) * P] = gd
            else:
                o = C_GMASK + 2 * P + (d * (LEVELS - 1) + lv - 1) * HD
                c[:, o:o + HD] = gd[:, (np.arange(P) // s) % 2 == d]
        c[:, C_LMASK + lv * P:C_LMASK + (lv + 1) * P] = g | g.T
    t = np.arange(NT)
    c[:, C_SCAN:C_SCAN + NT] = t % P != 0
    c[:, C_SCAN + NT:C_SCAN + 2 * NT] = t % P != P - 1
    quarter = D // 4
    omega = (1.0 / (np.float32(10000.0) ** (np.arange(quarter, dtype=np.float32) / np.float32(quarter)))).astype(np.float32)
    for n, o in ((LAT // GRID_W, C_POS), (GRID_W, C_POS + 4 * (LAT // GRID_W))):
        ang = (np.arange(n, dtype=np.float32)[:, None] * omega).astype(np.float32)
        tab = np.concatenate([np.sin(ang), np.cos(ang)], axis=1).astype(np.float32)
        c[:, o:o + 4 * n] = tab.T.reshape(4, P, n).transpose(1, 0, 2).reshape(P, 4 * n)
    return c


def kernel(**inputs):
    import numpy as _np
    import concourse.bacc as _bacc
    from concourse import mybir as _mybir
    from concourse.bass_utils import run_bass_kernel_spmd as _run

    nc = _bacc.Bacc("TRN2", target_bir_lowering=False, num_devices=1)
    f32 = _mybir.dt.float32
    arrays, aps = {}, {}
    for name in _NAMES:
        a = _np.ascontiguousarray(inputs[name])
        arrays[f"in_{name}"] = a
        aps[name] = nc.dram_tensor(f"in_{name}", a.shape, _mybir.dt.from_np(a.dtype), kind="ExternalInput").ap()
    arrays["in_const"] = shape_constants(_np)
    const = nc.dram_tensor("in_const", (P, C_ALL), f32, kind="ExternalInput").ap()
    outs = {name: nc.dram_tensor(f"out_{name}", shape, f32, kind="ExternalOutput").ap() for name, shape in _OUTS}
    xspill = nc.dram_tensor("parked_residual", (P, KT * NT), f32).ap()
    build(nc, aps, const, outs, xspill)
    r = _run(nc, [arrays], core_ids=[0])
    return tuple(r.results[0][f"out_{name}"] for name, _ in _OUTS)
```

```python
import concourse.bass as bass
from concourse import mybir
from contextlib import ExitStack

P = 128
D = 1024
KT = D // P
CTX = 128
LAT = 512
NT = CTX + LAT
NCH = NT // P
SEGS = ((0, CTX), (CTX, NT))
GRID_W = 64
DA = D // 2
NH_A = DA // P
NTA = DA // P
LEVELS = 7
HD = 64
EPS_RMS = 1e-6
EPS_GN = 64e-5
W_DECAY = 0.6065306597126334
LRU_C = 8.0
NE = 16
NG = 4
EPG = NE // NG
DE = 256
SLOT = 2048
RING_W = 3
RING_P = 4
TW = 1024
HG = 4
NGRP = 16 // HG
UC = HG // 2
UW = UC * P
N_OVER = (2 * NT - NE) // P
N_SLOTS = (NE + N_OVER) * P
RING_M = 9

C_IDENT, C_ONES, C_BONES, C_HSEL, C_EPS = 0, 128, 256, 384, 386
C_E128 = 388
C_XIDX = C_E128 + NE
C_RMASK = C_XIDX + 12
C_GMASK = C_RMASK + 4 * P
C_PERSIST = C_GMASK + 2 * P + 2 * (LEVELS - 1) * HD
C_LMASK = C_PERSIST
C_SCAN = C_LMASK + LEVELS * P
C_POS = C_SCAN + 2 * NT
C_ALL = C_POS + 4 * (LAT // GRID_W) + 4 * GRID_W

VECS = [("b_mod", 96), ("hgrn_lb", 16), ("hgrn_norm_g", 1), ("c", 8),
        ("rw_mu", 48), ("rg_conv_w", 16), ("rg_conv_b", 4), ("rg_ba", 8), ("rg_bx", 8), ("rg_lambda", 8),
        ("norm_f_g", 8), ("c_ctx", 8), ("state_rglru", 8),
        ("norm_mix_g", 16), ("norm_ffn_g", 16), ("rw_w0", 16), ("rw_a0", 16), ("rw_kk", 8), ("rw_ka", 8),
        ("rw_rk", 8), ("rw_lnw", 8), ("rw_lnb", 8)]


def vec_places():
    at, place = 0, {}
    for name, rows in VECS:
        if at // P != (at + rows - 1) // P:
            at = (at // P + 1) * P
        place[name] = at
        at += rows
    assert at <= 3 * P
    return place


def next_step(g, st):
    return (g, st + 1) if st + 1 < NCH else (g + 1, 0)


def expert_tiles(l):
    names = []
    for e in range(NE):
        if e + 1 < NE:
            names += [(f"XT{l}_{e + 1}", 1)]
        names += [(f"H13{l}_{e}", 1)]
        if e:
            names += [(f"HT{l}_{e - 1}", 1), (f"Y{l}_{e - 1}", 1)]
        if l == 0:
            names += [(f"mod1_{e}", 1)] + ([(f"mod1_T{e // 4}", 1)] if e % 4 == 3 else [])
    return names + [(f"HT{l}_{NE - 1}", 1), (f"Y{l}_{NE - 1}", 1)]


def tile_plan():
    names = [("vecT", 1)]
    names += [("xT", KT), ("mod0a0", 5), ("mod0a1", 5), ("norm0", 1), ("xr", 4), ("yr", 4)]
    for u in range(8):
        names += [(f"gate{u}", 2), (f"qk{u}", 1)]
        if u % 2 == 1:
            names += [(f"mod0b{u // 2}", 5)]
    names += [("kb", 4), ("v", NCH), ("og", 4), ("lruT", 1)]
    for h in range(NH_A):
        names += [(f"lvl{h}", LEVELS + 1), (f"khT{h}", 2), (f"U{h}", 2), (f"o{h}", 1), (f"on{h}", 1)]
    names += [("wout", KT), ("norm1", 1), ("router0", 1), ("htok0", NCH),
              ("mod1_a", 5), ("rank0", 1), ("mod1_b", 5), ("XT0_0", 1)]
    names += expert_tiles(0)
    names += [("w2_0", KT), ("norm2", 1), ("lora", 3), ("r", KT), ("k", KT), ("V", 2 * NCH), ("stT", 2)]
    for g in range(NGRP):
        for st in range(NCH):
            u = f"_{g}_{st}"
            if (g, st) == (0, 0):
                names += [("P" + u, 2)]
            names += [("AR" + u, 2), ("BR" + u, 2), ("AN" + u, 2), ("M0" + u, 2)]
            for lv in range(1, LEVELS):
                names += [(f"G{lv}" + u, 2)]
                if lv == 2 and (g, st) != (NGRP - 1, NCH - 1):
                    gn, sn = next_step(g, st)
                    names += [(f"P_{gn}_{sn}", 2)]
                names += [(f"D{lv}" + u, 2)]
            names += [("N6" + u, 2), ("RHS" + u, 2), ("Us" + u, 2), ("OT" + u, 2)]
            if st == 0:
                names += [("fin" + u, 1)]
    for k in range(KT):
        names += [(f"post{k}", 3)]
    names += [("wo", KT), ("norm3", 1), ("router1", 1), ("htok1", NCH), ("rank1", 1), ("XT1_0", 1)]
    names += expert_tiles(1)
    names += [("w2_1", KT), ("norm4", 1), ("yT", NCH)]
    base, at = {}, 0
    for name, n in names:
        base[name] = at
        at += n
    return base


def build(nc, A, const, outs, xspill, slots_in, slots_out):
    f32 = mybir.dt.float32
    i32 = mybir.dt.int32
    u32 = mybir.dt.uint32
    ALU = mybir.AluOpType
    ACT = mybir.ActivationFunctionType
    AX = mybir.AxisListType
    T = tile_plan()
    VB = vec_places()
    ctx = ExitStack()
    with ctx:
        def sb(name, n):
            return ctx.enter_context(nc.sbuf_tensor(name, [P, n], f32))

        def sem(name):
            return ctx.enter_context(nc.semaphore(name))

        Xf = sb("x_resid", KT * NT)
        Hf = sb("h_normed", KT * NT)
        Wf = sb("weight_ring", RING_W * SLOT)
        CO = sb("consts", C_PERSIST)
        VT = sb("vectors", 3 * P)
        MODf = sb("modulation", 2 * 48 * 2)
        SM = sb("small", 432)
        ARENA_N = 53200 - (2 * KT * NT + RING_W * SLOT + C_PERSIST + 3 * P + 192 + 432)
        AR = sb("arena", ARENA_N)
        PSt = ctx.enter_context(nc.psum_tensor("psum_ring", [P, RING_P * TW], f32))

        X = Xf[:, :].rearrange("p (k t) -> p k t", k=KT)
        H = Hf[:, :].rearrange("p (k t) -> p k t", k=KT)
        MOD = MODf[:, :].rearrange("p (l j s) -> p l j s", l=2, j=48)
        ident = CO[:, C_IDENT:C_IDENT + P]
        ones = CO[:, C_ONES:C_ONES + P]
        bones = CO[:, C_BONES:C_BONES + P]
        hsel = CO[:, C_HSEL:C_HSEL + 2]
        eps_rms = CO[:, C_EPS:C_EPS + 1]
        eps_gn = CO[:, C_EPS + 1:C_EPS + 2]

        def vcol(name, i, n=1):
            return VT[:, VB[name] + i:VB[name] + i + n]

        arena_at = [0, 0]

        def carve(n):
            a = arena_at[0]
            arena_at[0] += n
            assert arena_at[0] <= ARENA_N, (arena_at[0], ARENA_N)
            return AR[:, a:a + n]

        sm_at = [0]

        def small(n):
            a = sm_at[0]
            sm_at[0] += n
            assert sm_at[0] <= 432
            return SM[:, a:a + n]

        silu_c = small(16)
        coef = [small(16) for _ in range(4)]
        lb = small(8)
        omlb = small(8)
        lbt = small(16)
        splam = small(8)
        nsp8 = small(8)
        psp8 = small(8)
        lru_fin = small(8)
        nw0 = small(16)
        na0 = small(16)
        omka = small(8)
        gend = small(16)
        half_one = small(4)
        hb = small(8)
        em = small(8)
        rwR = small(KT * NE)
        rbias = small(NE)
        lut = small(48)

        psum_full = sem("psum_full")
        psum_free = [sem(f"psum_free{i}") for i in range(RING_P)]
        w_landed = [sem(f"w_landed{i}") for i in range(RING_W)]
        dve_chain = sem("dve_chain")
        act_chain = sem("act_chain")
        S = {name: sem(name) for name in (
            "consts_in", "consts_l0", "vec_clear", "vec_in", "x_in", "silu_c", "lb_diff", "lb_exp", "lb_done",
            "sq_ready", "coef_ready", "rms_root", "h_scaled", "h_affine",
            "gates_clear", "gates_in", "router_in", "conv_base", "lru_th", "lru_q", "lru_root", "lru_done",
            "lru_sent", "f_log", "head_diff", "head_exp", "head_ready",
            "lvl_diff", "lvl_exp", "lvl_q", "lvl_k", "st_in", "s_final", "s_final_sent", "on_root", "o_a_ready",
            "chosen", "routed", "zero_ready", "zero_filled", "slots_filled", "over_done", "x_parked", "x_back", "xi_ready", "lora_in", "rw_st_in", "rw_clear",
            "kk_sq", "gates_exp", "decay_sum", "decay_exp", "unit_ready", "kb_t", "mn_ready",
            "r0_ready", "n_out", "gates_clamped", "gates_done", "ctx_state", "ctx_state_sent", "scan_done", "gn_centred", "gn_sq", "gn_var", "gn_root",
            "z_ready", "silu_out", "acc_ready", "y_sent")}
        m_landed = [sem(f"m_landed{i}") for i in range(RING_M)]
        xg_landed = [sem(f"xg_landed{i}") for i in range(2)]
        y_stored = [sem(f"y_stored{i}") for i in range(2)]
        gathered = [sem(f"gathered{c}") for c in range(NCH)]
        over = [{name: sem(f"over_{name}{l}") for name in ("in", "pe", "silu", "out_of_psum", "stored",
                                                                 "through")}
                for l in range(2)]

        def full(eng, n):
            eng.wait_ge(psum_full, n + 1)
            return tile(n)

        def tile(n):
            return PSt[:, (n % RING_P) * TW:(n % RING_P + 1) * TW]

        def free(ins, n):
            ins.then_inc(psum_free[n % RING_P], 1)

        def read_out(eng, n):
            eng.wait_ge(psum_free[n % RING_P], n // RING_P + 1)

        stream = []

        def cols(w, c0, n, kt=KT):
            return (lambda s: s[:, 0:kt * n].rearrange("p (k c) -> p k c", c=n),
                    w.rearrange("(k p) c -> p k c", p=P)[:, :, c0:c0 + n])

        def add(key, last_tile, *parts):
            stream.append((key, last_tile, parts))

        def add_mod(layer, i, n):
            add(("mod", layer, i), n, cols(A["w_mod"][layer], 256 * i, 256))

        def add_in(i, n):
            add(("in", i), n, cols(A["ab_w_in"][0], 256 * i, 256))

        for i in range(8):
            add_mod(0, i, T[f"mod0a{i // 4}"] + i % 4)
        for i in range(2):
            add_in(10 + i, T["xr"] + 2 * i + 1)
        for i in range(2):
            add_in(12 + i, T["yr"] + 2 * i + 1)
        for u in range(1, 8, 2):
            add_in(u // 2, T[f"qk{u}"])
            for q in range(4):
                add_mod(0, 8 + 4 * (u // 2) + q, T[f"mod0b{u // 2}"] + q)
        for i in range(2):
            add_in(4 + i, T["kb"] + 2 * i + 1)
        for i in range(2):
            add_in(6 + i, T["v"] + NCH - 1)
        for i in range(2):
            add_in(8 + i, T["og"] + 2 * i + 1)
        for i in range(4):
            add(("ab_w_out", i), T["wout"] + 2 * i + 1, cols(A["ab_w_out"][0], 256 * i, 256))

        def mods_of_expert(e):
            return (8 + e,)

        for i in range(8):
            add_mod(1, i, T["mod1_a"] + i if i < 4 else T["mod1_b"] + i - 4)

        for e in range(NE):
            for q, i in enumerate(mods_of_expert(e)):
                add_mod(1, i, T[f"mod1_{e}"] + q)
        for q, name in enumerate(("rw_w1", "rw_a1")):
            w = A[name][0]
            add((name, 0), T["lora"] + q,
                *[((lambda s, d=d: s[:, 0:KT * P].rearrange("p (k c) -> p k c", c=P)[:, :, HD * d:HD * d + HD]),
                   w[d].rearrange("(k p) c -> p k c", p=P)) for d in range(2)])
        add(("rw_g1", 0), T["lora"] + 2, cols(A["rw_g1"][0], 0, P))
        for name, tn in (("rw_wr", "r"), ("rw_wk", "k")):
            for i in range(4):
                add((name, i), T[tn] + 2 * i + 1, cols(A[name][0], 256 * i, 256))
        for i in range(4):
            add(("rw_wv", i), T["V"] + NCH * (i // 2) + NCH - 1, cols(A["rw_wv"][0], 256 * i, 256))
        add(("rw_g2", 0), T["post7"] + 2, (lambda s: s[:, 0:D], A["rw_g2"][0]))
        for i in range(4):
            add(("rw_wo", i), T["wo"] + 2 * i + 1, cols(A["rw_wo"][0], 256 * i, 256))
        slot_no = {key: i for i, (key, _, _) in enumerate(stream)}
        landed_at, per_slot = [], [0] * RING_W
        for i, (_, _, parts) in enumerate(stream):
            per_slot[i % RING_W] += 16 * len(parts)
            landed_at.append(per_slot[i % RING_W])

        def slot(i):
            return Wf[:, (i % RING_W) * SLOT:(i % RING_W + 1) * SLOT]

        l0c = carve(C_ALL - C_PERSIST)
        lmask = [l0c[:, i * P:(i + 1) * P] for i in range(LEVELS)]
        scanm = [l0c[:, C_SCAN - C_PERSIST + d * NT:C_SCAN - C_PERSIST + (d + 1) * NT] for d in range(2)]
        pos_r = l0c[:, C_POS - C_PERSIST:C_POS - C_PERSIST + 32]
        pos_c = l0c[:, C_POS - C_PERSIST + 32:C_POS - C_PERSIST + 32 + 256]
        nA = NTA * NT
        XCf, YGf, Qf, OGf = carve(nA), carve(nA), carve(nA), carve(nA)
        Kf = [carve(nA), carve(nA)]
        Bf = [carve(nA), carve(nA)]
        VAf = carve(NCH * DA)
        GW = carve(16 * P)
        ZERO = carve(D)
        lr, li, la, lth, lh = [carve(NT) for _ in range(5)]
        t3 = lambda a, k=NTA: a.rearrange("p (k t) -> p k t", k=k)
        XC, YG, Q, OG = t3(XCf), t3(YGf), t3(Qf), t3(OGf)
        K = [t3(a) for a in Kf]
        B = [t3(a) for a in Bf]
        VA = t3(VAf, NCH)
        vrow = XCf[:, 0:3 * P]
        xtok = Hf[:, :].rearrange("p (c d) -> p c d", d=D)
        hs_at = [0]

        def hcarve(n):
            a = hs_at[0]
            hs_at[0] += n
            return Hf[:, a:a + n]

        ATT = hcarve(NT)
        EQ = [hcarve(NT) for _ in range(3)]
        EK = [hcarve(NT) for _ in range(2)] + [lth]
        QIN = [hcarve(NT) for _ in range(2)]
        KHT = [XCf[:, 0:NT], XCf[:, NT:2 * NT]]
        KH = [XCf[:, 2 * NT:3 * NT], XCf[:, 3 * NT:4 * NT]]
        SST = [GW[:, 0:4 * P], GW[:, 4 * P:8 * P]]
        SIN = GW[:, 8 * P:16 * P]
        OCP, OSQ = lr, li
        SFIN = [la[:, 0:P], la[:, P:2 * P]]
        l0_end = arena_at[0]

        MROW = AR[:, ARENA_N - 4 * 256:ARENA_N]
        assert l0_end <= ARENA_N - 4 * 256

        arena_at[0] = 0
        MR = [carve(SLOT) for _ in range(RING_M)]
        HTOK = carve(NCH * D).rearrange("p (c d) -> p c d", d=D)
        XG = [carve(D) for _ in range(2)]
        XGT = [carve(D) for _ in range(2)]
        SH = [carve(DE) for _ in range(2)]
        HM = [carve(DE) for _ in range(2)]
        HMT = [carve(DE) for _ in range(2)]
        YB = [carve(D) for _ in range(2)]
        sc_, sl_, ch_, gs_, w0_, w1_, pos_, se0_, se1_, ge_ = [carve(NCH * NE) for _ in range(10)]
        exo_ = carve(12 * NE)
        nov_, ovi_, adj_, wj_ = carve(NE), carve(NE), carve(NE), carve(4 * NCH)
        posf_ = carve(2 * NCH)
        PI = carve(2 * NCH).bitcast(u32)
        OVI = carve(12).bitcast(i32)
        ovf_ = carve(12)
        assert arena_at[0] <= ARENA_N - 4 * 256, arena_at
        G0 = HTOK
        G1 = AR[:, 0:NCH * D].rearrange("p (c d) -> p c d", d=D)

        arena_at[0] = 0
        Rf, KKf, VVf = carve(KT * NT), carve(KT * NT), carve(NCH * D)
        R1 = Rf.rearrange("p (k t) -> p k t", k=KT)
        K1 = KKf.rearrange("p (k t) -> p k t", k=KT)
        V1 = VVf.rearrange("p (c d) -> p c d", d=D)
        hw, ha, hg = carve(NT), carve(NT), carve(NT)
        W2s, A2s = carve(D), carve(D)
        STf = carve(16 * HD)
        ST = STf.rearrange("p (j v) -> p j v", v=HD)
        BON = carve(NCH * 16).rearrange("p (c h) -> p c h", h=16)
        GNS = carve(2 * NCH * HG)
        mark = arena_at[0]
        XXf = carve(KT * NT)
        XX = XXf.rearrange("p (k t) -> p k t", k=KT)
        XI = [a.rearrange("p (k t) -> p k t", k=KT) for a in (Xf[:, :], carve(KT * NT))]
        arena_at[0] = mark
        OT = Hf[:, :].rearrange("p (c d) -> p c d", d=D)
        STR = []
        xat = [0]

        def stream_carve(n):
            if arena_at[0] + n <= ARENA_N:
                return carve(n)
            a = xat[0]
            xat[0] += n
            assert xat[0] <= KT * NT, (xat, arena_at, ARENA_N)
            return Xf[:, a:a + n]

        for d in range(2):
            z = {}
            for name, n in (("LA", 2 * UW), ("B", UW), ("E1", UW), ("E2", UW), ("E3", UW), ("KK", UW), ("SQ", UW),
                            ("BE", UW), ("KP", UW), ("RHS4_0", 4 * UW), ("RHS4_1", 4 * UW), ("KBT", 2 * UW),
                            ("AR", HG * 256), ("BR", HG * 256), ("M", HG * P), ("N", HG * P), ("G", HG * HD),
                            ("RHU", 2 * HG * HD), ("R0", UC * HD), ("SF", UC * HD)):
                z[name] = stream_carve(n)
            z["RH"], z["U"] = z["RHU"][:, 0:HG * HD], z["RHU"][:, HG * HD:]
            z["KD"] = z["B"]
            STR.append(z)
        NATST = STR[0]["AR"], STR[0]["BR"]
        FINB = STR[1]["RHU"]

        def gn_stats(c):
            a = 2 * HG * c
            return GNS[:, a:a + HG], GNS[:, a + HG:a + 2 * HG]

        OC = R1
        Z2 = [KKf[:, g * UC * NT:(g + 1) * UC * NT].rearrange("p (c d) -> p c d", d=UW) for g in range(NGRP)]
        YT = AR[:, 0:NCH * D].rearrange("p (c d) -> p c d", d=D)
        KSUM, LROWS = lh, la[:, 2 * P:3 * P]

        def unit_id(g, st, d):
            return (g * NCH + st) * 2 + d

        def n_count(g, st, lv, d):
            return 2 * ((g * NCH + st) * (LEVELS - 2) + lv - 2) + d + 1

        def chunk_of(st, d):
            return 0 if st == 0 else (st if d == 0 else NCH - st)

        def hgrn_state(d, c, h):
            if c == (1 if d == 0 else NCH - 1):
                return SIN[:, (d * NH_A + h) * P:(d * NH_A + h + 1) * P]
            return SST[d][:, (c - 1) * P:c * P]

        block = ctx.enter_context(nc.Block())

        @block.sync
        def _(sp):
            sp.dma_start(CO[:, :], const[:, 0:C_PERSIST]).then_inc(S["consts_in"], 16)
            sp.dma_start(l0c, const[:, C_PERSIST:C_ALL]).then_inc(S["consts_l0"], 16)
            sp.dma_start(xtok[:, 0, :], A["x_prompt"][0]).then_inc(S["x_in"], 16)
            sp.dma_start(xtok[:, 1:NCH, :], A["x_sample"][0].rearrange("(c p) d -> p c d", p=P)).then_inc(S["x_in"], 16)
            at = [0]

            def load_until(key):
                while at[0] <= slot_no[key]:
                    i = at[0]
                    if i >= RING_W:
                        sp.wait_ge(psum_full, stream[i - RING_W][1] + 1)
                    for view, src in stream[i][2]:
                        sp.dma_start(view(slot(i)), src).then_inc(w_landed[i % RING_W], 16)
                    at[0] += 1

            def expert_weights(l, e):
                for q, w in enumerate((A["moe_w1"], A["moe_w3"], A["moe_w2"])):
                    i = 3 * e + q
                    if e >= RING_M // 3:
                        old = e - RING_M // 3
                        sp.wait_ge(psum_full, T[f"H13{l}_{old}" if q < 2 else f"Y{l}_{old}"] + 1)
                    n = w.shape[2] // P
                    sp.dma_start(MR[i % RING_M].rearrange("p (k c) -> p k c", k=n),
                                 w[l, e].rearrange("(k p) c -> p k c", p=P)).then_inc(m_landed[i % RING_M], 16)

            def expert_rows(l, e):
                if e == 0:
                    sp.wait_ge(S["slots_filled"], 16 * 2 * NCH * (l + 1))
                if e >= 2:
                    sp.wait_ge(psum_full, T[f"XT{l}_{e - 2}"] + 1)
                sp.dma_start(XG[e % 2], slots_in[e * P:(e + 1) * P, :]).then_inc(xg_landed[e % 2], 16)

            def overflow(l):
                ov = over[l]
                sp.wait_ge(psum_full, T[f"Y{l}_{NE - 1}"] + 1)
                sp.wait_ge(S["routed"], l + 1)
                n = sp.value_load(OVI[0:1, 0:1], min_val=0, max_val=N_OVER)
                with sp.If(n > 0):
                    with sp.Fori(0, n) as x:
                        x = nc.s_assert_within(x, 0, N_OVER - 1)
                        e = sp.value_load(OVI[0:1, bass.ds(x + 1, 1)], min_val=0, max_val=NE - 1)
                        for q, w in enumerate((A["moe_w1"], A["moe_w3"], A["moe_w2"])):
                            sp.dma_start(MR[q].rearrange("p (k c) -> p k c", k=w.shape[2] // P),
                                         w[l][bass.ds(e, 1)].rearrange("o (k p) c -> p (o k) c", p=P)
                                         ).then_inc(ov["in"], 16)
                        sp.dma_start(XG[0], slots_in[bass.ds(x * P + NE * P, P), :]).then_inc(ov["in"], 16)
                        sp.wait_ge(ov["out_of_psum"], x * 4 + 4)
                        sp.dma_start(slots_out[bass.ds(x * P + NE * P, P), :], YB[0]).then_inc(ov["stored"], 16)
                        sp.wait_ge(ov["stored"], x * 16 + 16)
                        sp.nop().then_inc(ov["through"], 1)
                sp.nop().then_inc(S["over_done"], 1)

            def moe(l):
                sp.wait_ge(psum_full, T["wout" if l == 0 else "wo"] + KT)
                if l == 0:
                    load_until(("mod", 1, 2))
                    sp.wait_ge(S["zero_filled"], 32)
                for e in range(3):
                    expert_weights(l, e)
                if l == 0:
                    load_until(("mod", 1, 7))
                for e in range(2):
                    expert_rows(l, e)
                    if l == 0:
                        load_until(("mod", 1, mods_of_expert(e)[-1]))
                expert_rows(l, 2)
                for e in range(3, NE):
                    expert_rows(l, e)
                    expert_weights(l, e)
                    if l == 0:
                        load_until(("mod", 1, mods_of_expert(e - 1)[-1]))
                if l == 0:
                    load_until(("mod", 1, mods_of_expert(NE - 1)[-1]))
                    load_until(("rw_g1", 0))
                overflow(l)

            load_until(("ab_w_out", 3))
            moe(0)
            load_until(("rw_wo", 3))
            moe(1)
            for c in range(NCH):
                read_out(sp, T["yT"] + c)
                dst = outs["y_prompt"][0] if c == 0 else outs["y_sample"][0, (c - 1) * P:c * P, :]
                sp.dma_start(dst, YT[:, c, :]).then_inc(S["y_sent"], 16)
            sp.wait_ge(S["y_sent"], 16 * NCH)

        @block.gpsimd
        def _(pool):
            nc.gpsimd.memset(vrow, 0.0).then_inc(S["vec_clear"], 1)
            pool.wait_ge(S["vec_clear"], 1)
            for name, rows in VECS:
                at = VB[name]
                src = A[name]
                nd = len(src.shape)
                letters = " ".join("abcdefg"[:nd])
                flat = src.rearrange(f"{letters} -> ({letters})") if nd > 1 else src
                pool.dma_start(vrow[at % P:at % P + rows, (at // P) * P:(at // P + 1) * P],
                               flat.rearrange("(r c) -> r c", c=P)).then_inc(S["vec_in"], 16)
            nc.gpsimd.memset(GW, 0.0).then_inc(S["gates_clear"], 1)
            pool.wait_ge(S["gates_clear"], 1)
            gw = GW.rearrange("p (j c) -> p j c", c=P)
            for wi, name in enumerate(("rg_wa", "rg_wx")):
                for d in range(2):
                    src = A[name][0, d].rearrange("(c b) i j -> b i c j", b=2)
                    for b in range(2):
                        j0 = (d * 2 + wi) * 4
                        pool.dma_start(gw[HD * b:HD * b + HD, j0:j0 + 4, HD * b:HD * b + HD],
                                       src[b]).then_inc(S["gates_in"], 16)
            pool.dma_start(rwR.rearrange("p (k e) -> p k e", e=NE),
                           A["moe_router"].rearrange("(k p) e -> p k e", p=P)).then_inc(S["router_in"], 16)
            rb = A["moe_router_bias"].rearrange("(o e) -> o e", o=1)
            pool.dma_start(rbias, rb.to_broadcast([P, NE])).then_inc(S["router_in"], 16)
            nc.gpsimd.memset(ZERO, 0.0).then_inc(S["zero_ready"], 1)
            pool.wait_ge(psum_full, T["gate7"] + 2)
            pool.dma_start(SIN.rearrange("p (j v) -> p j v", v=P),
                           A["state_hgrn"][0, 0].rearrange("d h k v -> k (d h) v")).then_inc(S["st_in"], 16)
            for h in range(NH_A):
                for lv in range(LEVELS):
                    i = h * LEVELS + lv
                    s = 1 << lv
                    nb = NT // (2 * s)
                    ek = EK[i % 3].rearrange("p (n two s) -> p n two s", two=2, s=s)
                    kf = K[0][:, h, :].rearrange("p (n two s) -> p n two s", two=2, s=s)
                    kb = K[1][:, h, :].rearrange("p (n two s) -> p n two s", two=2, s=s)
                    pool.wait_ge(S["lvl_exp"], 2 * i + 2)
                    nc.gpsimd.tensor_tensor(ek[:, :, 0, :], ek[:, :, 0, :], kf[:, :, 0, :], ALU.mult)
                    nc.gpsimd.tensor_tensor(ek[:, :, 1, :], ek[:, :, 1, :], kb[:, :, 1, :],
                                            ALU.mult).then_inc(S["lvl_k"], 1)
            def moe(l):
                pool.wait_ge(S["zero_filled"], 32)
                pool.wait_ge(S["routed"], l + 1)
                for c in range(NCH):
                    read_out(pool, T[f"htok{l}"] + c)
                    for j in range(2):
                        pool.indirect_dma_start(
                            slots_in, bass.IndirectOffsetOnAxis(ap=PI[:, j * NCH + c:j * NCH + c + 1], axis=0),
                            HTOK[:, c, :], None).then_inc(S["slots_filled"], 16)
                for e in range(NE):
                    read_out(pool, T[f"Y{l}_{e}"])
                    pool.dma_start(slots_out[e * P:(e + 1) * P, :], YB[e % 2]).then_inc(y_stored[e % 2], 16)
                for i in range(2):
                    pool.wait_ge(y_stored[i], 16 * (NE // 2) * (l + 1))
                pool.wait_ge(S["over_done"], l + 1)
                for c in range(NCH):
                    for j in range(2):
                        pool.indirect_dma_start(
                            (G0, G1)[j][:, c, :], None, slots_out,
                            bass.IndirectOffsetOnAxis(ap=PI[:, j * NCH + c:j * NCH + c + 1], axis=0)
                        ).then_inc(gathered[c], 16)

            moe(0)
            pool.wait_ge(psum_full, T["w2_0"] + KT)
            for dst, name in ((W2s, "rw_w2"), (A2s, "rw_a2")):
                pool.dma_start(dst, A[name][0].rearrange("d r c -> (d r) c")).then_inc(S["lora_in"], 16)
            pool.wait_ge(psum_full, T["V"] + 2 * NCH)
            stsrc = A["state_rwkv"][0, 0]
            for d in range(2):
                pool.dma_start(NATST[d][0:HD, :].rearrange("v (h k) -> v h k", k=HD),
                               stsrc[d].rearrange("h v k -> v h k")).then_inc(S["rw_st_in"], 16)
            for d in range(2):
                for q in range(2):
                    nc.gpsimd.memset(STR[d][f"RHS4_{q}"], 0.0).then_inc(S["rw_clear"], 1)
            nc.gpsimd.memset(Hf[:, :], 0.0).then_inc(S["rw_clear"], 1)
            nc.gpsimd.memset(BON, 0.0).then_inc(S["rw_clear"], 1)
            moe(1)

        @block.tensor
        def _(pe):
            nxt = [0]

            def open_tile(n):
                assert n == nxt[0], (n, nxt[0])
                nxt[0] += 1
                if n >= RING_P:
                    pe.wait_ge(psum_free[n % RING_P], n // RING_P)
                return tile(n)

            def done(ins):
                ins.then_inc(psum_full, 1)

            def weights(key, c=256, kt=KT):
                i = slot_no[key]
                pe.wait_ge(w_landed[i % RING_W], landed_at[i])
                return slot(i)[:, 0:kt * c].rearrange("p (k c) -> p k c", c=c)

            def mm(out, lhsT, rhs, start=True, stop=True):
                return nc.tensor.matmul(out, lhsT, rhs, start=start, stop=stop)

            def wide(ps, lhsT, rhs, start=True, stop=True):
                mm(ps[:, 0:512], lhsT, rhs[:, 0:512], start, stop)
                return mm(ps[:, 512:NT], lhsT, rhs[:, 512:NT], start, stop)

            def project(n, key, j, rhs, c=256):
                w = weights(key, c)
                ps = open_tile(n)
                for k in range(KT):
                    ins = wide(ps, w[:, k, j * P:(j + 1) * P], rhs(k), k == 0, k == KT - 1)
                done(ins)

            def project_tokens(n0, keys, lhs):
                ws = [weights(key) for key in keys]
                for c in range(NCH):
                    ps = open_tile(n0 + c)
                    for q in range(2):
                        for k in range(KT):
                            ins = mm(ps[:, 256 * q:256 * q + 256], lhs[:, k, c * P:(c + 1) * P], ws[q][:, k, :],
                                     k == 0, k == KT - 1)
                    done(ins)

            def mod_piece(n, layer, i):
                w = weights(("mod", layer, i))
                ps = open_tile(n)
                for k in range(KT):
                    ins = mm(ps[0:2, 0:256], silu_c[:, 2 * k:2 * k + 2], w[:, k, :], k == 0, k == KT - 1)
                done(ins)

            def mod_turn(n):
                read_out(pe, n - 1)
                ps = open_tile(n)
                for j in range(8):
                    ins = nc.tensor.transpose(ps[:, 2 * j:2 * j + 2], MROW[0:2, j * P:(j + 1) * P], ident[0:2, 0:2])
                done(ins)

            def norm_sums(i):
                ps = open_tile(T[f"norm{i}"])
                for k in range(KT):
                    pe.wait_ge(S["sq_ready"], KT * i + k + 1)
                    ins = wide(ps, ones, H[:, k, :], k == 0, k == KT - 1)
                done(ins)

            def fresh(i, k):
                pe.wait_ge(S["h_affine"], 2 * KT * i + 2 * (k + 1))
                return H[:, k, :]

            def moe(l):
                if l == 0:
                    pe.wait_ge(S["router_in"], 32)
                ps = open_tile(T[f"router{l}"])
                for c in range(NCH):
                    for k in range(KT):
                        ins = mm(ps[:, c * NE:(c + 1) * NE], fresh(2 * l + 1, k)[:, c * P:(c + 1) * P], rwR[:, k * NE:(k + 1) * NE],
                                 k == 0, k == KT - 1)
                done(ins)
                for c in range(NCH):
                    ps = open_tile(T[f"htok{l}"] + c)
                    for k in range(KT):
                        ins = nc.tensor.transpose(ps[:, k * P:(k + 1) * P], H[:, k, c * P:(c + 1) * P], ident)
                    done(ins)
                if l == 0:
                    for i in range(4):
                        mod_piece(T["mod1_a"] + i, 1, i)
                    mod_turn(T["mod1_a"] + 4)
                pe.wait_ge(S["chosen"], l + 1)
                ps = open_tile(T[f"rank{l}"])
                for c in range(NCH + 1):
                    out = ps[:, c * NE:(c + 1) * NE]
                    for c1 in range(min(c, NCH)):
                        ins = mm(out, ones, ch_[:, c1 * NE:(c1 + 1) * NE], c1 == 0, c == NCH and c1 == NCH - 1)
                    if c < NCH:
                        ins = mm(out, CO[:, C_RMASK:C_RMASK + P], ch_[:, c * NE:(c + 1) * NE], c == 0, True)
                done(ins)

                if l == 0:
                    for i in range(4, 8):
                        mod_piece(T["mod1_b"] + i - 4, 1, i)
                    mod_turn(T["mod1_b"] + 4)

                def turn_rows(ps, src, n):
                    for k in range(n):
                        ins = nc.tensor.transpose(ps[:, k * P:(k + 1) * P], src[:, k * P:(k + 1) * P], ident)
                    return ins

                def up(ps, xt, w1, w3):
                    for k in range(KT):
                        for q, w in enumerate((w1, w3)):
                            ins = mm(ps[:, 512 * q:512 * q + DE], xt[:, k * P:(k + 1) * P],
                                     w.rearrange("p (k c) -> p k c", c=DE)[:, k, :], k == 0, k == KT - 1)
                    return ins

                def down(ps, ht, w2):
                    w = w2.rearrange("p (f d) -> p f d", d=D)
                    for f in range(DE // P):
                        for q in range(2):
                            ins = mm(ps[:, 512 * q:512 * q + 512], ht[:, f * P:(f + 1) * P],
                                     w[:, f, 512 * q:512 * q + 512], f == 0, f == DE // P - 1)
                    return ins

                def m_weights(e, q):
                    i = 3 * e + q
                    per_layer = [len([x for x in range(3 * NE) if x % RING_M == i % RING_M]) for _ in range(l)]
                    pe.wait_ge(m_landed[i % RING_M], 16 * (sum(per_layer) + i // RING_M + 1))
                    return MR[i % RING_M]

                def rows_up(e):
                    pe.wait_ge(xg_landed[e % 2], 16 * (NE // 2 * l + e // 2 + 1))
                    ps = open_tile(T[f"XT{l}_{e}"])
                    done(turn_rows(ps, XG[e % 2], KT))

                def second_half(e):
                    read_out(pe, T[f"H13{l}_{e}"])
                    ps = open_tile(T[f"HT{l}_{e}"])
                    done(turn_rows(ps, HM[e % 2], DE // P))
                    read_out(pe, T[f"HT{l}_{e}"])
                    w2 = m_weights(e, 2)
                    ps = open_tile(T[f"Y{l}_{e}"])
                    done(down(ps, HMT[e % 2], w2))

                rows_up(0)
                for e in range(NE):
                    if e + 1 < NE:
                        rows_up(e + 1)
                    read_out(pe, T[f"XT{l}_{e}"])
                    w1, w3 = m_weights(e, 0), m_weights(e, 1)
                    ps = open_tile(T[f"H13{l}_{e}"])
                    done(up(ps, XGT[e % 2], w1, w3))
                    if e:
                        second_half(e - 1)
                    if l == 0:
                        for q, i in enumerate(mods_of_expert(e)):
                            mod_piece(T[f"mod1_{e}"] + q, 1, i)
                        if e % 4 == 3:
                            mod_turn(T[f"mod1_T{e // 4}"])
                second_half(NE - 1)
                ov = over[l]
                last = T[f"Y{l}_{NE - 1}"]
                for n in range(last - RING_P + 1, last + 1):
                    read_out(pe, n)
                pe.wait_ge(S["routed"], l + 1)
                n = pe.value_load(OVI[0:1, 0:1], min_val=0, max_val=N_OVER)
                with pe.If(n > 0):
                    with pe.Fori(0, n) as x:
                        pe.wait_ge(ov["in"], x * 64 + 64)
                        turn_rows(tile(0), XG[0], KT).then_inc(ov["pe"], 1)
                        pe.wait_ge(ov["out_of_psum"], x * 4 + 1)
                        up(tile(1), XGT[0], MR[0], MR[1]).then_inc(ov["pe"], 1)
                        pe.wait_ge(ov["out_of_psum"], x * 4 + 2)
                        turn_rows(tile(2), HM[0], DE // P).then_inc(ov["pe"], 1)
                        pe.wait_ge(ov["out_of_psum"], x * 4 + 3)
                        down(tile(3), HMT[0], MR[2]).then_inc(ov["pe"], 1)
                for k in range(KT):
                    ps = open_tile(T[f"w2_{l}"] + k)
                    for c in range(NCH):
                        pe.wait_ge(S["acc_ready"], NCH * l + c + 1)
                        ins = nc.tensor.transpose(ps[:, c * P:(c + 1) * P], G0[:, c, k * P:(k + 1) * P], ident)
                    done(ins)

            pe.wait_ge(S["consts_in"], 16)
            pe.wait_ge(S["vec_in"], 16 * len(VECS))
            ps = open_tile(T["vecT"])
            for i in range(3):
                ins = nc.tensor.transpose(ps[:, i * P:(i + 1) * P], vrow[:, i * P:(i + 1) * P], ident)
            done(ins)
            pe.wait_ge(S["x_in"], 32)
            for k in range(KT):
                ps = open_tile(T["xT"] + k)
                for c in range(NCH):
                    ins = nc.tensor.transpose(ps[:, c * P:(c + 1) * P], xtok[:, c, k * P:(k + 1) * P], ident)
                done(ins)
            pe.wait_ge(S["silu_c"], 1)
            for i in range(8):
                mod_piece(T[f"mod0a{i // 4}"] + i % 4, 0, i)
                if i % 4 == 3:
                    mod_turn(T[f"mod0a{i // 4}"] + 4)
            norm_sums(0)
            for j in range(4):
                project(T["xr"] + j, ("in", 10 + j // 2), j % 2, lambda k: fresh(0, k))
            for j in range(4):
                project(T["yr"] + j, ("in", 12 + j // 2), j % 2, lambda k: H[:, k, :])
            gw = GW.rearrange("p (j c) -> p j c", c=P)
            pe.wait_ge(S["gates_in"], 16 * 8)
            for u in range(8):
                c, d = u // 2, u % 2
                read_out(pe, T["xr"] + c)
                for g in range(2):
                    ps = open_tile(T[f"gate{u}"] + g)
                    done(wide(ps, gw[:, (d * 2 + g) * 4 + c, :], XC[:, c, :]))
                project(T[f"qk{u}"], ("in", u // 2), u % 2, lambda k: H[:, k, :])
                if u % 2 == 1:
                    for q in range(4):
                        mod_piece(T[f"mod0b{u // 2}"] + q, 0, 8 + 4 * (u // 2) + q)
                    mod_turn(T[f"mod0b{u // 2}"] + 4)
            for j in range(4):
                project(T["kb"] + j, ("in", 4 + j // 2), j % 2, lambda k: H[:, k, :])
            project_tokens(T["v"], [("in", 6), ("in", 7)], H)
            for j in range(4):
                project(T["og"] + j, ("in", 8 + j // 2), j % 2, lambda k: H[:, k, :])
            pe.wait_ge(S["lru_done"], 8)
            ps = open_tile(T["lruT"])
            done(nc.tensor.transpose(ps[0:8, 0:P], lru_fin, ident))
            pe.wait_ge(S["st_in"], 16)
            for h in range(NH_A):
                for lv in range(LEVELS):
                    i = h * LEVELS + lv
                    pe.wait_ge(S["lvl_q"], i + 1)
                    pe.wait_ge(S["lvl_k"], i + 1)
                    ps = open_tile(T[f"lvl{h}"] + lv)
                    for c in range(NCH):
                        cs = slice(c * P, (c + 1) * P)
                        ins = mm(ps[:, cs], EK[i % 3][:, cs], EQ[i % 3][:, cs])
                    done(ins)
                pe.wait_ge(S["head_ready"], h + 1)
                ps = open_tile(T[f"lvl{h}"] + LEVELS)
                for c in range(NCH):
                    cs = slice(c * P, (c + 1) * P)
                    ins = mm(ps[:, cs], KSUM[:, cs], Q[:, h, cs])
                done(ins)
                for d in range(2):
                    ps = open_tile(T[f"khT{h}"] + d)
                    for c in range(NCH):
                        ins = nc.tensor.transpose(ps[:, c * P:(c + 1) * P], KH[d][:, c * P:(c + 1) * P], ident)
                    done(ins)
                for d in range(2):
                    read_out(pe, T[f"khT{h}"] + d)
                    ps = open_tile(T[f"U{h}"] + d)
                    for c in range(NCH):
                        ins = mm(ps[:, c * P:(c + 1) * P], KHT[d][:, c * P:(c + 1) * P], VA[:, c, h * P:(h + 1) * P])
                    done(ins)
                read_out(pe, T[f"lvl{h}"] + LEVELS)
                for d in range(2):
                    read_out(pe, T[f"U{h}"] + d)
                ps = open_tile(T[f"o{h}"])
                for c in range(NCH):
                    cs = slice(c * P, (c + 1) * P)
                    ins = mm(ps[:, cs], VA[:, c, h * P:(h + 1) * P], ATT[:, cs], True, c == 0)
                    if c:
                        for d in range(2):
                            ins = mm(ps[:, cs], hgrn_state(d, c, h), QIN[d][:, cs], False, d == 1)
                done(ins)
                read_out(pe, T[f"o{h}"])
                ps = open_tile(T[f"on{h}"])
                done(wide(ps, ones, OSQ))
            pe.wait_ge(S["o_a_ready"], NH_A)
            for j in range(KT):
                project(T["wout"] + j, ("ab_w_out", j // 2), j % 2,
                        lambda k: OG[:, k, :] if k < NTA else YG[:, k - NTA, :])
            norm_sums(1)
            moe(0)
            norm_sums(2)

            def mixture(q, k):
                pe.wait_ge(S["xi_ready"], KT * q + k + 1)
                return XI[q % 2][:, k, :]

            for q, name in enumerate(("rw_w1", "rw_a1", "rw_g1")):
                project(T["lora"] + q, (name, 0), 0, lambda k: mixture(q, k), P)
            for q, (tn, name) in enumerate((("r", "rw_wr"), ("k", "rw_wk"))):
                for j in range(KT):
                    project(T[tn] + j, (name, j // 2), j % 2, lambda k: mixture(q + 3, k))
            pe.wait_ge(S["xi_ready"], KT * 6)
            for hf in range(2):
                project_tokens(T["V"] + hf * NCH, [("rw_wv", 2 * hf), ("rw_wv", 2 * hf + 1)], XI[1])
            pe.wait_ge(S["rw_st_in"], 32)
            for d in range(2):
                ps = open_tile(T["stT"] + d)
                for j in range(KT):
                    ins = nc.tensor.transpose(ps[:, j * HD:(j + 1) * HD], NATST[d][0:HD, j * P:(j + 1) * P],
                                              ident[0:HD, 0:HD])
                done(ins)
            pe.wait_ge(S["lora_in"], 32)

            def gate_tiles(g, st):
                for d in range(2):
                    z, ch, uid = STR[d], chunk_of(st, d), unit_id(g, st, d)
                    lo, ts = slice(HD * d, HD * d + HD), slice(ch * P, (ch + 1) * P)
                    ps = open_tile(T[f"P_{g}_{st}"] + d)
                    for q, (w2, hid) in enumerate(((W2s, hw), (A2s, ha))):
                        for j in range(UC):
                            ct = UC * g + j
                            mm(ps[:, (UC * q + j) * P:(UC * q + j + 1) * P], w2[lo, ct * P:(ct + 1) * P], hid[lo, ts])
                    pe.wait_ge(S["kk_sq"], uid + 1)
                    done(mm(ps[:, 2 * UW:3 * UW], bones, z["SQ"]))

            gate_tiles(0, 0)
            for g in range(NGRP):
                for st in range(NCH):
                    u = f"_{g}_{st}"
                    rh = f"RHS4_{(g * NCH + st) % 2}"
                    for d in range(2):
                        z = STR[d]
                        pe.wait_ge(S["unit_ready"], unit_id(g, st, d) + 1)
                        ps = open_tile(T["AR" + u] + d)
                        for j in range(UC):
                            ins = mm(ps[:, 512 * j:512 * j + 512], z["BE"][:, j * P:(j + 1) * P],
                                     z[rh][:, 512 * j:512 * j + 512])
                        done(ins)
                    for d in range(2):
                        z = STR[d]
                        ps = open_tile(T["BR" + u] + d)
                        for j in range(UC):
                            ins = mm(ps[:, 512 * j:512 * j + 512], z["KP"][:, j * P:(j + 1) * P],
                                     z[rh][:, 512 * j:512 * j + 512])
                        done(ins)
                    for d in range(2):
                        z = STR[d]
                        ps = open_tile(T["AN" + u] + d)
                        for j in range(UC):
                            mm(ps[:, 2 * j:2 * j + 2], z["SQ"][:, j * P:(j + 1) * P], hsel)
                        for q, key in enumerate(("KP", "BE")):
                            for j in range(UC):
                                c0 = 512 + (UC * q + j) * P
                                ins = nc.tensor.transpose(ps[:, c0:c0 + P], z[key][:, j * P:(j + 1) * P], ident)
                        done(ins)

                    def turn_over(ps, c0, src):
                        for hl in range(HG):
                            ins = nc.tensor.transpose(ps[:, c0 + hl * P:c0 + (hl + 1) * P],
                                                      src[:, hl * P:(hl + 1) * P], ident)
                        return ins

                    for d in range(2):
                        pe.wait_ge(S["mn_ready"], unit_id(g, st, d) + 1)
                        ps = open_tile(T["M0" + u] + d)
                        done(turn_over(ps, 0, STR[d]["N"]))
                    for lv in range(1, LEVELS):
                        s = 1 << lv
                        for d in range(2):
                            z = STR[d]
                            if lv == 1:
                                read_out(pe, T["M0" + u] + d)
                            else:
                                read_out(pe, T[f"D{lv - 1}" + u] + d)
                            ps = open_tile(T[f"G{lv}" + u] + d)
                            if lv > 1:
                                turn_over(ps, 512, z["M"])
                            for hl in range(HG):
                                m = z["M"][:, hl * P:(hl + 1) * P].rearrange("p (n w s) -> p n w s", w=2, s=s)
                                ins = mm(ps[:, hl * HD:(hl + 1) * HD], z["AR"][:, hl * 256:hl * 256 + P], m[:, :, d, :])
                            done(ins)
                        if lv == 2 and (g, st) != (NGRP - 1, NCH - 1):
                            gate_tiles(*next_step(g, st))
                        for d in range(2):
                            z, uid = STR[d], unit_id(g, st, d)
                            read_out(pe, T[f"G{lv}" + u] + d)
                            if lv > 1:
                                pe.wait_ge(S["n_out"], n_count(g, st, lv, d))
                            ps = open_tile(T[f"D{lv}" + u] + d)
                            for hl in range(HG):
                                ins = mm(ps[:, hl * HD:(hl + 1) * HD], z["N"][:, hl * P:(hl + 1) * P],
                                         z["G"][:, hl * HD:(hl + 1) * HD])
                            done(ins)
                    for d in range(2):
                        read_out(pe, T[f"D{LEVELS - 1}" + u] + d)
                        ps = open_tile(T["N6" + u] + d)
                        done(turn_over(ps, 0, STR[d]["M"]))
                    for d in range(2):
                        z, ch = STR[d], chunk_of(st, d)
                        if st:
                            pe.wait_ge(S["r0_ready"], 2 * (g * (NCH - 1) + st - 1) + d + 1)
                        ps = open_tile(T["RHS" + u] + d)
                        for hl in range(HG):
                            out = ps[:, hl * HD:(hl + 1) * HD]
                            hv = slice((HG * g + hl) * HD, (HG * g + hl + 1) * HD)
                            if st:
                                mm(out, z[rh][:, hl * 256:hl * 256 + P], z["R0"][:, (hl // 2) * HD:(hl // 2 + 1) * HD],
                                   True, False)
                            ins = mm(out, z["BR"][:, hl * 256:hl * 256 + P], V1[:, ch, hv], st == 0, True)
                        done(ins)
                    for d in range(2):
                        z = STR[d]
                        read_out(pe, T["RHS" + u] + d)
                        read_out(pe, T["N6" + u] + d)
                        ps = open_tile(T["Us" + u] + d)
                        for hl in range(HG):
                            ins = mm(ps[:, hl * HD:(hl + 1) * HD], z["N"][:, hl * P:(hl + 1) * P],
                                     z["RH"][:, hl * HD:(hl + 1) * HD])
                        done(ins)
                    for d in range(2):
                        z, ch = STR[d], chunk_of(st, d)
                        ps = open_tile(T["OT" + u] + d)
                        read_out(pe, T["Us" + u] + d)
                        pe.wait_ge(S["kb_t"], unit_id(g, st, d) + 1)
                        for j in range(UC):
                            out = ps[:, 512 + j * P:512 + (j + 1) * P]
                            pv = slice((UC * g + j) * P, (UC * g + j + 1) * P)
                            mm(out, z["KBT"][:, j * P:(j + 1) * P], V1[:, ch, pv], True, False)
                            mm(out, z["KBT"][:, (UC + j) * P:(UC + j + 1) * P], z["U"][:, j * P:(j + 1) * P],
                               False, True)
                        for hl in range(HG):
                            out = ps[:, hl * HD:(hl + 1) * HD]
                            hv = slice((HG * g + hl) * HD, (HG * g + hl + 1) * HD)
                            mm(out, z["BR"][:, hl * 256 + P:(hl + 1) * 256], V1[:, ch, hv], True, False)
                            ins = mm(out, z["AR"][:, hl * 256 + P:(hl + 1) * 256], z["U"][:, hl * HD:(hl + 1) * HD],
                                     False, st == 0)
                            if st:
                                ins = mm(out, z[rh][:, hl * 256 + P:(hl + 1) * 256],
                                         z["R0"][:, (hl // 2) * HD:(hl // 2 + 1) * HD], False, True)
                        done(ins)
                    if st == 0:
                        pe.wait_ge(S["ctx_state"], 2 * g + 2)
                        ps = open_tile(T["fin" + u])
                        for d in range(2):
                            for j in range(UC):
                                ins = nc.tensor.transpose(ps[0:HD, (UC * d + j) * P:(UC * d + j + 1) * P],
                                                          STR[d]["SF"][:, j * HD:(j + 1) * HD], ident)
                        done(ins)
            for k in range(KT):
                gk, jk = divmod(k, UC)
                pe.wait_ge(S["z_ready"], NCH * (gk + 1))
                for q in range(2):
                    ps = open_tile(T[f"post{k}"] + q)
                    for c in range(NCH):
                        src = Z2[gk][:, c, jk * P:(jk + 1) * P] if q else OT[:, c, k * P:(k + 1) * P]
                        ins = nc.tensor.transpose(ps[:, c * P:(c + 1) * P], src, ident)
                    done(ins)
                w = weights(("rw_g2", 0), D, 1)
                ps = open_tile(T[f"post{k}"] + 2)
                done(wide(ps, w[:, 0, k * P:(k + 1) * P], hg))
            read_out(pe, T["post7"] + 2)
            for j in range(KT):
                project(T["wo"] + j, ("rw_wo", j // 2), j % 2, lambda k: OC[:, k, :])
            norm_sums(3)
            moe(1)
            norm_sums(4)
            pe.wait_ge(S["h_affine"], 4 * 2 * KT + KT)
            for c in range(NCH):
                ps = open_tile(T["yT"] + c)
                for k in range(KT):
                    ins = nc.tensor.transpose(ps[:, k * P:(k + 1) * P], H[:, k, c * P:(c + 1) * P], ident)
                done(ins)

        @block.scalar
        def _(act):
            n_chain = [0]
            A_ = nc.scalar.activation

            def link(ins):
                n_chain[0] += 1
                ins.then_inc(act_chain, 1)
                act.wait_ge(act_chain, n_chain[0])

            def squares():
                for k in range(KT):
                    A_(H[:, k, :], X[:, k, :], ACT.Square).then_inc(S["sq_ready"], 1)

            def norm_tail(i, layer, shift):
                n = T[f"norm{i}"]
                ps = full(act, n)
                link(A_(ps[:, 0:NT], ps[:, 0:NT], ACT.Ln, bias=eps_rms, scale=1.0 / D))
                A_(ps[:, 0:NT], ps[:, 0:NT], ACT.Exp, scale=-0.5).then_inc(S["rms_root"], 1)
                if i < 4:
                    act.wait_ge(S["coef_ready"], i + 1)
                for k in range(KT):
                    if k % 2 == 0:
                        act.wait_ge(S["h_scaled"], 4 * i + k // 2 + 1)
                    if i == 4:
                        A_(H[:, k, :], H[:, k, :], ACT.Identity, scale=vcol("norm_f_g", k)).then_inc(S["h_affine"], 1)
                        continue
                    for s, (a, b) in enumerate(SEGS):
                        A_(H[:, k, a:b], H[:, k, a:b], ACT.Identity, scale=coef[i][:, 2 * k + s:2 * k + s + 1],
                           bias=MOD[:, layer, shift + k, s:s + 1]).then_inc(S["h_affine"], 1)

            def moe(l):
                n = T[f"router{l}"]
                ps = full(act, n)
                free(A_(sc_, ps[:, 0:NCH * NE], ACT.Sigmoid), n)
                for c in range(NCH):
                    n = T[f"htok{l}"] + c
                    ps = full(act, n)
                    free(A_(HTOK[:, c, :], ps, ACT.Copy), n)

                def outputs(e):
                    n = T[f"HT{l}_{e}"]
                    ps = full(act, n)
                    free(A_(HMT[e % 2], ps[:, 0:DE], ACT.Copy), n)
                    n = T[f"Y{l}_{e}"]
                    ps = full(act, n)
                    if e >= 2:
                        act.wait_ge(y_stored[e % 2], 16 * (NE // 2 * l + e // 2))
                    free(A_(YB[e % 2], ps, ACT.Copy), n)

                for e in range(NE):
                    n = T[f"H13{l}_{e}"]
                    ps = full(act, n)
                    A_(SH[e % 2], ps[:, 0:DE], ACT.Silu).then_inc(S["silu_out"], 1)
                    if e:
                        outputs(e - 1)
                outputs(NE - 1)
                ov = over[l]
                act.wait_ge(S["routed"], l + 1)
                n = act.value_load(OVI[0:1, 0:1], min_val=0, max_val=N_OVER)
                with act.If(n > 0):
                    with act.Fori(0, n) as x:
                        act.wait_ge(ov["pe"], x * 4 + 2)
                        A_(SH[0], tile(1)[:, 0:DE], ACT.Silu).then_inc(ov["silu"], 1)

            read_out(act, T["vecT"])
            sc2 = silu_c.rearrange("p (k s) -> p k s", s=2)
            A_(sc2[:, :, 0], vcol("c_ctx", 0, KT), ACT.Silu)
            A_(sc2[:, :, 1], vcol("c", 0, KT), ACT.Silu).then_inc(S["silu_c"], 1)
            act.wait_ge(S["lb_diff"], 1)
            A_(lbt, lbt, ACT.Exp)
            A_(splam, splam, ACT.Exp, scale=-1.0).then_inc(S["lb_exp"], 1)
            read_out(act, T["xT"] + KT - 1)
            squares()
            norm_tail(0, 0, 0)
            act.wait_ge(S["lb_done"], 1)
            for j in range(4):
                n = T["xr"] + j
                ps = full(act, n)
                A_(XC[:, j, :], ps[:, 0:NT], ACT.Identity, scale=vcol("rg_conv_w", 2 * NTA + j),
                   bias=vcol("rg_conv_b", j)).then_inc(S["conv_base"], 1)
            for j in range(4):
                n = T["yr"] + j
                ps = full(act, n)
                free(A_(YG[:, j, :], ps[:, 0:NT], ACT.Gelu_apprx_tanh), n)
            for u in range(8):
                c, d = u // 2, u % 2
                n = T[f"gate{u}"]
                if u:
                    act.wait_ge(S["lru_done"], u)
                ps = full(act, n)
                free(A_(lr, ps[:, 0:NT], ACT.Sigmoid, bias=vcol("rg_ba", 4 * d + c)), n)
                ps = full(act, n + 1)
                free(A_(li, ps[:, 0:NT], ACT.Sigmoid, bias=vcol("rg_bx", 4 * d + c)), n + 1)
                read_out(act, n)
                A_(lth, lr, ACT.Tanh, scale=psp8[:, 4 * d + c:4 * d + c + 1])
                A_(la, lr, ACT.Exp, scale=nsp8[:, 4 * d + c:4 * d + c + 1]).then_inc(S["lru_th"], 1)
                act.wait_ge(S["lru_q"], u + 1)
                A_(lth, lth, ACT.Sqrt, scale=2.0).then_inc(S["lru_root"], 1)
                n = T[f"qk{u}"]
                ps = full(act, n)
                if u < 4:
                    free(A_(Q[:, u, :], ps[:, 0:NT], ACT.Silu), n)
                else:
                    A_(B[0][:, u - 4, :], ps[:, 0:NT], ACT.Sigmoid)
                    free(A_(K[0][:, u - 4, :], ps[:, 0:NT], ACT.Sigmoid, scale=-1.0), n)
            for j in range(4):
                n = T["kb"] + j
                ps = full(act, n)
                A_(B[1][:, j, :], ps[:, 0:NT], ACT.Sigmoid)
                free(A_(K[1][:, j, :], ps[:, 0:NT], ACT.Sigmoid, scale=-1.0), n)
            for c in range(NCH):
                n = T["v"] + c
                ps = full(act, n)
                free(A_(VA[:, c, :], ps[:, 0:DA], ACT.Copy), n)
            for d in range(2):
                if d == 1:
                    read_out(act, T["kb"] + 3)
                else:
                    read_out(act, T["qk7"])
                for j in range(4):
                    A_(B[d][:, j, :], B[d][:, j, :], ACT.Ln, scale=omlb[:, 4 * d + j:4 * d + j + 1],
                       bias=lb[:, 4 * d + j:4 * d + j + 1]).then_inc(S["f_log"], 1)
            for j in range(4):
                n = T["og"] + j
                ps = full(act, n)
                free(A_(OG[:, j, :], ps[:, 0:NT], ACT.Silu), n)
            act.wait_ge(S["zero_ready"], 1)
            for dst in (slots_in, slots_out):
                act.dma_start(dst.rearrange("(a p) d -> p a d", p=P),
                              ZERO.unsqueeze(1).broadcast_to([P, NE + N_OVER, D])).then_inc(S["zero_filled"], 16)
            read_out(act, T["lruT"])
            act.dma_start(outs["rglru"][0, 0].rearrange("d (c p) -> (d c) p", p=P),
                          LROWS[0:8, 0:P]).then_inc(S["lru_sent"], 16)
            def head_root(h):
                ps = full(act, T[f"on{h}"])
                link(A_(ps[:, 0:NT], ps[:, 0:NT], ACT.Ln, bias=eps_rms, scale=1.0 / P))
                A_(ps[:, 0:NT], ps[:, 0:NT], ACT.Exp, scale=-0.5).then_inc(S["on_root"], 1)

            act.preload_act_table_set("natural_log_exp_and_others")
            for h in range(NH_A):
                act.wait_ge(S["head_diff"], h + 1)
                for d in range(2):
                    A_(KH[d], KH[d], ACT.Exp)
                    A_(QIN[d][:, CTX:NT], B[d][:, h, CTX:NT], ACT.Exp)
                    e0 = P - 1 if d == 0 else 0
                    ins = A_(gend[:, NCH * d:NCH * (d + 1)], B[d][:, h, e0::P], ACT.Exp)
                ins.then_inc(S["head_exp"], 1)
                for lv in range(LEVELS):
                    i = h * LEVELS + lv
                    act.wait_ge(S["lvl_diff"], i + 1)
                    A_(EQ[i % 3], EQ[i % 3], ACT.Exp).then_inc(S["lvl_exp"], 1)
                    A_(EK[i % 3], EK[i % 3], ACT.Exp).then_inc(S["lvl_exp"], 1)
                    if h and lv == 0:
                        head_root(h - 1)
                for d in range(2):
                    n = T[f"khT{h}"] + d
                    ps = full(act, n)
                    free(A_(KHT[d], ps[:, 0:NT], ACT.Copy), n)
                for d in range(2):
                    act.wait_ge(S["s_final"], 2 * h + d + 1)
                    act.dma_start(outs["hgrn"][0, 0, d, h], SFIN[d]).then_inc(S["s_final_sent"], 16)
                n = T[f"o{h}"]
                ps = full(act, n)
                if h:
                    act.wait_ge(S["o_a_ready"], h)
                A_(OCP, ps[:, 0:NT], ACT.Copy)
                free(A_(OSQ, ps[:, 0:NT], ACT.Square), n)
            head_root(NH_A - 1)
            act.wait_ge(S["lru_sent"], 16)
            act.wait_ge(S["s_final_sent"], 16 * 2 * NH_A)
            read_out(act, T["wout"] + KT - 1)
            squares()
            norm_tail(1, 0, 24)
            moe(0)
            read_out(act, T["w2_0"] + KT - 1)
            squares()
            norm_tail(2, 1, 0)
            act.dma_start(xspill, Xf[:, :]).then_inc(S["x_parked"], 16)
            for q, f in enumerate((ACT.Tanh, ACT.Copy, ACT.Sigmoid)):
                n = T["lora"] + q
                ps = full(act, n)
                free(A_((hw, ha, hg)[q], ps[:, 0:NT], f), n)
            for tn, dst in (("r", R1), ("k", K1)):
                for j in range(KT):
                    n = T[tn] + j
                    ps = full(act, n)
                    free(A_(dst[:, j, :], ps[:, 0:NT], ACT.Copy), n)
            for hf in range(2):
                for c in range(NCH):
                    n = T["V"] + hf * NCH + c
                    ps = full(act, n)
                    free(A_(V1[:, c, 512 * hf:512 * hf + 512], ps[:, 0:512], ACT.Copy), n)
            read_out(act, T["k"] + KT - 1)

            def key_squares(g, st, d):
                z, ch, uid = STR[d], chunk_of(st, d), unit_id(g, st, d)
                ts = slice(ch * P, (ch + 1) * P)
                if uid >= 2:
                    act.wait_ge(S["unit_ready"], uid - 1)
                    pg, pst = (g, st - 1) if st else (g - 1, NCH - 1)
                    act.wait_ge(psum_full, T[f"AN_{pg}_{pst}"] + d + 1)
                else:
                    act.wait_ge(psum_full, T["V"] + 2 * NCH)
                for j in range(UC):
                    ct = UC * g + j
                    ins = A_(z["KK"][:, j * P:(j + 1) * P], K1[:, ct, ts], ACT.Identity, scale=vcol("rw_kk", ct))
                link(ins)
                A_(z["SQ"], z["KK"], ACT.Square).then_inc(S["kk_sq"], 1)

            def gate_exps(g, st, d):
                z = STR[d]
                n = T[f"P_{g}_{st}"] + d
                ps = full(act, n)
                for q, nb in enumerate((nw0, na0)):
                    for j in range(UC):
                        c0 = (UC * q + j) * P
                        bi = 8 * d + UC * g + j
                        ins = A_(z["LA"][:, c0:c0 + P], ps[:, c0:c0 + P], ACT.Exp, scale=-1.0, bias=nb[:, bi:bi + 1])
                ins.then_inc(S["gates_exp"], 1)

            def gate_logs(g, st, d):
                z, uid = STR[d], unit_id(g, st, d)
                act.wait_ge(S["gates_clamped"], uid + 1)
                A_(z["SQ"], z["SQ"], ACT.Ln)
                link(A_(z["LA"], z["LA"], ACT.Ln, bias=half_one[:, 0:1]))
                A_(z["SQ"], z["SQ"], ACT.Exp, scale=-0.5)
                A_(z["LA"], z["LA"], ACT.Exp, scale=-1.0).then_inc(S["gates_done"], 1)

            def decay_exps(g, st, d):
                z, uid = STR[d], unit_id(g, st, d)
                h0 = 4 * ((g * NCH + st) % 2) + 2 * d
                act.wait_ge(S["decay_sum"], uid + 1)
                A_(em[:, h0:h0 + 2], hb[:, h0:h0 + 2], ACT.Exp, scale=-W_DECAY)
                A_(z["E1"], z["B"], ACT.Exp, scale=-W_DECAY)
                A_(z["E2"], z["B"], ACT.Exp, scale=W_DECAY)
                A_(z["E3"], z["E3"], ACT.Exp, scale=-W_DECAY).then_inc(S["decay_exp"], 1)

            def gn_square(g, c):
                act.wait_ge(S["gn_centred"], NCH * g + c + 1)
                A_(Z2[g][:, c, :], OT[:, c, UW * g:UW * (g + 1)], ACT.Square).then_inc(S["gn_sq"], 1)

            def gn_root(g, c):
                act.wait_ge(S["gn_var"], NCH * g + c + 1)
                var = gn_stats(c)[1]
                link(A_(var, var, ACT.Ln, bias=eps_gn, scale=1.0 / HD))
                A_(var, var, ACT.Exp, scale=-0.5).then_inc(S["gn_root"], 1)

            act.preload_act_table_set("natural_log_exp_and_others")
            for stage in (key_squares, gate_exps, gate_logs, decay_exps):
                for d in range(2):
                    stage(0, 0, d)
            for g in range(NGRP):
                for st in range(NCH):
                    u = f"_{g}_{st}"
                    nx = None if (g, st) == (NGRP - 1, NCH - 1) else next_step(g, st)
                    for d in range(2):
                        n = T["AN" + u] + d
                        ps = full(act, n)
                        A_(STR[d]["KBT"], ps[:, 512:512 + 2 * UW], ACT.Copy).then_inc(S["kb_t"], 1)
                    for d in range(2):
                        n = T["M0" + u] + d
                        ps = full(act, n)
                        free(A_(STR[d]["M"], ps[:, 0:HG * P], ACT.Copy), n)
                    if nx:
                        for d in range(2):
                            key_squares(*nx, d)
                    for lv in range(2, LEVELS):
                        for d in range(2):
                            ps = full(act, T[f"G{lv}" + u] + d)
                            A_(STR[d]["N"], ps[:, 512:512 + HG * P], ACT.Copy).then_inc(S["n_out"], 1)
                        if nx:
                            if lv == 2:
                                gate_exps(*nx, 0)
                                gate_exps(*nx, 1)
                            elif lv == 3:
                                gate_logs(*nx, 0)
                                gate_logs(*nx, 1)
                                if g:
                                    gn_square(g - 1, st)
                            elif lv == 4:
                                decay_exps(*nx, 0)
                            elif lv == 5:
                                decay_exps(*nx, 1)
                        elif lv == 3:
                            gn_square(g - 1, st)
                        if g and lv == 6:
                            gn_root(g - 1, st)
                    for name, key, size, scale in (("N6", "N", HG * P, 1.0), ("RHS", "RH", HG * HD, 1.0),
                                                   ("Us", "U", HG * HD, -1.0)):
                        for d in range(2):
                            n = T[name + u] + d
                            ps = full(act, n)
                            if name == "RHS" and st == 1:
                                act.wait_ge(S["ctx_state_sent"], 32 * (g + 1))
                            free(A_(STR[d][key], ps[:, 0:size], ACT.Copy, scale=scale), n)
                    if st == 0:
                        read_out(act, T["fin" + u])
                        for d in range(2):
                            act.dma_start(outs["rwkv"][0, 0, d, HG * g:HG * (g + 1)].rearrange("h v k -> v h k"),
                                          FINB[0:HD, d * 256:(d + 1) * 256].rearrange("v (h k) -> v h k", k=HD)
                                          ).then_inc(S["ctx_state_sent"], 16)
            act.wait_ge(S["ctx_state_sent"], 32 * NGRP)
            act.wait_ge(S["scan_done"], 1)
            act.dma_start(Xf[:, :], xspill).then_inc(S["x_back"], 16)
            for c in range(NCH):
                gn_square(NGRP - 1, c)
            for c in range(NCH):
                gn_root(NGRP - 1, c)
            for k in range(KT):
                n = T[f"post{k}"]
                ps = full(act, n)
                free(A_(OC[:, k, :], ps[:, 0:NT], ACT.Identity, scale=vcol("rw_lnw", k), bias=vcol("rw_lnb", k)), n)
            read_out(act, T["wo"] + KT - 1)
            squares()
            norm_tail(3, 1, 24)
            moe(1)
            read_out(act, T["w2_1"] + KT - 1)
            squares()
            norm_tail(4, 1, 0)

        @block.vector
        def _(dve):
            n_chain = [0]
            TT = nc.vector.tensor_tensor
            TS = nc.vector.tensor_scalar
            STT = nc.vector.scalar_tensor_tensor

            def link(ins):
                n_chain[0] += 1
                ins.then_inc(dve_chain, 1)
                dve.wait_ge(dve_chain, n_chain[0])

            def mod_evac(n, layer, i):
                q = i % 4
                ps = full(dve, n)
                free(nc.vector.tensor_copy(MROW[0:2, q * 256:q * 256 + 256], ps[0:2, 0:256]), n)
                if q == 3:
                    n += 1
                    ps = full(dve, n)
                    b = vcol("b_mod", 48 * layer + 2 * i - 6, 8).unsqueeze(2).broadcast_to([P, 8, 2])
                    free(TT(MOD[:, layer, 2 * i - 6:2 * i + 2, :], ps[:, 0:16].rearrange("p (j s) -> p j s", s=2), b,
                            ALU.add), n)

            def make_coef(i, layer, scale, g):
                gv = g.unsqueeze(2).broadcast_to([P, KT, 2])
                STT(coef[i].rearrange("p (k s) -> p k s", s=2), MOD[:, layer, scale:scale + KT, :], 1.0, gv,
                    ALU.add, ALU.mult).then_inc(S["coef_ready"], 1)

            def norm_apply(i):
                n = T[f"norm{i}"]
                dve.wait_ge(S["rms_root"], i + 1)
                ps = tile(n)
                for q in range(4):
                    r = ps[:, 0:NT].unsqueeze(1).broadcast_to([P, 2, NT])
                    TT(H[:, 2 * q:2 * q + 2, :], X[:, 2 * q:2 * q + 2, :], r, ALU.mult).then_inc(S["h_scaled"], 1)
                dve.wait_ge(S["h_scaled"], 4 * i + 4)
                free(nc.vector.tensor_copy(lut[:, 0:1], ps[:, 0:1]), n)

            def residual(tn, layer, gate):
                for k in range(KT):
                    n = T[tn] + k
                    ps = full(dve, n)
                    for s, (a, b) in enumerate(SEGS):
                        ins = STT(X[:, k, a:b], ps[:, a:b], MOD[:, layer, gate + k, s:s + 1], X[:, k, a:b],
                                  ALU.mult, ALU.add)
                    free(ins, n)

            def moe(l):
                n = T[f"router{l}"]
                read_out(dve, n)
                sc3 = sc_.rearrange("p (c e) -> p c e", e=NE)
                sl3 = sl_.rearrange("p (c e) -> p c e", e=NE)
                bias = rbias.unsqueeze(1).broadcast_to([P, NCH, NE])
                link(TT(sl3, sc3, bias, ALU.add))
                sl = sl_.rearrange("p (g i) -> p g i", i=EPG)
                NGT = NCH * NG
                rank = w0_.rearrange("p (g i) -> p g i", i=EPG)
                t0, t1 = w1_[:, 0:NGT], w1_[:, NGT:2 * NGT]
                gsc, gmx = w1_[:, 2 * NGT:3 * NGT], w1_[:, 3 * NGT:4 * NGT]
                link(TT(gsc, sl[:, :, 0], sl[:, :, 1], ALU.add))
                for i in range(EPG):
                    for j in range(i + 1, EPG):
                        if (i, j) != (0, 1):
                            link(TT(t0, sl[:, :, i], sl[:, :, j], ALU.add))
                            link(TT(gsc, gsc, t0, ALU.max))
                g3 = gsc.rearrange("p (c g) -> p c g", g=NG)
                best = gs_[:, 0:NGT].rearrange("p (c g) -> p c g", g=NG)
                mx = gmx[:, 0:NCH]
                link(nc.vector.reduce_max(mx, g3, AX.X))
                link(TT(best, g3, mx.unsqueeze(2).broadcast_to([P, NCH, NG]), ALU.is_ge))
                seen = gmx[:, NCH:2 * NCH]
                inv = gmx[:, 2 * NCH:3 * NCH]
                link(nc.vector.tensor_copy(seen, best[:, :, 0]))
                for g in range(1, NG):
                    link(TS(inv, seen, -1.0, 1.0, ALU.mult, ALU.add))
                    link(TT(best[:, :, g], best[:, :, g], inv, ALU.mult))
                    link(TT(seen, seen, best[:, :, g], ALU.add))
                for i in range(EPG):
                    first = True
                    for j in range(EPG):
                        if j == i:
                            continue
                        op = ALU.is_ge if j < i else ALU.is_gt
                        if first:
                            link(TT(rank[:, :, i], sl[:, :, j], sl[:, :, i], op))
                            first = False
                        else:
                            link(TT(t0, sl[:, :, j], sl[:, :, i], op))
                            link(TT(rank[:, :, i], rank[:, :, i], t0, ALU.add))
                gb = gs_[:, 0:NGT].unsqueeze(2).broadcast_to([P, NGT, EPG])
                ce = lambda a: a.rearrange("p (c e) -> p c e", e=NE)
                for j, se in enumerate((se0_, se1_)):
                    link(TS(se, w0_, float(j), None, ALU.is_equal))
                    link(TT(se.rearrange("p (g i) -> p g i", i=EPG), se.rearrange("p (g i) -> p g i", i=EPG), gb, ALU.mult))
                TT(ch_, se0_, se1_, ALU.add).then_inc(S["chosen"], 1)
                for j, se in enumerate((se0_, se1_)):
                    link(TT(w1_, se, sc_, ALU.mult))
                    link(nc.vector.reduce_sum(wj_[:, j * NCH:(j + 1) * NCH], ce(w1_), AX.X))
                if l == 0:
                    for i in range(4):
                        mod_evac(T["mod1_a"] + i, 1, i)
                wsum = wj_[:, 2 * NCH:3 * NCH]
                link(TT(wsum, wj_[:, 0:NCH], wj_[:, NCH:2 * NCH], ALU.add))
                link(nc.vector.reciprocal(wsum, wsum))
                for j in range(2):
                    link(TT(wj_[:, j * NCH:(j + 1) * NCH], wj_[:, j * NCH:(j + 1) * NCH], wsum, ALU.mult))
                n = T[f"rank{l}"]
                ps = full(dve, n)
                tot = ps[:, NCH * NE:(NCH + 1) * NE]
                link(TS(nov_, tot, float(P), None, ALU.is_gt))
                for q in range(2, NT // P):
                    link(TS(adj_, tot, float(q * P), None, ALU.is_gt))
                    link(TT(nov_, nov_, adj_, ALU.add))
                one = half_one[:, 0:1].broadcast_to([P, NE])
                link(nc.vector.tensor_tensor_scan(ovi_, one, nov_, 0.0, ALU.mult, ALU.add))
                e128 = CO[:, C_E128:C_E128 + NE]
                link(TT(adj_, ovi_, nov_, ALU.subtract))
                link(TS(adj_, adj_, float(P), float((NE - 1) * P), ALU.mult, ALU.add))
                link(TT(adj_, adj_, e128, ALU.subtract))
                link(TS(ge_, ps[:, 0:NCH * NE], float(P), None, ALU.is_ge))
                link(TT(ce(ge_), ce(ge_), adj_.unsqueeze(1).broadcast_to([P, NCH, NE]), ALU.mult))
                link(TT(ce(pos_), ce(ps[:, 0:NCH * NE]), e128.unsqueeze(1).broadcast_to([P, NCH, NE]), ALU.add))
                free(TT(pos_, pos_, ge_, ALU.add), n)
                read_out(dve, n)
                for j, se in enumerate((se0_, se1_)):
                    link(TT(w1_, se, pos_, ALU.mult))
                    link(nc.vector.reduce_sum(posf_[:, j * NCH:(j + 1) * NCH], ce(w1_), AX.X))
                nc.vector.tensor_copy(PI, posf_)
                ex3 = exo_.rearrange("p (x e) -> p x e", e=NE)
                link(TT(ex3, ovi_.unsqueeze(1).broadcast_to([P, 12, NE]),
                        CO[:, C_XIDX:C_XIDX + 12].unsqueeze(2).broadcast_to([P, 12, NE]), ALU.is_le))
                link(nc.vector.reduce_sum(ovf_, ex3, AX.X))
                link(TS(ovf_, ovf_, float(NE - 1), None, ALU.min))
                nc.vector.tensor_copy(OVI[:, 1:12], ovf_[:, 0:11])
                nc.vector.tensor_copy(OVI[:, 0:1], ovi_[:, NE - 1:NE]).then_inc(S["routed"], 1)

                if l == 0:
                    for i in range(4, 8):
                        mod_evac(T["mod1_b"] + i - 4, 1, i)

                def rows_out(e):
                    n = T[f"XT{l}_{e}"]
                    ps = full(dve, n)
                    free(nc.vector.tensor_copy(XGT[e % 2], ps), n)

                rows_out(0)
                for e in range(NE):
                    if e + 1 < NE:
                        rows_out(e + 1)
                    n = T[f"H13{l}_{e}"]
                    dve.wait_ge(S["silu_out"], NE * l + e + 1)
                    free(TT(HM[e % 2], SH[e % 2], tile(n)[:, 512:512 + DE], ALU.mult), n)
                    if l == 0:
                        for q, i in enumerate(mods_of_expert(e)):
                            mod_evac(T[f"mod1_{e}"] + q, 1, i)
                ov = over[l]
                dve.wait_ge(S["routed"], l + 1)
                n = dve.value_load(OVI[0:1, 0:1], min_val=0, max_val=N_OVER)
                with dve.If(n > 0):
                    dve.wait_ge(y_stored[0], 16 * (NE // 2) * (l + 1))
                    with dve.Fori(0, n) as x:
                        dve.wait_ge(ov["pe"], x * 4 + 1)
                        nc.vector.tensor_copy(XGT[0], tile(0)).then_inc(ov["out_of_psum"], 1)
                        dve.wait_ge(ov["silu"], x + 1)
                        TT(HM[0], SH[0], tile(1)[:, 512:512 + DE], ALU.mult).then_inc(ov["out_of_psum"], 1)
                        dve.wait_ge(ov["pe"], x * 4 + 3)
                        nc.vector.tensor_copy(HMT[0], tile(2)[:, 0:DE]).then_inc(ov["out_of_psum"], 1)
                        dve.wait_ge(ov["pe"], x * 4 + 4)
                        nc.vector.tensor_copy(YB[0], tile(3)).then_inc(ov["out_of_psum"], 1)
                for c in range(NCH):
                    dve.wait_ge(gathered[c], 32 * (l + 1))
                    link(TS(G0[:, c, :], G0[:, c, :], wj_[:, c:c + 1], None, ALU.mult))
                    STT(G0[:, c, :], G1[:, c, :], wj_[:, NCH + c:NCH + c + 1], G0[:, c, :], ALU.mult,
                        ALU.add).then_inc(S["acc_ready"], 1)
                residual(f"w2_{l}", l, 40)

            ps = full(dve, T["vecT"])
            free(nc.vector.tensor_copy(VT[:, :], ps[:, 0:3 * P]), T["vecT"])
            read_out(dve, T["vecT"])
            raw = vcol("hgrn_lb", 0, 16).rearrange("p (d n c) -> p d n c", d=2, n=2)
            l4 = lbt.rearrange("p (d n c) -> p d n c", d=2, n=2)
            m2 = lut[:, 0:8].rearrange("p (d c) -> p d c", d=2)
            link(TT(m2, raw[:, :, 0, :], raw[:, :, 1, :], ALU.max))
            for q in range(2):
                TT(l4[:, :, q, :], raw[:, :, q, :], m2, ALU.subtract)
            lam = vcol("rg_lambda", 0, 8)
            link(TS(lut[:, 8:16], lam, -1.0, None, ALU.mult))
            link(TS(lut[:, 8:16], lut[:, 8:16], 0.0, None, ALU.max))
            link(TS(lut[:, 16:24], lam, -1.0, None, ALU.mult))
            TT(splam, lam, lut[:, 16:24], ALU.max).then_inc(S["lb_diff"], 1)
            dve.wait_ge(S["consts_l0"], 16)
            for k in range(KT):
                n = T["xT"] + k
                ps = full(dve, n)
                nc.vector.tensor_copy(X[:, k, 0:CTX], ps[:, 0:CTX])
                rows = LAT // GRID_W
                if k < KT // 2:
                    pos = pos_r[:, k * rows:(k + 1) * rows].unsqueeze(2).broadcast_to([P, rows, GRID_W])
                else:
                    q = k - KT // 2
                    pos = pos_c[:, q * GRID_W:(q + 1) * GRID_W].unsqueeze(1).broadcast_to([P, rows, GRID_W])
                free(TT(X[:, k, CTX:NT].rearrange("p (r c) -> p r c", c=GRID_W),
                        ps[:, CTX:NT].rearrange("p (r c) -> p r c", c=GRID_W), pos, ALU.add), n)
            for i in range(8):
                mod_evac(T[f"mod0a{i // 4}"] + i % 4, 0, i)
            read_out(dve, T["mod0a1"] + 4)
            make_coef(0, 0, 8, vcol("norm_mix_g", 0, KT))
            dve.wait_ge(S["lb_exp"], 1)
            m3 = lut[:, 0:8].rearrange("p (d c) -> p d c", d=2)
            link(TT(m3, l4[:, :, 0, :], l4[:, :, 1, :], ALU.add))
            link(nc.vector.reciprocal(lut[:, 0:8], lut[:, 0:8]))
            TT(lb.rearrange("p (d c) -> p d c", d=2), l4[:, :, 0, :], m3, ALU.mult)
            TT(omlb.rearrange("p (d c) -> p d c", d=2), l4[:, :, 1, :], m3, ALU.mult)
            zz, z2, acc = lut[:, 16:24], lut[:, 24:32], lut[:, 32:40]
            link(TS(zz, splam, 2.0, None, ALU.add))
            link(nc.vector.reciprocal(zz, zz))
            link(TT(zz, zz, splam, ALU.mult))
            link(TT(z2, zz, zz, ALU.mult))
            link(TS(acc, z2, 1.0 / 17, 1.0 / 15, ALU.mult, ALU.add))
            for q in (13, 11, 9, 7, 5, 3, 1):
                link(TT(acc, acc, z2, ALU.mult))
                link(TS(acc, acc, 1.0 / q, None, ALU.add))
            link(TT(acc, acc, zz, ALU.mult))
            link(STT(splam, acc, 2.0, lut[:, 8:16], ALU.mult, ALU.add))
            TS(nsp8, splam, -LRU_C, None, ALU.mult)
            TS(psp8, splam, LRU_C, None, ALU.mult)
            TS(nw0, vcol("rw_w0", 0, 16), -1.0, None, ALU.mult)
            TS(na0, vcol("rw_a0", 0, 16), -1.0, None, ALU.mult)
            nc.vector.memset(half_one, 1.0)
            TS(omka, vcol("rw_ka", 0, 8), -1.0, 1.0, ALU.mult, ALU.add).then_inc(S["lb_done"], 1)
            norm_apply(0)
            for j in range(4):
                n = T["xr"] + j
                dve.wait_ge(S["conv_base"], j + 1)
                ps = tile(n)
                for tap, off in ((0, -2), (1, -1), (3, 1)):
                    w = vcol("rg_conv_w", tap * NTA + j)
                    for a, b in SEGS:
                        lo, hi = max(a, a - off), min(b, b - off)
                        ins = STT(XC[:, j, lo:hi], ps[:, lo + off:hi + off], w, XC[:, j, lo:hi], ALU.mult, ALU.add)
                    if tap == 3:
                        free(ins, n)
                    else:
                        link(ins)
            read_out(dve, T["xr"] + 3)

            def lru_unit(u):
                c, d = u // 2, u % 2
                dve.wait_ge(S["lru_th"], u + 1)
                if c == 0 and d == 0:
                    read_out(dve, T["yr"] + 3)
                link(TS(lr, lth, 1.0, None, ALU.add))
                link(nc.vector.reciprocal(lr, lr))
                TT(lth, lth, lr, ALU.mult).then_inc(S["lru_q"], 1)
                link(TT(li, li, XC[:, c, :], ALU.mult))
                dve.wait_ge(S["lru_root"], u + 1)
                link(TT(lth, lth, li, ALU.mult))
                dst = lh if d == 0 else lr
                for s, (a, b) in enumerate(SEGS):
                    init = 0.0 if s == 0 else vcol("state_rglru", 4 * d + c)
                    if d == 0:
                        o_, a_, b_ = dst[:, a:b], la[:, a:b], lth[:, a:b]
                    else:
                        r = slice(b - 1, a - 1 if a else None, -1)
                        o_, a_, b_ = dst[:, r], la[:, r], lth[:, r]
                    link(nc.vector.tensor_tensor_scan(o_, a_, b_, init, ALU.mult, ALU.add))
                e0 = CTX - 1 if d == 0 else 0
                ins = nc.vector.tensor_copy(lru_fin[:, 4 * d + c:4 * d + c + 1], dst[:, e0:e0 + 1])
                if d == 1:
                    link(TT(lh, lh, lr, ALU.add))
                    ins = TT(YG[:, c, :], YG[:, c, :], lh, ALU.mult)
                ins.then_inc(S["lru_done"], 1)

            for u in range(8):
                lru_unit(u)
                if u % 2 == 1:
                    for q in range(4):
                        mod_evac(T[f"mod0b{u // 2}"] + q, 0, 8 + 4 * (u // 2) + q)
            read_out(dve, T["mod0b3"] + 4)
            make_coef(1, 0, 32, vcol("norm_ffn_g", 0, KT))
            n = T["lruT"]
            read_out(dve, T["kb"] + 3)
            for d in range(2):
                for j in range(4):
                    TS(K[d][:, j, :], K[d][:, j, :], omlb[:, 4 * d + j:4 * d + j + 1], None, ALU.mult)
            for d in range(2):
                for j in range(4):
                    dve.wait_ge(S["f_log"], 4 * d + j + 1)
                    m = scanm[d]
                    v = B[d][:, j, :]
                    if d == 0:
                        ins = nc.vector.tensor_tensor_scan(v, m, v, 0.0, ALU.mult, ALU.add)
                    else:
                        ins = nc.vector.tensor_tensor_scan(v[:, ::-1], m[:, ::-1], v[:, ::-1], 0.0, ALU.mult, ALU.add)
            link(ins)
            ps = full(dve, n)
            free(nc.vector.tensor_copy(LROWS[0:8, 0:P], ps[0:8, 0:P]), n)

            def level_views(ap, s):
                return ap.rearrange("p (n w s) -> p n w s", w=2, s=s)

            def level_diff(h, lv):
                i = h * LEVELS + lv
                s = 1 << lv
                nb = NT // (2 * s)
                if i >= 3:
                    hp, lp = divmod(i - 3, LEVELS)
                    dve.wait_ge(psum_full, T[f"lvl{hp}"] + lp + 1)
                f, b = level_views(B[0][:, h, :], s), level_views(B[1][:, h, :], s)
                fm = f[:, :, 0, s - 1:s].broadcast_to([P, nb, s])
                bm = b[:, :, 1, 0:1].broadcast_to([P, nb, s])
                eq, ek = level_views(EQ[i % 3], s), level_views(EK[i % 3], s)
                TT(eq[:, :, 0, :], b[:, :, 0, :], bm, ALU.subtract)
                TT(eq[:, :, 1, :], f[:, :, 1, :], fm, ALU.subtract)
                TT(ek[:, :, 0, :], fm, f[:, :, 0, :], ALU.subtract)
                TT(ek[:, :, 1, :], bm, b[:, :, 1, :], ALU.subtract).then_inc(S["lvl_diff"], 1)

            att3 = ATT.rearrange("p (c t) -> p c t", t=P)

            def level_take(h, lv):
                n = T[f"lvl{h}"] + lv
                if lv:
                    read_out(dve, n - 1)
                ps = full(dve, n)
                m = (lmask[lv] if lv < LEVELS else ident).bitcast(i32)
                m = m.unsqueeze(1).broadcast_to([P, NCH, P])
                free(nc.vector.copy_predicated(att3, m, ps[:, 0:NT].rearrange("p (c t) -> p c t", t=P)), n)

            def norm_head(h):
                n = T[f"on{h}"]
                dve.wait_ge(S["on_root"], h + 1)
                free(STT(OCP, OCP, vcol("hgrn_norm_g", 0), tile(n)[:, 0:NT], ALU.mult, ALU.mult), n)
                read_out(dve, n)
                TT(OG[:, h, :], OG[:, h, :], OCP, ALU.mult).then_inc(S["o_a_ready"], 1)

            read_out(dve, T["og"] + 3)
            for h in range(NH_A):
                if h:
                    dve.wait_ge(psum_full, T[f"o{h - 1}"] + 1)
                for d in range(2):
                    b3 = B[d][:, h, :].rearrange("p (c t) -> p c t", t=P)
                    e0 = P - 1 if d == 0 else 0
                    end = b3[:, :, e0:e0 + 1].broadcast_to([P, NCH, P])
                    ins = TT(KH[d].rearrange("p (c t) -> p c t", t=P), end, b3, ALU.subtract)
                ins.then_inc(S["head_diff"], 1)
                level_diff(h, 0)
                level_diff(h, 1)
                TT(KSUM, K[0][:, h, :], K[1][:, h, :], ALU.add)
                dve.wait_ge(S["head_exp"], h + 1)
                for d in range(2):
                    TT(KH[d], KH[d], K[d][:, h, :], ALU.mult)
                    ins = TT(QIN[d][:, CTX:NT], QIN[d][:, CTX:NT], Q[:, h, CTX:NT], ALU.mult)
                ins.then_inc(S["head_ready"], 1)
                for lv in range(LEVELS):
                    i = h * LEVELS + lv
                    if lv + 2 < LEVELS:
                        level_diff(h, lv + 2)
                    dve.wait_ge(S["lvl_exp"], 2 * i + 1)
                    TT(EQ[i % 3], EQ[i % 3], Q[:, h, :], ALU.mult).then_inc(S["lvl_q"], 1)
                    if lv:
                        level_take(h, lv - 1)
                    if h and lv == 1:
                        norm_head(h - 1)
                level_take(h, LEVELS - 1)
                level_take(h, LEVELS)
                if h:
                    dve.wait_ge(S["s_final_sent"], 32 * h)
                for d in range(2):
                    n = T[f"U{h}"] + d
                    ps = full(dve, n)
                    nc.vector.tensor_copy(SFIN[d], ps[:, 0:P]).then_inc(S["s_final"], 1)
                    order = range(1, NCH - 1) if d == 0 else range(NCH - 1, 1, -1)
                    for c in order:
                        nxt_c = c + 1 if d == 0 else c - 1
                        ins = STT(hgrn_state(d, nxt_c, h), hgrn_state(d, c, h), gend[:, NCH * d + c:NCH * d + c + 1],
                                  ps[:, c * P:(c + 1) * P], ALU.mult, ALU.add)
                        if c == order[-1]:
                            free(ins, n)
                        else:
                            link(ins)
            norm_head(NH_A - 1)
            residual("wout", 0, 16)
            norm_apply(1)
            moe(0)
            read_out(dve, T["mod1_T3"])
            make_coef(2, 1, 8, vcol("norm_mix_g", KT, KT))
            make_coef(3, 1, 32, vcol("norm_ffn_g", KT, KT))
            norm_apply(2)
            dve.wait_ge(S["h_affine"], 3 * 2 * KT)
            for a, b in SEGS:
                TT(XX[:, :, a + 1:b - 1], H[:, :, a:b - 2], H[:, :, a + 2:b], ALU.add)
                nc.vector.tensor_copy(XX[:, :, a:a + 1], H[:, :, a + 1:a + 2])
                ins = nc.vector.tensor_copy(XX[:, :, b - 1:b], H[:, :, b - 2:b - 1])
            link(ins)
            link(STT(XXf, XXf, 0.5, Hf[:, :], ALU.mult, ALU.subtract))
            dve.wait_ge(S["x_parked"], 16)
            after = [None, T["lora"], T["lora"] + 1, T["lora"] + 2, T["r"] + KT - 1, T["k"] + KT - 1]
            for q, mi in enumerate((1, 4, 5, 0, 2, 3)):
                if q >= 2:
                    dve.wait_ge(psum_full, after[q - 1] + 1)
                for k in range(KT):
                    STT(XI[q % 2][:, k, :], XX[:, k, :], vcol("rw_mu", mi * KT + k), H[:, k, :], ALU.mult,
                        ALU.add).then_inc(S["xi_ready"], 1)
            for d in range(2):
                n = T["stT"] + d
                ps = full(dve, n)
                free(nc.vector.tensor_copy(ST[:, KT * d:KT * (d + 1), :],
                                           ps[:, 0:KT * HD].rearrange("p (j v) -> p j v", v=HD)), n)
            read_out(dve, T["stT"] + 1)
            dve.wait_ge(S["rw_clear"], 6)

            def c3(a):
                return a.rearrange("p (j t) -> p j t", t=P)

            def h3(a):
                return a.rearrange("p (h c) -> p h c", c=P)

            def clamp_gates(g, st, d):
                z, uid = STR[d], unit_id(g, st, d)
                n = T[f"P_{g}_{st}"] + d
                dve.wait_ge(S["gates_exp"], uid + 1)
                free(TS(z["SQ"], tile(n)[:, 2 * UW:3 * UW], 1e-24, 65536.0, ALU.max, ALU.mult), n)
                read_out(dve, n)
                TS(z["LA"], z["LA"], 2.0 ** 62, None, ALU.min).then_inc(S["gates_clamped"], 1)

            def sum_decays(g, st, d):
                z, uid = STR[d], unit_id(g, st, d)
                h0 = 4 * ((g * NCH + st) % 2) + 2 * d
                dve.wait_ge(S["gates_done"], uid + 1)
                one = half_one[:, 0:1].broadcast_to([P, P])
                for j in range(UC):
                    js = slice(j * P, (j + 1) * P) if d == 0 else slice((j + 1) * P - 1, j * P - 1 if j else None, -1)
                    ins = nc.vector.tensor_tensor_scan(z["B"][:, js], one, z["LA"][:, js], 0.0, ALU.mult, ALU.add)
                link(ins)
                e0 = P - 1 if d == 0 else 0
                link(TS(hb[:, h0:h0 + 2], z["B"][:, e0::P], 0.5, None, ALU.mult))

            def centre_decays(g, st, d):
                z = STR[d]
                h0 = 4 * ((g * NCH + st) % 2) + 2 * d
                b3 = c3(z["B"])
                link(TT(b3, b3, hb[:, h0:h0 + 2].unsqueeze(2).broadcast_to([P, UC, P]), ALU.subtract))
                TT(z["E3"], z["B"], z["LA"][:, 0:UW], ALU.subtract).then_inc(S["decay_sum"], 1)

            def rate_operands(g, st, d):
                z = STR[d]
                aa = z["LA"][:, UW:2 * UW]
                for j in range(UC):
                    ct = UC * g + j
                    js = slice(j * P, (j + 1) * P)
                    TS(z["KP"][:, js], aa[:, js], vcol("rw_ka", ct), omka[:, ct:ct + 1], ALU.mult, ALU.add)
                link(STT(z["KK"], z["KK"], 256.0, z["SQ"], ALU.mult, ALU.mult))
                TT(z["BE"], z["KK"], aa, ALU.mult)

            def bonus_operands(g, st, d):
                z, ch, uid = STR[d], chunk_of(st, d), unit_id(g, st, d)
                ts, cg = slice(ch * P, (ch + 1) * P), slice(UC * g, UC * (g + 1))
                dve.wait_ge(S["decay_exp"], uid + 1)
                link(TT(c3(z["KD"]), K1[:, cg, ts], c3(z["KP"]), ALU.mult))
                for j in range(UC):
                    ct = UC * g + j
                    js = slice(j * P, (j + 1) * P)
                    STT(z["SQ"][:, js], R1[:, ct, ts], vcol("rw_rk", ct), z["KD"][:, js], ALU.mult, ALU.mult)

            def decayed_operands(g, st, d):
                z, ch = STR[d], chunk_of(st, d)
                ts, cg = slice(ch * P, (ch + 1) * P), slice(UC * g, UC * (g + 1))
                TT(z["KP"], z["KD"], z["E2"], ALU.mult)
                TT(z["BE"], z["BE"], z["E2"], ALU.mult)
                r5 = z[f"RHS4_{(g * NCH + st) % 2}"].rearrange("p (j h a t) -> p j h a t", j=UC, h=2, a=2)
                for hh in range(2):
                    pr = slice(HD * hh, HD * hh + HD)
                    TT(r5[pr, :, hh, 0, :], c3(z["KK"])[pr], c3(z["E3"])[pr], ALU.mult)
                    ins = TT(r5[pr, :, hh, 1, :], R1[pr, cg, ts], c3(z["E1"])[pr], ALU.mult)
                ins.then_inc(S["unit_ready"], 1)

            def heads(a):
                return a.rearrange("p (h v) -> p h v", v=HD)

            def per_head(a):
                return a.unsqueeze(2).broadcast_to([P, HG, HD])

            def gn_centre(g, c):
                o, mu = heads(OT[:, c, UW * g:UW * (g + 1)]), gn_stats(c)[0]
                link(nc.vector.reduce_sum(mu, o, AX.X))
                link(TS(mu, mu, 1.0 / HD, None, ALU.mult))
                TT(o, o, per_head(mu), ALU.subtract).then_inc(S["gn_centred"], 1)

            def gn_variance(g, c):
                dve.wait_ge(S["gn_sq"], NCH * g + c + 1)
                nc.vector.reduce_sum(gn_stats(c)[1], heads(Z2[g][:, c, :]), AX.X).then_inc(S["gn_var"], 1)

            def gn_apply(g, c):
                dve.wait_ge(S["gn_root"], NCH * g + c + 1)
                o = heads(OT[:, c, UW * g:UW * (g + 1)])
                TT(o, o, per_head(gn_stats(c)[1]), ALU.mult)
                TT(heads(Z2[g][:, c, :]), heads(V1[:, c, UW * g:UW * (g + 1)]),
                   per_head(BON[:, c, HG * g:HG * (g + 1)]), ALU.mult).then_inc(S["z_ready"], 1)

            for stage in (clamp_gates, sum_decays, centre_decays, rate_operands, bonus_operands, decayed_operands):
                for d in range(2):
                    stage(0, 0, d)
            idb = ident.unsqueeze(1).broadcast_to([P, HG, P])
            for g in range(NGRP):
                for st in range(NCH):
                    u = f"_{g}_{st}"
                    nx = None if (g, st) == (NGRP - 1, NCH - 1) else next_step(g, st)
                    par = 4 * ((g * NCH + st) % 2)
                    for d in range(2):
                        z, uid = STR[d], unit_id(g, st, d)
                        n = T["AR" + u] + d
                        ps = full(dve, n)
                        m = CO[:, C_RMASK + 256 * d:C_RMASK + 256 * d + 256].unsqueeze(1).broadcast_to([P, HG, 256])
                        free(TT(z["AR"].rearrange("p (h c) -> p h c", c=256),
                                ps.rearrange("p (h c) -> p h c", c=256), m, ALU.mult), n)
                        read_out(dve, n)
                        at = z["AR"].rearrange("p (h c) -> p h c", c=256)[:, :, 0:P]
                        g0 = CO[:, C_GMASK + (1 - d) * P:C_GMASK + (2 - d) * P].unsqueeze(1).broadcast_to([P, HG, P])
                        link(TT(h3(z["N"]), at, g0, ALU.mult))
                        TT(h3(z["N"]), idb, h3(z["N"]), ALU.subtract).then_inc(S["mn_ready"], 1)
                    for d in range(2):
                        z = STR[d]
                        n = T["BR" + u] + d
                        ps = full(dve, n)
                        m = CO[:, C_RMASK + 256 * d:C_RMASK + 256 * d + 256].unsqueeze(1).broadcast_to([P, HG, 256])
                        free(TT(z["BR"].rearrange("p (h c) -> p h c", c=256),
                                ps.rearrange("p (h c) -> p h c", c=256), m, ALU.mult), n)
                    for d in range(2):
                        ch, uid = chunk_of(st, d), unit_id(g, st, d)
                        n = T["AN" + u] + d
                        dve.wait_ge(S["kb_t"], uid + 1)
                        if d:
                            read_out(dve, n - 1)
                        bo = BON[:, ch, HG * g:HG * (g + 1)]
                        free(TT(bo, bo, tile(n)[:, 0:HG], ALU.add), n)
                    if st:
                        for d in range(2):
                            TT(STR[d]["R0"].rearrange("p (j v) -> p j v", v=HD),
                               ST[:, KT * d + UC * g:KT * d + UC * (g + 1), :],
                               em[:, par + 2 * d:par + 2 * d + 2].unsqueeze(2).broadcast_to([P, UC, HD]),
                               ALU.mult).then_inc(S["r0_ready"], 1)
                    for lv in range(1, LEVELS):
                        s = 1 << lv
                        for d in range(2):
                            z = STR[d]
                            n = T[f"G{lv}" + u] + d
                            ps = full(dve, n)
                            o = C_GMASK + 2 * P + (d * (LEVELS - 1) + lv - 1) * HD
                            gm = CO[:, o:o + HD].unsqueeze(1).broadcast_to([P, HG, HD])
                            free(TT(z["G"].rearrange("p (h c) -> p h c", c=HD),
                                    ps[:, 0:HG * HD].rearrange("p (h c) -> p h c", c=HD), gm, ALU.mult), n)
                        if nx and lv == 2:
                            clamp_gates(*nx, 0)
                            clamp_gates(*nx, 1)
                        elif nx and lv == 4:
                            centre_decays(*nx, 0)
                        elif nx and lv == 5:
                            centre_decays(*nx, 1)
                        elif nx and lv == 6:
                            bonus_operands(*nx, 0)
                        for d in range(2):
                            z = STR[d]
                            n = T[f"D{lv}" + u] + d
                            ps = full(dve, n)
                            mv = z["M"].rearrange("p (n w s) -> p n w s", w=2, s=s)[:, :, d, :]
                            free(TT(mv, mv, ps[:, 0:HG * HD].rearrange("p (n s) -> p n s", s=s), ALU.subtract), n)
                        if nx:
                            if lv == 3:
                                sum_decays(*nx, 0)
                            elif lv == 4:
                                sum_decays(*nx, 1)
                            elif lv == 5:
                                rate_operands(*nx, 0)
                            elif lv == 6:
                                decayed_operands(*nx, 0)
                                rate_operands(*nx, 1)
                                bonus_operands(*nx, 1)
                                decayed_operands(*nx, 1)
                        if g and lv == 1:
                            gn_centre(g - 1, st)
                        if g and lv == 4:
                            gn_variance(g - 1, st)
                    for d in range(2):
                        z, ch = STR[d], chunk_of(st, d)
                        n = T["OT" + u] + d
                        ps = full(dve, n)
                        tt = ps[:, 512:512 + UC * P].rearrange("p (j c) -> p j c", c=P)
                        r0 = z["R0"].rearrange("p (j v) -> p j v", v=HD)
                        eb = em[:, par + 2 * d:par + 2 * d + 2]
                        if st:
                            for hh in range(2):
                                pr = slice(HD * hh, HD * hh + HD)
                                ins = TT(r0[pr], r0[pr], tt[pr, :, HD * hh:HD * hh + HD], ALU.add)
                            link(ins)
                            link(TT(ST[:, KT * d + UC * g:KT * d + UC * (g + 1), :], r0,
                                    eb.unsqueeze(2).broadcast_to([P, UC, HD]), ALU.mult))
                        else:
                            sf = z["SF"].rearrange("p (j v) -> p j v", v=HD)
                            for hh in range(2):
                                pr = slice(HD * hh, HD * hh + HD)
                                e2 = eb[pr].unsqueeze(2).broadcast_to([HD, UC, HD])
                                ins = TT(sf[pr], tt[pr, :, HD * hh:HD * hh + HD], e2, ALU.mult)
                            ins.then_inc(S["ctx_state"], 1)
                        o = OT[:, ch, HG * HD * g:HG * HD * (g + 1)]
                        if st == 0 and d:
                            read_out(dve, n - 1)
                        free(TT(o, o, ps[:, 0:HG * HD], ALU.add), n)
                    if g:
                        gn_apply(g - 1, st)
                    if st == 0:
                        n = T["fin" + u]
                        ps = full(dve, n)
                        free(nc.vector.tensor_copy(FINB[0:HD, :], ps[0:HD, 0:4 * P]), n)
            read_out(dve, T[f"OT_{NGRP - 1}_{NCH - 1}"] + 1)
            nc.vector.memset(lut[:, 2:3], 0.0).then_inc(S["scan_done"], 1)
            for stage in (gn_centre, gn_variance, gn_apply):
                for c in range(NCH):
                    stage(NGRP - 1, c)
            for k in range(KT):
                n = T[f"post{k}"]
                read_out(dve, n)
                ps = full(dve, n + 1)
                free(TT(OC[:, k, :], OC[:, k, :], ps[:, 0:NT], ALU.add), n + 1)
                ps = full(dve, n + 2)
                read_out(dve, n + 1)
                free(TT(OC[:, k, :], OC[:, k, :], ps[:, 0:NT], ALU.mult), n + 2)
            dve.wait_ge(S["x_back"], 16)
            residual("wo", 1, 16)
            norm_apply(3)
            moe(1)
            norm_apply(4)
            for c in range(NCH):
                n = T["yT"] + c
                ps = full(dve, n)
                free(nc.vector.tensor_copy(YT[:, c, :], ps), n)


_NAMES = ["x_prompt", "x_sample", "state_hgrn", "state_rglru", "state_rwkv", "c", "c_ctx", "norm_mix_g", "norm_ffn_g",
          "w_mod", "b_mod", "ab_w_in", "ab_w_out", "hgrn_lb", "hgrn_norm_g", "rg_conv_w", "rg_conv_b", "rg_wa", "rg_ba",
          "rg_wx", "rg_bx", "rg_lambda", "rw_mu", "rw_wr", "rw_wk", "rw_wv", "rw_wo", "rw_w0", "rw_w1", "rw_w2",
          "rw_a0", "rw_a1", "rw_a2", "rw_g1", "rw_g2", "rw_kk", "rw_ka", "rw_rk", "rw_lnw", "rw_lnb", "moe_router",
          "moe_router_bias", "moe_w1", "moe_w3", "moe_w2", "norm_f_g"]
_OUTS = [("y_prompt", (1, CTX, D)), ("y_sample", (1, LAT, D)), ("hgrn", (1, 1, 2, NH_A, P, P)),
         ("rglru", (1, 1, 2, DA)), ("rwkv", (1, 1, 2, 16, HD, HD))]


def shape_constants(np):
    c = np.zeros((P, C_ALL), np.float32)
    i, j = np.arange(P)[:, None], np.arange(P)[None, :]
    c[:, C_IDENT:C_IDENT + P] = i == j
    c[:, C_ONES:C_ONES + P] = 1.0
    c[:, C_BONES:C_BONES + P] = i // HD == j // HD
    c[:, C_HSEL:C_HSEL + 2] = np.arange(2)[None, :] == i // HD
    c[:, C_EPS] = EPS_RMS
    c[:, C_EPS + 1] = EPS_GN
    c[:, C_E128:C_E128 + NE] = np.arange(NE) * P
    c[:, C_XIDX:C_XIDX + 12] = np.arange(12)
    for d in range(2):
        o = C_RMASK + 256 * d
        c[:, o:o + P] = (i < j) if d == 0 else (i > j)
        c[:, o + P:o + 2 * P] = (i <= j) if d == 0 else (i >= j)
    for lv in range(LEVELS):
        s = 1 << lv
        g = (i // (2 * s) == j // (2 * s)) & ((i // s) % 2 == 1) & ((j // s) % 2 == 0)
        for d, gd in enumerate((g, g.T)):
            if lv == 0:
                c[:, C_GMASK + d * P:C_GMASK + (d + 1) * P] = gd
            else:
                o = C_GMASK + 2 * P + (d * (LEVELS - 1) + lv - 1) * HD
                c[:, o:o + HD] = gd[:, (np.arange(P) // s) % 2 == d]
        c[:, C_LMASK + lv * P:C_LMASK + (lv + 1) * P] = g | g.T
    t = np.arange(NT)
    c[:, C_SCAN:C_SCAN + NT] = t % P != 0
    c[:, C_SCAN + NT:C_SCAN + 2 * NT] = t % P != P - 1
    quarter = D // 4
    omega = (1.0 / (np.float32(10000.0) ** (np.arange(quarter, dtype=np.float32) / np.float32(quarter)))).astype(np.float32)
    for n, o in ((LAT // GRID_W, C_POS), (GRID_W, C_POS + 4 * (LAT // GRID_W))):
        ang = (np.arange(n, dtype=np.float32)[:, None] * omega).astype(np.float32)
        tab = np.concatenate([np.sin(ang), np.cos(ang)], axis=1).astype(np.float32)
        c[:, o:o + 4 * n] = tab.T.reshape(4, P, n).transpose(1, 0, 2).reshape(P, 4 * n)
    return c


def kernel(**inputs):
    import numpy as _np
    import concourse.bacc as _bacc
    from concourse import mybir as _mybir
    from concourse.bass_utils import run_bass_kernel_spmd as _run

    nc = _bacc.Bacc("TRN2", target_bir_lowering=False, num_devices=1)
    f32 = _mybir.dt.float32
    arrays, aps = {}, {}
    for name in _NAMES:
        a = _np.ascontiguousarray(inputs[name])
        arrays[f"in_{name}"] = a
        aps[name] = nc.dram_tensor(f"in_{name}", a.shape, _mybir.dt.from_np(a.dtype), kind="ExternalInput").ap()
    arrays["in_const"] = shape_constants(_np)
    const = nc.dram_tensor("in_const", (P, C_ALL), f32, kind="ExternalInput").ap()
    outs = {name: nc.dram_tensor(f"out_{name}", shape, f32, kind="ExternalOutput").ap() for name, shape in _OUTS}
    xspill = nc.dram_tensor("parked_residual", (P, KT * NT), f32).ap()
    slots_in = nc.dram_tensor("expert_inputs", (N_SLOTS, D), f32).ap()
    slots_out = nc.dram_tensor("expert_outputs", (N_SLOTS, D), f32).ap()
    build(nc, aps, const, outs, xspill, slots_in, slots_out)
    r = _run(nc, [arrays], core_ids=[0])
    return tuple(r.results[0][f"out_{name}"] for name, _ in _OUTS)
```
